# Optimizing a Trainium2 kernel written in Bass

```python
import jax
import jax.numpy as jnp
from jax import lax
import numpy as np

D_MODEL = 1024
BATCH = 1
SEQ = 128
DEPTH = 2
DEC_BATCH = 1
DEC_SEQ = 512
PAST_LEN = 128

GRID_W = 64
HEAD_DIM = 64
MLA_HEADS = 8
MLA_Q_LORA = 256
MLA_KV_LORA = 128
MLA_NOPE = 64
MLA_ROPE = 32
MLA_V = 64
SWA_HEADS = 4
SWA_KV_HEADS = 2
SWA_GROUP = SWA_HEADS // SWA_KV_HEADS
SWA_WINDOW = 128
SWA_BLOCK = 128
NA_HEADS = 4
NA_KH_MAX = 8
NA_KW = 16
N_GROUPS = 4
EXPERTS_PER_GROUP = 4
N_EXPERTS = N_GROUPS * EXPERTS_PER_GROUP
EXPERT_FF = 256
TOP_K = 2
N_MOD = 6
Q_BLOCK = 128
ROPE_THETA = 10000.0
EPS = 1e-6
MASK_VALUE = -1e30
MLA_SCALE = (MLA_NOPE + MLA_ROPE) ** -0.5
HEAD_SCALE = HEAD_DIM ** -0.5
MIX_WIDTH = MLA_HEADS * MLA_V + SWA_HEADS * HEAD_DIM + NA_HEADS * HEAD_DIM
IN_SWA = (SWA_HEADS + 2 * SWA_KV_HEADS) * HEAD_DIM
IN_NA = 3 * NA_HEADS * HEAD_DIM
D_IN = MLA_Q_LORA + MLA_KV_LORA + MLA_ROPE + IN_SWA + IN_NA

kernel_name = 'hybrid_dit_mla_swa_na_hmoe_step'

def rmsnorm(x, g):
    xf = x.astype(jnp.float32)
    y = xf * lax.rsqrt(jnp.mean(xf * xf, axis=-1, keepdims=True) + EPS)
    return (y * g.astype(jnp.float32)).astype(x.dtype)

def rope_1d(x, pos):
    half = x.shape[-1] // 2
    inv_freq = ROPE_THETA ** (-jnp.arange(half, dtype=jnp.float32) / half)
    ang = pos[:, None] * inv_freq[None, :]
    shape = (1, pos.shape[0]) + (1,) * (x.ndim - 3) + (half,)
    cos = jnp.cos(ang).reshape(shape).astype(x.dtype)
    sin = jnp.sin(ang).reshape(shape).astype(x.dtype)
    x1, x2 = x[..., :half], x[..., half:]
    return jnp.concatenate([x1 * cos - x2 * sin, x1 * sin + x2 * cos], axis=-1)

def axial_rope(x):
    t = x.shape[1]
    pos = jnp.arange(t)
    row = (pos // GRID_W).astype(jnp.float32)
    col = (pos % GRID_W).astype(jnp.float32)
    d2 = x.shape[-1] // 2
    return jnp.concatenate([rope_1d(x[..., :d2], row), rope_1d(x[..., d2:], col)], axis=-1)

def modulate(cvec, w_mod_l, b_mod_l):
    m = jnp.einsum('bd,de->be', jax.nn.silu(cvec), w_mod_l) + b_mod_l
    return jnp.split(m[:, None, :], N_MOD, axis=-1)

def mixer_projections(h, w_in_l, g_qa_l, w_uq_l, g_kva_l):
    b, t, _ = h.shape
    p = jnp.einsum('btd,de->bte', h, w_in_l)
    s1 = MLA_Q_LORA
    s2 = s1 + MLA_KV_LORA
    s3 = s2 + MLA_ROPE
    s4 = s3 + IN_SWA
    cq, ckv, kpe, swa, na = jnp.split(p, [s1, s2, s3, s4], axis=-1)
    q_mla = jnp.einsum('btr,re->bte', rmsnorm(cq, g_qa_l), w_uq_l).reshape(b, t, MLA_HEADS, MLA_NOPE + MLA_ROPE)
    ckv = rmsnorm(ckv, g_kva_l)
    q_swa, k_swa, v_swa = jnp.split(swa, [SWA_HEADS * HEAD_DIM, (SWA_HEADS + SWA_KV_HEADS) * HEAD_DIM], axis=-1)
    q_swa = q_swa.reshape(b, t, SWA_HEADS, HEAD_DIM)
    k_swa = k_swa.reshape(b, t, SWA_KV_HEADS, HEAD_DIM)
    v_swa = v_swa.reshape(b, t, SWA_KV_HEADS, HEAD_DIM)
    q_na, k_na, v_na = jnp.split(na, 3, axis=-1)
    q_na = q_na.reshape(b, t, NA_HEADS, HEAD_DIM)
    k_na = k_na.reshape(b, t, NA_HEADS, HEAD_DIM)
    v_na = v_na.reshape(b, t, NA_HEADS, HEAD_DIM)
    return q_mla, ckv, kpe, q_swa, k_swa, v_swa, q_na, k_na, v_na

def mla_expand(ckv, kpe, w_ukv_l):
    b, t, _ = ckv.shape
    kv = jnp.einsum('btc,ce->bte', ckv, w_ukv_l).reshape(b, t, MLA_HEADS, MLA_NOPE + MLA_V)
    k_nope, v = kv[..., :MLA_NOPE], kv[..., MLA_NOPE:]
    k = jnp.concatenate([k_nope, jnp.broadcast_to(kpe[:, :, None, :], (b, t, MLA_HEADS, MLA_ROPE))], axis=-1)
    return k, v

def dense_attention(q, k, v, scale, sink=None):
    b, tq, kh, g, d = q.shape
    nb = tq // Q_BLOCK
    qb = jnp.moveaxis(q.reshape(b, nb, Q_BLOCK, kh, g, d), 1, 0)

    def one_block(q_blk):
        s = jnp.einsum('bqkgd,bskd->bkgqs', q_blk, k).astype(jnp.float32) * scale
        if sink is not None:
            sk = jnp.broadcast_to(sink.astype(jnp.float32)[None, :, :, None, None], s.shape[:-1] + (1,))
            p = jax.nn.softmax(jnp.concatenate([s, sk], axis=-1), axis=-1)[..., :-1]
        else:
            p = jax.nn.softmax(s, axis=-1)
        return jnp.einsum('bkgqs,bskv->bqkgv', p.astype(v.dtype), v)

    o = lax.map(one_block, qb)
    return jnp.moveaxis(o, 0, 1).reshape(b, tq, kh * g * v.shape[-1])

def window_attention(q, k, v, k_ctx, v_ctx, sink, scale):
    b, t, kh, g, d = q.shape
    nb = t // SWA_BLOCK
    qb = q.reshape(b, nb, SWA_BLOCK, kh, g, d)

    def neighbours(a):
        pad = jnp.pad(a, ((0, 0), (SWA_BLOCK, SWA_BLOCK), (0, 0), (0, 0)))
        blk = pad.reshape(b, nb + 2, SWA_BLOCK, kh, a.shape[-1])
        return jnp.concatenate([blk[:, :-2], blk[:, 1:-1], blk[:, 2:]], axis=2)

    kb, vb = neighbours(k), neighbours(v)
    qi = jnp.arange(SWA_BLOCK)
    kj = jnp.arange(3 * SWA_BLOCK)
    rel = kj[None, :] - SWA_BLOCK - qi[:, None]
    kpos = jnp.arange(nb)[:, None, None] * SWA_BLOCK - SWA_BLOCK + kj[None, None, :]
    mask = (jnp.abs(rel)[None] <= SWA_WINDOW) & (kpos >= 0) & (kpos < t)
    s_loc = jnp.einsum('bnqkgd,bnskd->bnkgqs', qb, kb).astype(jnp.float32) * scale
    s_loc = jnp.where(mask[None, :, None, None], s_loc, MASK_VALUE)
    s_ctx = jnp.einsum('bnqkgd,bpkd->bnkgqp', qb, k_ctx).astype(jnp.float32) * scale
    sk = jnp.broadcast_to(sink.astype(jnp.float32)[None, None, :, :, None, None], s_loc.shape[:-1] + (1,))
    p = jax.nn.softmax(jnp.concatenate([s_loc, s_ctx, sk], axis=-1), axis=-1)
    n_loc = 3 * SWA_BLOCK
    n_ctx = k_ctx.shape[1]
    p_loc = p[..., :n_loc].astype(v.dtype)
    p_ctx = p[..., n_loc:n_loc + n_ctx].astype(v.dtype)
    o = jnp.einsum('bnkgqs,bnskv->bnqkgv', p_loc, vb) + jnp.einsum('bnkgqp,bpkv->bnqkgv', p_ctx, v_ctx)
    return o.reshape(b, t, kh * g * v.shape[-1])

def neighbourhood_attention(q, k, v, k_ctx, v_ctx, rpb, scale):
    b, t, h, d = q.shape
    rows = t // GRID_W
    kh = min(NA_KH_MAX, rows)
    r = jnp.arange(rows)
    cidx = jnp.arange(GRID_W)
    row_start = jnp.clip(r - kh // 2, 0, rows - kh)
    key_rows = row_start[:, None] + jnp.arange(kh)[None, :]
    col_start = jnp.clip(cidx - NA_KW // 2, 0, GRID_W - NA_KW)
    col_ok = (cidx[None, :] >= col_start[:, None]) & (cidx[None, :] < col_start[:, None] + NA_KW)
    off_r = key_rows - r[:, None] + NA_KH_MAX - 1
    off_c = jnp.clip(cidx[None, :] - cidx[:, None], -(NA_KW - 1), NA_KW - 1) + NA_KW - 1
    bias = rpb[:, off_r[:, None, :, None], off_c[None, :, None, :]].astype(jnp.float32)
    bias = jnp.where(col_ok[None, None, :, None, :], bias, MASK_VALUE)
    bias = bias.transpose(1, 0, 2, 3, 4).reshape(rows, h, GRID_W, kh * GRID_W)
    qg = q.reshape(b, rows, GRID_W, h, d)
    kg = k.reshape(b, rows, GRID_W, h, d)[:, key_rows].reshape(b, rows, kh * GRID_W, h, d)
    vg = v.reshape(b, rows, GRID_W, h, v.shape[-1])[:, key_rows].reshape(b, rows, kh * GRID_W, h, v.shape[-1])
    s_loc = jnp.einsum('brqhd,brshd->brhqs', qg, kg).astype(jnp.float32) * scale + bias[None]
    s_ctx = jnp.einsum('brqhd,bphd->brhqp', qg, k_ctx).astype(jnp.float32) * scale
    p = jax.nn.softmax(jnp.concatenate([s_loc, s_ctx], axis=-1), axis=-1)
    n_loc = kh * GRID_W
    o = (jnp.einsum('brhqs,brshv->brqhv', p[..., :n_loc].astype(v.dtype), vg)
         + jnp.einsum('brhqp,bphv->brqhv', p[..., n_loc:].astype(v.dtype), v_ctx))
    return o.reshape(b, t, h * v.shape[-1])

def hier_moe(h, w_rg_l, w_re_l, w_gate_l, w_up_l, w_down_l):
    b, t, _ = h.shape
    grp_logits = jnp.einsum('btd,dg->btg', h, w_rg_l).astype(jnp.float32)
    grp_prob = jax.nn.softmax(grp_logits, axis=-1)
    grp_idx = jnp.argmax(grp_logits, axis=-1)
    grp_gate = jnp.max(grp_prob, axis=-1, keepdims=True)
    exp_logits = jnp.einsum('btd,de->bte', h, w_re_l).astype(jnp.float32).reshape(b, t, N_GROUPS, EXPERTS_PER_GROUP)
    grp_onehot = jax.nn.one_hot(grp_idx, N_GROUPS, dtype=jnp.float32)
    exp_logits = jnp.sum(exp_logits * grp_onehot[..., None], axis=2)
    top_val, top_idx = lax.top_k(exp_logits, TOP_K)
    top_w = jax.nn.softmax(top_val, axis=-1) * grp_gate
    expert_id = grp_idx[..., None] * EXPERTS_PER_GROUP + top_idx
    gates = jnp.sum(jax.nn.one_hot(expert_id, N_EXPERTS, dtype=jnp.float32) * top_w[..., None], axis=-2)
    hidden = jax.nn.silu(jnp.einsum('btd,edf->btef', h, w_gate_l)) * jnp.einsum('btd,edf->btef', h, w_up_l)
    hidden = hidden * gates[..., None].astype(hidden.dtype)
    return jnp.einsum('btef,efd->btd', hidden, w_down_l)

def residual_tail(x, heads_out, g1, sh2, sc2, g2, norm2_l, w_out_l, w_rg_l, w_re_l, w_gate_l, w_up_l, w_down_l):
    x = x + g1 * jnp.einsum('bte,ed->btd', heads_out, w_out_l)
    h2 = rmsnorm(x, norm2_l) * (1 + sc2) + sh2
    return x + g2 * hier_moe(h2, w_rg_l, w_re_l, w_gate_l, w_up_l, w_down_l)

def context_layer(x, c_ctx, w_mod_l, b_mod_l, norm1_l, norm2_l, w_in_l, g_qa_l, w_uq_l, g_kva_l, w_ukv_l,
                  sink_l, w_out_l, w_rg_l, w_re_l, w_gate_l, w_up_l, w_down_l):
    b, t, _ = x.shape
    sh1, sc1, g1, sh2, sc2, g2 = modulate(c_ctx[None, :], w_mod_l, b_mod_l)
    h = rmsnorm(x, norm1_l) * (1 + sc1) + sh1
    q_mla, ckv, kpe, q_swa, k_swa, v_swa, q_na, k_na, v_na = mixer_projections(h, w_in_l, g_qa_l, w_uq_l, g_kva_l)
    k_mla, v_mla = mla_expand(ckv, kpe, w_ukv_l)
    o_mla = dense_attention(q_mla[:, :, :, None, :], k_mla, v_mla, MLA_SCALE)
    o_swa = dense_attention(q_swa.reshape(b, t, SWA_KV_HEADS, SWA_GROUP, HEAD_DIM), k_swa, v_swa, HEAD_SCALE,
                            sink_l.reshape(SWA_KV_HEADS, SWA_GROUP))
    o_na = dense_attention(q_na[:, :, :, None, :], k_na, v_na, HEAD_SCALE)
    heads_out = jnp.concatenate([o_mla, o_swa, o_na], axis=-1)
    x = residual_tail(x, heads_out, g1, sh2, sc2, g2, norm2_l, w_out_l, w_rg_l, w_re_l, w_gate_l, w_up_l, w_down_l)
    return x, ckv, kpe, k_swa, v_swa, k_na, v_na

def latent_layer(x, c, ckv_c, kpe_c, kswa_c, vswa_c, kna_c, vna_c, rpb_l,
                 w_mod_l, b_mod_l, norm1_l, norm2_l, w_in_l, g_qa_l, w_uq_l, g_kva_l, w_ukv_l,
                 sink_l, w_out_l, w_rg_l, w_re_l, w_gate_l, w_up_l, w_down_l):
    b, t, _ = x.shape
    sh1, sc1, g1, sh2, sc2, g2 = modulate(c, w_mod_l, b_mod_l)
    h = rmsnorm(x, norm1_l) * (1 + sc1) + sh1
    q_mla, ckv, kpe, q_swa, k_swa, v_swa, q_na, k_na, v_na = mixer_projections(h, w_in_l, g_qa_l, w_uq_l, g_kva_l)
    q_mla = jnp.concatenate([q_mla[..., :MLA_NOPE], axial_rope(q_mla[..., MLA_NOPE:])], axis=-1)
    kpe = axial_rope(kpe[:, :, None, :])[:, :, 0, :]
    k_lat, v_lat = mla_expand(ckv, kpe, w_ukv_l)
    k_ctx, v_ctx = mla_expand(ckv_c, kpe_c, w_ukv_l)
    o_mla = dense_attention(q_mla[:, :, :, None, :], jnp.concatenate([k_lat, k_ctx], axis=1),
                            jnp.concatenate([v_lat, v_ctx], axis=1), MLA_SCALE)
    q_swa = axial_rope(q_swa).reshape(b, t, SWA_KV_HEADS, SWA_GROUP, HEAD_DIM)
    k_swa = axial_rope(k_swa)
    o_swa = window_attention(q_swa, k_swa, v_swa, kswa_c, vswa_c, sink_l.reshape(SWA_KV_HEADS, SWA_GROUP), HEAD_SCALE)
    o_na = neighbourhood_attention(q_na, k_na, v_na, kna_c, vna_c, rpb_l, HEAD_SCALE)
    heads_out = jnp.concatenate([o_mla, o_swa, o_na], axis=-1)
    return residual_tail(x, heads_out, g1, sh2, sc2, g2, norm2_l, w_out_l, w_rg_l, w_re_l, w_gate_l, w_up_l, w_down_l)

def setup_inputs(seed: int = 0) -> dict:
    key = jax.random.key(seed)
    ks = jax.random.split(key, 28)

    def nrm(k, shape, scale=1.0):
        return jax.random.normal(k, shape, jnp.float32) * scale

    return {
        'x_prompt': nrm(ks[0], (BATCH, SEQ, D_MODEL)),
        'x_sample': nrm(ks[1], (DEC_BATCH, DEC_SEQ, D_MODEL)),
        'cache_mla_ckv': nrm(ks[2], (DEC_BATCH, DEPTH, PAST_LEN, MLA_KV_LORA)),
        'cache_mla_kpe': nrm(ks[3], (DEC_BATCH, DEPTH, PAST_LEN, MLA_ROPE)),
        'cache_swa_k': nrm(ks[4], (DEC_BATCH, DEPTH, PAST_LEN, SWA_KV_HEADS, HEAD_DIM)),
        'cache_swa_v': nrm(ks[5], (DEC_BATCH, DEPTH, PAST_LEN, SWA_KV_HEADS, HEAD_DIM)),
        'cache_na_k': nrm(ks[6], (DEC_BATCH, DEPTH, PAST_LEN, NA_HEADS, HEAD_DIM)),
        'cache_na_v': nrm(ks[7], (DEC_BATCH, DEPTH, PAST_LEN, NA_HEADS, HEAD_DIM)),
        'c': nrm(ks[8], (DEC_BATCH, D_MODEL)),
        'c_ctx': nrm(ks[9], (D_MODEL,)),
        'w_mod': nrm(ks[10], (DEPTH, D_MODEL, N_MOD * D_MODEL), 0.5 * D_MODEL ** -0.5),
        'b_mod': nrm(ks[11], (DEPTH, N_MOD * D_MODEL), 0.02),
        'norm1': 1.0 + nrm(ks[12], (DEPTH, D_MODEL), 0.02),
        'norm2': 1.0 + nrm(ks[13], (DEPTH, D_MODEL), 0.02),
        'w_in': nrm(ks[14], (DEPTH, D_MODEL, D_IN), D_MODEL ** -0.5),
        'g_qa': 1.0 + nrm(ks[15], (DEPTH, MLA_Q_LORA), 0.02),
        'w_uq': nrm(ks[16], (DEPTH, MLA_Q_LORA, MLA_HEADS * (MLA_NOPE + MLA_ROPE)), MLA_Q_LORA ** -0.5),
        'g_kva': 1.0 + nrm(ks[17], (DEPTH, MLA_KV_LORA), 0.02),
        'w_ukv': nrm(ks[18], (DEPTH, MLA_KV_LORA, MLA_HEADS * (MLA_NOPE + MLA_V)), MLA_KV_LORA ** -0.5),
        'swa_sink': nrm(ks[19], (DEPTH, SWA_HEADS)),
        'na_rpb': nrm(ks[20], (DEPTH, NA_HEADS, 2 * NA_KH_MAX - 1, 2 * NA_KW - 1), 0.1),
        'w_out': nrm(ks[21], (DEPTH, MIX_WIDTH, D_MODEL), MIX_WIDTH ** -0.5),
        'w_router_grp': nrm(ks[22], (DEPTH, D_MODEL, N_GROUPS), D_MODEL ** -0.5),
        'w_router_exp': nrm(ks[23], (DEPTH, D_MODEL, N_EXPERTS), D_MODEL ** -0.5),
        'w_gate': nrm(ks[24], (DEPTH, N_EXPERTS, D_MODEL, EXPERT_FF), D_MODEL ** -0.5),
        'w_up': nrm(ks[25], (DEPTH, N_EXPERTS, D_MODEL, EXPERT_FF), D_MODEL ** -0.5),
        'w_down': nrm(ks[26], (DEPTH, N_EXPERTS, EXPERT_FF, D_MODEL), EXPERT_FF ** -0.5),
        'norm_final': 1.0 + nrm(ks[27], (D_MODEL,), 0.02),
    }

def reference(x_prompt, x_sample, cache_mla_ckv, cache_mla_kpe, cache_swa_k, cache_swa_v, cache_na_k, cache_na_v,
              c, c_ctx, w_mod, b_mod, norm1, norm2, w_in, g_qa, w_uq, g_kva, w_ukv, swa_sink, na_rpb, w_out,
              w_router_grp, w_router_exp, w_gate, w_up, w_down, norm_final):
    xp, xs = x_prompt, x_sample
    new_ckv, new_kpe, new_ks, new_vs, new_kn, new_vn = [], [], [], [], [], []
    for l in range(DEPTH):
        shared = (w_mod[l], b_mod[l], norm1[l], norm2[l], w_in[l], g_qa[l], w_uq[l], g_kva[l], w_ukv[l],
                  swa_sink[l], w_out[l], w_router_grp[l], w_router_exp[l], w_gate[l], w_up[l], w_down[l])
        xp, ckv, kpe, ks_, vs_, kn_, vn_ = context_layer(xp, c_ctx, *shared)
        new_ckv.append(ckv)
        new_kpe.append(kpe)
        new_ks.append(ks_)
        new_vs.append(vs_)
        new_kn.append(kn_)
        new_vn.append(vn_)
        xs = latent_layer(xs, c, cache_mla_ckv[:, l], cache_mla_kpe[:, l], cache_swa_k[:, l], cache_swa_v[:, l],
                          cache_na_k[:, l], cache_na_v[:, l], na_rpb[l], *shared)
    y_prompt = rmsnorm(xp, norm_final)
    y_sample = rmsnorm(xs, norm_final)
    return (y_prompt, y_sample, jnp.stack(new_ckv, axis=1), jnp.stack(new_kpe, axis=1), jnp.stack(new_ks, axis=1),
            jnp.stack(new_vs, axis=1), jnp.stack(new_kn, axis=1), jnp.stack(new_vn, axis=1))


_drawn_inputs = setup_inputs


def setup_inputs(seed=0):
    import zlib

    import numpy as np

    out = dict(_drawn_inputs(seed))
    spreads = {}
    factors = {'cache_mla_ckv': 5.09,
     'cache_mla_kpe': 7.331,
     'cache_swa_k': 4.556,
     'cache_swa_v': 3.866,
     'cache_na_k': 3.364,
     'cache_na_v': 2.788,
     'norm1': 2.991,
     'norm2': 3.988,
     'g_qa': 8.0,
     'g_kva': 3.027,
     'swa_sink': 64.0,
     'na_rpb': 8.0,
     'norm_final': 9.396}
    for name, (base, spread) in spreads.items():
        noise = np.random.default_rng([zlib.crc32(name.encode()), seed]).standard_normal(out[name].shape)
        drawn = base * np.exp(spread * noise) if base else spread * noise
        out[name] = jnp.asarray(drawn.astype(out[name].dtype))
    for name, factor in factors.items():
        out[name] = (out[name] * factor).astype(out[name].dtype)
    return out
```

```python
from contextlib import ExitStack

import numpy as np

import concourse.bass as bass
from concourse import mybir

F32 = mybir.dt.float32
BF16 = mybir.dt.bfloat16
I32 = mybir.dt.int32
ALU = mybir.AluOpType
ACT = mybir.ActivationFunctionType
AX = mybir.AxisListType

P = 128
D = 1024
KD = D // P
DEPTH = 2
SEQ = 128
DEC = 512
TILES = 5
KVT = 6
TOK = TILES * P
KEYS = KVT * P
GRID_W = 64
EPS = 1e-6
NE = 16
FF = 256
MLA_H, NOPE, ROPE, MV = 8, 64, 32, 64
QK = NOPE + ROPE
NOVF = 9
CAP = P
SLOTS = (NE + NOVF) * P
MLA_SCALE = float(QK) ** -0.5
HEAD_SCALE = 0.125
NEG = -3.0e38
ORDER = [4, 0, 1, 2, 3]
CHUNKS = [(0, 416), (416, 384), (800, 512), (1312, 384)]
C_CQ, C_CKV, C_KPE, C_QS, C_KS, C_QN, C_KN = 0, 256, 384, 416, 672, 800, 1056
PW = 1312
RPB_ROW, RPB_LEN = 64, 128 + 15 * 64 + 64


def norm_no(L, phase, i):
    return TILES * (2 * L + (phase == 5)) + i + 1


def x_no(L, phase, i):
    per = 3 - i % 2
    return 16 * (per * (2 * L + (phase == 5)) + i // 2 + 1)


class Lane:

    def __init__(self, full, free):
        self.full, self.free = full, free
        self.number, self.freed, self.jobs, self.frees = {}, {}, 0, 0

    def take(self, pe, key, frees=1):
        if self.frees:
            pe.wait_ge(self.free, self.frees)
        self.jobs += 1
        self.frees += frees
        self.number[key] = self.jobs
        self.freed[key] = self.frees

    def __getitem__(self, key):
        return self.number[key]


def program(nc, t_in, t_out):
    with ExitStack() as ctx:
        def sb(name, shape, dt=F32):
            return ctx.enter_context(nc.sbuf_tensor(name, shape, dt))

        def sem(name):
            return ctx.enter_context(nc.semaphore(name))

        xbuf = nc.dram_tensor("x_rows", (TOK, D), F32).ap()
        slots_x = nc.dram_tensor("slots_x", (SLOTS, D), F32).ap()
        slots_y = nc.dram_tensor("slots_y", (SLOTS, D), F32).ap()

        ring = sb("ring", [P, 4 * 8 * 512])
        slot = [ring[:, i * 4096:(i + 1) * 4096].rearrange("p (k n) -> p k n", k=8) for i in range(4)]
        big = sb("big", [P, 5120])
        hT = big[:, :].rearrange("p (k n) -> p k n", k=KD)
        heads = big[:, :].rearrange("p (t n) -> p t n", t=TILES)
        mrow = sb("mrow", [P, 3, 512])
        brow = sb("brow", [P, 3, 512])
        wuq = sb("wuq", [P, 2, 768])
        wukv = sb("wukv", [P, 1024])
        wr = sb("wr", [P, KD, 20])
        gqa = sb("gqa", [P, 256])
        gkva = sb("gkva", [P, 128])
        nrm = sb("nrm", [P, D])
        sink = sb("sink", [P, 4])
        sc = sb("sc", [P, KD, 32])
        cc = sb("cc", [P, 2, KD])
        consts = sb("consts", [P, sum(w for _, w in CONSTS)])
        cst, at = {}, 0
        for name, w in CONSTS:
            cst[name] = consts[:, at:at + w]
            at += w
        ident, flip, upper = (cst[n] for n in ("ident", "flip", "upper"))
        ones = cst["w4"][:, 3:4].broadcast_to([P, P])
        mhalf = sb("mhalf", [P, 8])
        zeros = sb("zeros", [P, 256])
        ssq = sb("ssq", [P, 32])
        rsd = sb("rsd", [P, 32])
        wts = sb("wts", [P, TILES, 2])
        sidx = sb("sidx", [P, 2 * TILES], I32)
        ctl = sb("ctl", [P, 16], I32)

        ARENA = 21184
        arena = sb("arena", [P, ARENA])

        def place(at, *dims):
            n = int(np.prod(dims))
            assert at + n <= ARENA, (at, dims)
            a = arena[:, at:at + n]
            if len(dims) == 2:
                a = a.rearrange("p (a b) -> p a b", a=dims[0])
            return a, at + n

        cqT, o = place(0, 2, TOK)
        ckvT, o = place(o, KEYS)
        kpeT, A0 = place(o, KEYS)
        v_loc, o = place(A0, KVT, 384)
        qsP, o = place(o, 4, TOK)
        qnP, o = place(o, 4, TOK)
        ksT, o = place(o, KEYS)
        knT, A1 = place(o, 2, KEYS)
        proj, o = place(A1, 2, PW)
        rowA, o = place(o, D)
        rowB, o = place(o, D)
        xt, o = place(o, 2, D)
        junk1, o = place(o, 512)
        rt, o = place(o, 2, 384)
        ck, o = place(o, 544)
        bias, o = place(A1, 4, 960)
        braw, o = place(o, 960)
        sB, o = place(o, 2, 640)
        pB2, o = place(o, 2, 640)
        pT2, o = place(o, 2, 640)
        qT, o = place(A0, 8, TOK)
        kT, o = place(o, 8, KEYS)
        v_mla, A3 = place(o, KVT, 512)
        qt, o = place(A3, 2, 768)
        rq, o = place(o, 2, 256)
        pB4, o = place(A3, 2, 640)
        pT4, o = place(o, 2, 640)
        rowG1, o = place(0, 2, D)
        rowA2, o = place(o, 2, D)
        rowB2, o = place(o, 2, D)
        hoT, o = place(o, 2, D)
        xt5, o = place(o, 2, D)
        tmp5, o = place(o, D)
        h2, o = place(o, 5, D)
        h2T, o = place(o, 2, D)
        R0 = o
        xg, o = place(0, 2, D)
        xgT, o = place(o, 2, D)
        sg, o = place(o, 2, FF)
        hid, o = place(o, 2, FF)
        hidT, o = place(o, 2, FF)
        yb, o = place(o, 2, D)
        dn2, o = place(o, 2048)
        exp3, o = place(o, 6144)
        gu_at = [ring[:, 0:4096], ring[:, 6144:10240], ring[:, 12288:16384], exp3[:, 0:4096]]
        dn_at = [ring[:, 4096:6144], ring[:, 10240:12288], dn2, exp3[:, 4096:6144]]
        w_gu = [a.rearrange("p (g k n) -> p g k n", g=2, k=KD) for a in gu_at]
        w_dn = [a.rearrange("p (k n) -> p k n", k=2) for a in dn_at]
        rowG2, o = place(0, 2, D)
        x7, o = place(o, TILES, D)
        y1, o = place(o, TILES, D)
        y2, o = place(o, TILES, D)
        junk7, o = place(o, 512)
        rt_at = [R0]

        def rtile(*dims):
            n = int(np.prod(dims))
            a = arena[:, rt_at[0]:rt_at[0] + n]
            rt_at[0] += n
            assert rt_at[0] <= ARENA
            if len(dims) == 2:
                a = a.rearrange("p (a b) -> p a b", a=dims[0])
            if len(dims) == 3:
                a = a.rearrange("p (a b c) -> p a b c", a=dims[0], b=dims[1])
            return a

        r_lg = rtile(TILES, 20)
        r_g, r_d2, r_e2, r_m = (rtile(TILES) for _ in range(4))
        r_gd, r_ge, r_eq, r_oh, r_sel, r_oh1, r_oh2 = (rtile(TILES, 4) for _ in range(7))
        r_prod = rtile(TILES, 4, 4)
        r_c1, r_c2, r_T, r_pos, r_ge5, r_tmp = (rtile(TILES, NE) for _ in range(6))
        r_n, r_nov, r_ovb, r_dl = (rtile(NE) for _ in range(4))
        r_pr = rtile(NE, NE)
        r_ind = rtile(NOVF, NE)
        r_s = rtile(2, TILES)
        r_ctl = rtile(16)
        junk5 = arena[:, rt_at[0]:rt_at[0] + 512].bitcast(BF16)
        assert rt_at[0] + 512 <= ARENA

        stat = {n: sb("st_" + n, [P, 8]) for n in ("mx", "m2", "nm", "sm", "es", "ri")}

        ps = ctx.enter_context(nc.psum_tensor("ps", [P, 8, 512], F32))

        def two(b, n=1024):
            return ps[:, b:b + 2, :].rearrange("p a b -> p (a b)")[:, 0:n]

        S = [Lane(sem(f"s{i}_full"), sem(f"s{i}_free")) for i in range(2)]
        T = Lane(sem("t_full"), sem("t_free"))
        O = Lane(sem("o_full"), sem("o_free"))
        M = Lane(sem("m_full"), sem("m_free"))
        met = sem("met")
        const_in, c_in, bmod_in, small_in, vec_in, nrm_in = (sem(n) for n in
                                                    ("const_in", "c_in", "bmod_in", "small_in", "vec_in", "nrm_in"))
        slot_in = [sem(f"slot{i}_in") for i in range(4)]
        mods_done = sem("mods_done")
        xt_in = [sem(f"xt{i}_in") for i in range(2)]
        cache_in, ctx_out, zero_out, zero_set = (sem(n) for n in ("cache_in", "ctx_out", "zero_out", "zero_set"))
        silu_done, sc_set, half_set = (sem(n) for n in ("silu_done", "sc_set", "half_set"))
        sq_done, rs_done = sem("sq_done"), sem("rs_done")
        sq2_done, rs2_done = sem("sq2_done"), sem("rs2_done")
        hA_done, h_done = sem("hA_done"), sem("h_done")
        rows_done = sem("rows_done")
        post_done, pad_set = sem("post_done"), sem("pad_set")
        braw_in, bias_mul, bias_done = sem("braw_in"), sem("bias_mul"), sem("bias_done")
        nmax_done, q_done, routed = sem("nmax_done"), sem("q_done"), sem("routed")
        res_mul, res_done, xs_out = (sem(n) for n in ("res_mul", "res_done", "xs_out"))
        rx1, rx1_done, rx2, rx2_done = (sem(n) for n in ("rx1", "rx1_done", "rx2", "rx2_done"))
        pick_done, idx_done, scat_out = (sem(n) for n in ("pick_done", "idx_done", "scat_out"))
        ew_in = [sem(f"ew{i}_in") for i in range(4)]
        xg_in = [sem(f"xg{i}_in") for i in range(2)]
        e_xT, e_xTa, e_xTd, e_h, e_sg, e_hid, e_hT, e_hTe, e_d, e_ya, e_yd = (sem("e_" + n) for n in (
            "xT", "xTa", "xTd", "h", "sg", "hid", "hT", "hTe", "d", "ya", "yd"))
        ys_out = [sem(f"ys{i}_out") for i in range(2)]
        ov = [{n: sem(f"ov{L}_{n}") for n in ("x", "w", "xT", "xTe", "h", "sg", "hid", "hT", "hTe", "d", "y", "out")}
              for L in range(DEPTH)]
        x7_in = [sem(f"x7{i}_in") for i in range(TILES)]
        y_in = [sem(f"y{i}_in") for i in range(TILES)]
        comb, y1_scaled, comb_done, x7_out, fin_sq, fin_rs, fin_done = (sem(n) for n in (
            "comb", "y1_scaled", "comb_done", "x7_out", "fin_sq", "fin_rs", "fin_done"))
        step = {n: sem("step_" + n) for n in ("dve", "act", "pool")}
        steps = {n: 0 for n in step}

        def then(eng, who, ins):
            steps[who] += 1
            ins.then_inc(step[who], 1)
            eng.wait_ge(step[who], steps[who])

        meets = {}

        def meet(eng, who):
            meets[who] = meets.get(who, 0) + 1
            eng.drain().then_inc(met, 1)
            eng.wait_ge(met, 5 * meets[who])

        def unit_list(phase):
            out = []
            if phase == 2:
                for h in range(4):
                    for t in range(4):
                        lo, hi = max(t - 1, 0), min(t + 1, 3)
                        m0 = {0: 1, 1: 0, 2: 0, 3: 4}[t] * P
                        n = hi - lo + 2
                        out.append(dict(kind="swa", h=h, t=t, q=qsP[:, h, t * P:(t + 1) * P],
                                        k=[(0, ksT[:, lo * P:(hi + 1) * P]), ((n - 1) * P, ksT[:, 4 * P:5 * P])],
                                        n=n, mask=cst["swa"][:, m0:m0 + n * P],
                                        v=[v_loc[:, j, (h // 2) * 64:(h // 2) * 64 + 64] for j in [*range(lo, hi + 1), 4]],
                                        col=512 + h * 64))
                for h in range(4):
                    for t in range(4):
                        j0 = (7 - 2 * t) * 64
                        out.append(dict(kind="na", h=h, t=t, q=qnP[:, h, t * P:(t + 1) * P],
                                        k=[(0, knT[:, h // 2, 0:512]), (512, knT[:, h // 2, 512:640])],
                                        n=5, mask=bias[:, h, j0:j0 + 512],
                                        v=[v_loc[:, j, 128 + h * 64:192 + h * 64] for j in range(5)],
                                        col=768 + h * 64))
                for h in range(4):
                    out.append(dict(kind="swa_ctx", h=h, t=4, q=qsP[:, h, 512:640], k=[(0, ksT[:, 640:768])], n=1,
                                    v=[v_loc[:, 5, (h // 2) * 64:(h // 2) * 64 + 64]], col=512 + h * 64))
                for h in range(4):
                    out.append(dict(kind="ctx", h=h, t=4, q=qnP[:, h, 512:640], k=[(0, knT[:, h // 2, 640:768])],
                                    n=1, v=[v_loc[:, 5, 128 + h * 64:192 + h * 64]], col=768 + h * 64))
            else:
                for h in range(MLA_H):
                    for t in range(4):
                        out.append(dict(kind="mla", h=h, t=t, q=qT[0:QK, h, t * P:(t + 1) * P],
                                        k=[(0, kT[0:QK, h, 0:512]), (512, kT[0:QK, h, 512:640])], n=5,
                                        v=[v_mla[:, j, h * 64:h * 64 + 64] for j in range(5)], col=h * 64))
                    out.append(dict(kind="ctx", h=h, t=4, q=qT[0:QK, h, 512:640], k=[(0, kT[0:QK, h, 640:768])],
                                    n=1, v=[v_mla[:, 5, h * 64:h * 64 + 64]], col=h * 64))
            return out

        UNITS = {2: unit_list(2), 4: unit_list(4)}
        UBASE = {2: 0, 4: len(UNITS[2])}
        UPL = len(UNITS[2]) + len(UNITS[4])
        pB = {2: pB2, 4: pB4}
        pT = {2: pT2, 4: pT4}
        SINKS = sum(u["kind"].startswith("swa") for u in UNITS[2])

        def split(n):
            return (1, 0) if n == 1 else ((n + 1) // 2, n // 2)

        block = ctx.enter_context(nc.Block())

        @block.tensor
        def _(pe):
            def transpose(out, in_):
                return pe.transpose(out, in_, ident)

            def mod_group(L, g):
                for i in range(4):
                    pe.wait_ge(slot_in[i], 16 * ((4 if i < 2 else 5) * L + [1, 3, 4][g]))
                M.take(pe, ("mod", L, g))
                for k in range(KD):
                    for i in range(4):
                        mm = pe.matmul(ps[32 * i:32 * i + 32, 7, :], sc[:, k, :], slot[i][:, k, :],
                                       start=(k == 0), stop=(k == KD - 1), tile_position=(0, 32 * i))
                mm.then_inc(M.full, 1)

            bcn = [0]

            def broadcast(L, kind, vec, half):
                n = 2 * vec + half
                lane, b = ((O, 6), (M, 7))[bcn[0] % 2]
                bcn[0] += 1
                pe.wait_ge(mods_done, 3 * L + n // 4 + 1)
                lane.take(pe, ("bc", L, kind, vec, half))
                row = 32 * (n % 4) + kind
                pe.matmul(ps[:, b, :], ident[:, row:row + 1].broadcast_to([P, P]), mrow[:, n // 4, :],
                          start=True, stop=True).then_inc(lane.full, 1)

            def attention(L, phase):
                units = UNITS[phase]
                base = UPL * L + UBASE[phase]

                def scores(u):
                    un = units[u]
                    S[u % 2].take(pe, ("s", L, phase, u))
                    if phase == 2 and un["kind"] == "na" and un["t"] == 0:
                        pe.wait_ge(bias_done, 4 * L + un["h"] + 1)
                    b = 2 * (u % 2)
                    for at, k in un["k"]:
                        w = k.shape[-1]
                        mm = pe.matmul(two(b)[:, at:at + w], un["q"], k, start=(at % 512 == 0), stop=True,
                                       skip_group_check=True)
                    mm.then_inc(S[u % 2].full, 1)

                def turn(u):
                    n = units[u]["n"]
                    a, d = split(n)
                    T.take(pe, ("p", L, phase, u), frees=2 if d else 1)
                    pe.wait_ge(S[u % 2].free, S[u % 2].freed[("s", L, phase, u)])
                    for j in range(n):
                        o = ps[:, 4, j * P:(j + 1) * P] if j < a else ps[:, 5, (j - a) * P:(j - a + 1) * P]
                        mm = transpose(o, pB[phase][:, u % 2, j * P:(j + 1) * P])
                    mm.then_inc(T.full, 1)

                def values(u):
                    un = units[u]
                    O.take(pe, ("o", L, phase, u))
                    pe.wait_ge(T.free, T.freed[("p", L, phase, u)])
                    for j in range(un["n"]):
                        mm = pe.matmul(ps[:, 6, 0:64], pT[phase][:, u % 2, j * P:(j + 1) * P], un["v"][j],
                                       start=(j == 0), stop=(j == un["n"] - 1))
                    mm.then_inc(O.full, 1)

                for s in range(len(units) + 2):
                    if s < len(units):
                        scores(s)
                    if s >= 2:
                        values(s - 2)
                    if 1 <= s <= len(units):
                        turn(s - 1)
                    if phase == 2 and s in (16, 30):
                        mod_group(L, 1 if s == 16 else 2)

            pe.wait_ge(const_in, 16)
            pe.wait_ge(sc_set, 3)
            for L in range(DEPTH):
                if L == 0:
                    mod_group(L, 0)
                for v in range(2):
                    for half in range(2):
                        broadcast(L, 1, v, half)
                for s in range(TILES + 2):
                    if s < TILES:
                        t = ORDER[s]
                        T.take(pe, ("h", L, s))
                        pe.wait_ge(h_done, norm_no(L, 1, s))
                        for k in range(KD):
                            mm = transpose(ps[:, 4 + k // 4, (k % 4) * P:(k % 4 + 1) * P], xt[:, s % 2, k * P:(k + 1) * P])
                        mm.then_inc(T.full, 1)
                    if s == 0:
                        for v in range(2):
                            for half in range(2):
                                broadcast(L, 0, v, half)
                    if 1 <= s <= TILES:
                        t = ORDER[s - 1]
                        pe.wait_ge(T.free, T.freed[("h", L, s - 1)])
                        for half in range(2):
                            S[half].take(pe, ("in", L, s - 1))
                            for c in (2 * half, 2 * half + 1):
                                if s == 1:
                                    pe.wait_ge(slot_in[c], 16 * ((4 if c < 2 else 5) * L + 2))
                                for k in range(KD):
                                    mm = pe.matmul(ps[:, c, 0:CHUNKS[c][1]], hT[:, k, t * P:(t + 1) * P],
                                                   slot[c][:, k, 0:CHUNKS[c][1]], start=(k == 0), stop=(k == KD - 1))
                            mm.then_inc(S[half].full, 1)
                    if s >= 2:
                        q = proj[:, (s - 2) % 2, :]
                        T.take(pe, ("xp", L, s - 2), frees=2)
                        pe.wait_ge(post_done, TILES * L + s - 1)
                        for n, at in enumerate((C_CQ, C_CQ + P, C_CKV)):
                            transpose(ps[:, 4, n * P:(n + 1) * P], q[:, at:at + P])
                        transpose(ps[0:ROPE, 4, 384:512], q[:, C_KPE:C_KPE + ROPE])
                        for n, at in enumerate((C_QS, C_QS + P, C_KS)):
                            mm = transpose(ps[:, 5, n * P:(n + 1) * P], q[:, at:at + P])
                        mm.then_inc(T.full, 1)
                        O.take(pe, ("xn", L, s - 2))
                        pe.wait_ge(S[1].free, S[1].freed[("in", L, s - 2)])
                        for n, at in enumerate((C_QN, C_QN + P, C_KN, C_KN + P)):
                            mm = transpose(ps[:, 6, n * P:(n + 1) * P], q[:, at:at + P])
                        mm.then_inc(O.full, 1)
                T.take(pe, ("xp", L, 5), frees=2)
                pe.wait_ge(cache_in, 80 * (L + 1))
                transpose(ps[:, 4, 0:P], ck[:, 0:128])
                transpose(ps[0:ROPE, 4, 384:512], ck[:, 128:160])
                transpose(ps[:, 5, 0:P], ck[:, 160:288]).then_inc(T.full, 1)
                O.take(pe, ("xn", L, 5))
                transpose(ps[:, 6, 0:P], ck[:, 288:416])
                transpose(ps[:, 6, P:2 * P], ck[:, 416:544]).then_inc(O.full, 1)
                meet(pe, "pe")

                for h in range(4):
                    S[h % 2].take(pe, ("bias", L, h))
                    pe.wait_ge(braw_in, 16 * (4 * L + h + 1))
                    for n in range(2):
                        mm = pe.matmul(ps[:, 2 * (h % 2) + n, 0:480], flip, braw[:, n * 480:(n + 1) * 480],
                                       start=True, stop=True)
                    mm.then_inc(S[h % 2].full, 1)
                attention(L, 2)
                meet(pe, "pe")

                def uq(i):
                    t = ORDER[i]
                    T.take(pe, ("uq", L, i))
                    for n, w in ((0, 512), (512, 256)):
                        for k in range(2):
                            mm = pe.matmul(ps[:, 4 + n // 512, 0:w], cqT[:, k, t * P:(t + 1) * P], wuq[:, k, n:n + w],
                                           start=(k == 0), stop=(k == 1))
                    mm.then_inc(T.full, 1)

                def qturn(i):
                    S[i % 2].take(pe, ("qt", L, i))
                    pe.wait_ge(q_done, TILES * L + i + 1)
                    for h in range(MLA_H):
                        b = 2 * (i % 2) + h // 4
                        mm = transpose(ps[0:QK, b, (h % 4) * P:(h % 4 + 1) * P], qt[:, i % 2, h * QK:(h + 1) * QK])
                    mm.then_inc(S[i % 2].full, 1)

                for i in range(TILES + 1):
                    if i < TILES:
                        uq(i)
                    if i < 4:
                        S[i % 2].take(pe, ("uk", L, i))
                        for n, w in ((0, 512), (512, 256)):
                            mm = pe.matmul(ps[:, 2 * (i % 2) + n // 512, 0:w], wukv[:, i * P:(i + 1) * P],
                                           ckvT[:, n:n + w], start=True, stop=True)
                        mm.then_inc(S[i % 2].full, 1)
                    lane, b = ((O, 6), (M, 7))[i % 2]
                    lane.take(pe, ("uv", L, i))
                    pe.matmul(ps[:, b, :], ckvT[:, i * P:(i + 1) * P], wukv[:, 512:1024],
                              start=True, stop=True).then_inc(lane.full, 1)
                    if i >= 1:
                        qturn(i - 1)
                meet(pe, "pe")

                attention(L, 4)
                meet(pe, "pe")

                for vec in (2, 4, 3):
                    for kind in (1, 0):
                        for half in range(2):
                            broadcast(L, kind, vec, half)

                def ho_turn(i):
                    t = ORDER[i]
                    T.take(pe, ("ho", L, i), frees=2)
                    for k in range(KD):
                        mm = transpose(ps[:, 4 + k // 4, (k % 4) * P:(k % 4 + 1) * P], heads[:, t, k * P:(k + 1) * P])
                    mm.then_inc(T.full, 1)

                def h2_turn(i):
                    T.take(pe, ("h2", L, i), frees=2)
                    pe.wait_ge(h_done, norm_no(L, 5, i))
                    for k in range(KD):
                        mm = transpose(ps[:, 4 + k // 4, (k % 4) * P:(k % 4 + 1) * P], h2[:, ORDER[i], k * P:(k + 1) * P])
                    mm.then_inc(T.full, 1)

                def out_proj(i):
                    S[i % 2].take(pe, ("out", L, i))
                    pe.wait_ge(T.free, T.freed[("ho", L, i)])
                    for n in range(2):
                        if i == 0:
                            pe.wait_ge(slot_in[2 + n], 16 * (5 * L + 5))
                        for k in range(KD):
                            mm = pe.matmul(ps[:, 2 * (i % 2) + n, :], hoT[:, i % 2, k * P:(k + 1) * P], slot[2 + n][:, k, :],
                                           start=(k == 0), stop=(k == KD - 1))
                    mm.then_inc(S[i % 2].full, 1)

                def route(i):
                    t = ORDER[i]
                    if i == 0:
                        O.take(pe, ("rt", L))
                    pe.wait_ge(T.free, T.freed[("h2", L, i)])
                    for k in range(KD):
                        mm = pe.matmul(ps[:, 6, t * 20:(t + 1) * 20], h2T[:, i % 2, k * P:(k + 1) * P], wr[:, k, :],
                                       start=(k == 0), stop=(k == KD - 1))
                    mm.then_inc(O.full if i == TILES - 1 else routed, 1)

                for s in range(TILES + 4):
                    if s < TILES:
                        ho_turn(s)
                    if 1 <= s <= TILES:
                        out_proj(s - 1)
                    if 3 <= s < TILES + 3:
                        h2_turn(s - 3)
                    if s >= 4:
                        route(s - 4)
                O.take(pe, ("pos", L))
                M.take(pe, ("cnt", L))
                pe.wait_ge(pick_done, L + 1)
                pe.matmul(ps[:, 6, 0:80], upper, r_T[:, :, :].rearrange("p a b -> p (a b)"), start=True,
                          stop=True).then_inc(O.full, 1)
                pe.matmul(ps[:, 7, 0:80], ones, r_T[:, :, :].rearrange("p a b -> p (a b)"), start=True,
                          stop=True).then_inc(M.full, 1)
                meet(pe, "pe")

                n_ov = pe.value_load(ctl[0:1, 0:1], min_val=0, max_val=NOVF)
                E0 = NE * L

                def x_turn(e, b, first):
                    if not first:
                        pe.wait_ge(e_xTa, E0 + e)
                        pe.wait_ge(e_xTd, E0 + e)
                    pe.wait_ge(xg_in[b], 16 * (E0 // 2) + (e - b) * 8 + 16)
                    for k in range(KD):
                        mm = transpose(ps[:, 4 + k // 4, (k % 4) * P:(k % 4 + 1) * P], xg[:, b, k:D:KD])
                    mm.then_inc(e_xT, 1)

                def up(e, q, early):
                    b = q % 2
                    pe.wait_ge(ew_in[q], 12 * E0 + (e - q) * 12 + 48)
                    pe.wait_ge(e_xTa, E0 + e + 1)
                    pe.wait_ge(e_xTd, E0 + e + 1)
                    if not early:
                        pe.wait_ge(e_hid, E0 + e - 1)
                    for k in range(KD):
                        mm = pe.matmul(ps[:, b, :], xgT[:, b, k * P:(k + 1) * P], w_gu[q][:, :, k, :],
                                       start=(k == 0), stop=(k == KD - 1))
                    mm.then_inc(e_h, 1)

                def h_turn(e, b, first):
                    if not first:
                        pe.wait_ge(e_hTe, E0 + e)
                    pe.wait_ge(e_hid, E0 + e + 1)
                    for k in range(2):
                        mm = transpose(ps[:, 6, k * P:(k + 1) * P], hid[:, b, k:FF:2])
                    mm.then_inc(e_hT, 1)

                def down(e, q, first):
                    b = q % 2
                    pe.wait_ge(e_hTe, E0 + e + 1)
                    if not first:
                        pe.wait_ge(e_ya, E0 + e)
                        pe.wait_ge(e_yd, E0 + e)
                    for n in range(2):
                        for k in range(2):
                            mm = pe.matmul(ps[:, 2 + n, :], hidT[:, b, k * P:(k + 1) * P],
                                           w_dn[q][:, k, n * 512:(n + 1) * 512], start=(k == 0), stop=(k == 1))
                    mm.then_inc(e_d, 1)

                x_turn(0, 0, True)
                up(0, 0, True)
                x_turn(1, 1, False)
                h_turn(0, 0, True)
                up(1, 1, True)
                x_turn(2, 0, False)
                down(0, 0, True)
                h_turn(1, 1, False)
                with pe.Fori(2, NE - 2, 4) as e0:
                    for j in range(4):
                        e, q = e0 + j, (2 + j) % 4
                        up(e, q, False)
                        x_turn(e + 1, 1 - j % 2, False)
                        down(e - 1, (q - 1) % 4, False)
                        h_turn(e, j % 2, False)
                up(14, 2, False)
                x_turn(15, 1, False)
                down(13, 1, False)
                h_turn(14, 0, False)
                up(15, 3, False)
                down(14, 2, False)
                h_turn(15, 1, False)
                down(15, 3, False)
                pe.wait_ge(e_ya, E0 + NE)
                pe.wait_ge(e_yd, E0 + NE)
                with pe.If(n_ov > 0):
                    with pe.Fori(0, NOVF) as c:
                        n = c + 1
                        pe.wait_ge(ov[L]["x"], n * 16)
                        for k in range(KD):
                            mm = transpose(ps[:, 4 + k // 4, (k % 4) * P:(k % 4 + 1) * P], xg[:, 0, k:D:KD])
                        mm.then_inc(ov[L]["xT"], 1)
                        pe.wait_ge(ov[L]["w"], n * 48)
                        pe.wait_ge(ov[L]["xTe"], n)
                        for k in range(KD):
                            mm = pe.matmul(ps[:, 0, :], xgT[:, 0, k * P:(k + 1) * P], w_gu[0][:, :, k, :],
                                           start=(k == 0), stop=(k == KD - 1))
                        mm.then_inc(ov[L]["h"], 1)
                        pe.wait_ge(ov[L]["hid"], n)
                        for k in range(2):
                            mm = transpose(ps[:, 6, k * P:(k + 1) * P], hid[:, 0, k:FF:2])
                        mm.then_inc(ov[L]["hT"], 1)
                        pe.wait_ge(ov[L]["hTe"], n)
                        for h in range(2):
                            for k in range(2):
                                mm = pe.matmul(ps[:, 2 + h, :], hidT[:, 0, k * P:(k + 1) * P],
                                               w_dn[0][:, k, h * 512:(h + 1) * 512], start=(k == 0), stop=(k == 1))
                        mm.then_inc(ov[L]["d"], 1)
                meet(pe, "pe")

                for kind in (1, 0):
                    for half in range(2):
                        broadcast(L, kind, 5, half)
                if L < DEPTH - 1:
                    mod_group(L + 1, 0)
                meet(pe, "pe")

        @block.sync
        def _(sp):
            sp.dma_start(consts[:, :], t_in["consts"]).then_inc(const_in, 16)
            sp.dma_start(cc[:, 0, :], t_in["c"].rearrange("a (p k) -> (a p) k", k=KD)).then_inc(c_in, 16)
            sp.dma_start(cc[:, 1, :], t_in["c_ctx"].rearrange("(p k) -> p k", k=KD)).then_inc(c_in, 16)

            def mod_load(L, g):
                w_mod = t_in["w_mod"][L].rearrange("(p k) n -> p k n", k=KD)
                for i in range(4):
                    n = 4 * g + i
                    sp.dma_start(slot[i], w_mod[:, :, n * 512:(n + 1) * 512]).then_inc(slot_in[i], 16)

            def layer_loads(L):
                mod_load(L, 0)
                sp.dma_start(wuq[:, :, :], t_in["w_uq"][L].rearrange("(k p) n -> p k n", p=P)).then_inc(small_in, 16)
                sp.dma_start(wukv[:, :], t_in["w_ukv"][L]).then_inc(small_in, 16)
                sp.dma_start(wr[:, :, :], t_in["w_r"][L].rearrange("(k p) n -> p k n", p=P)).then_inc(small_in, 16)
                w_in = t_in["w_in"][L].rearrange("(k p) n -> p k n", p=P)
                sp.wait_ge(M.full, M[("mod", L, 0)])
                for c, (at, w) in enumerate(CHUNKS):
                    sp.dma_start(slot[c][:, :, 0:w], w_in[:, :, at:at + w]).then_inc(slot_in[c], 16)

            layer_loads(0)
            for L in range(DEPTH):
                w_out = t_in["w_out"][L].rearrange("(k p) n -> p k n", p=P)
                for half in range(2):
                    sp.wait_ge(S[half].full, S[half][("in", L, TILES - 1)])
                mod_load(L, 1)
                meet(sp, "sp")
                for h in range(4):
                    if h >= 1:
                        sp.wait_ge(S[(h - 1) % 2].full, S[(h - 1) % 2][("bias", L, h - 1)])
                    src = bass.AP(tensor=t_in["rpb"].tensor, offset=(L * 4 + h) * RPB_LEN + 16, ap=[[1, P], [1, 960]])
                    sp.dma_start(braw, src).then_inc(braw_in, 16)
                sp.wait_ge(M.full, M[("mod", L, 1)])
                mod_load(L, 2)
                sp.wait_ge(M.full, M[("mod", L, 2)])
                for n in range(2):
                    sp.dma_start(slot[2 + n], w_out[:, :, n * 512:(n + 1) * 512]).then_inc(slot_in[2 + n], 16)

                def up_load(e, q):
                    for n, w in enumerate(("w_gate", "w_up")):
                        sp.dma_start(w_gu[q][:, n], t_in[w][L][e].rearrange("(p k) n -> p k n", k=KD)).then_inc(ew_in[q], 16)

                def down_load(e, q):
                    sp.dma_start(w_dn[q], t_in["w_down"][L][e].rearrange("(p k) n -> p k n", k=2)).then_inc(ew_in[q], 16)

                up_load(0, 0)
                down_load(0, 0)
                meet(sp, "sp")
                meet(sp, "sp")
                meet(sp, "sp")
                for i in range(2):
                    sp.wait_ge(S[i].full, S[i][("out", L, TILES - 1 - i)])
                up_load(1, 1)
                down_load(1, 1)
                up_load(2, 2)
                meet(sp, "sp")
                n_ov = sp.value_load(ctl[0:1, 0:1], min_val=0, max_val=NOVF)
                E0 = NE * L
                for e in range(2):
                    sp.dma_start(xg[:, e, :], slots_x[e * P:(e + 1) * P, :]).then_inc(xg_in[e], 16)
                down_load(2, 2)
                up_load(3, 3)
                down_load(3, 3)
                for e in range(2, 4):
                    sp.wait_ge(e_xT, E0 + e - 1)
                    sp.dma_start(xg[:, e % 2, :], slots_x[e * P:(e + 1) * P, :]).then_inc(xg_in[e % 2], 16)
                with sp.Fori(1, NE // 4) as quad:
                    for q in range(4):
                        j = q % 2
                        e = sp.snap(quad * 4 + q)
                        row = sp.snap(quad * (4 * P) + q * P)
                        sp.wait_ge(e_xT, E0 + e - 1)
                        sp.dma_start(xg[:, j, :], slots_x[bass.ds(row, P), :]).then_inc(xg_in[j], 16)
                        sp.wait_ge(e_d, E0 + e - 3)
                        for n, w in enumerate(("w_gate", "w_up")):
                            sp.dma_start(w_gu[q][:, n], t_in[w][L][bass.ds(e, 1)].rearrange(
                                "o (p k) n -> (o p) k n", k=KD)).then_inc(ew_in[q], 16)
                        sp.dma_start(w_dn[q], t_in["w_down"][L][bass.ds(e, 1)].rearrange(
                            "o (p k) n -> (o p) k n", k=2)).then_inc(ew_in[q], 16)
                with sp.If(n_ov > 0):
                    sp.wait_ge(e_d, E0 + NE)
                    for c in range(NOVF):
                        e = sp.value_load(ctl[0:1, 1 + c:2 + c], min_val=0, max_val=NE - 1)
                        if c:
                            sp.wait_ge(ov[L]["out"], 16 * c)
                        row = (NE + c) * P
                        sp.dma_start(xg[:, 0, :], slots_x[row:row + P, :]).then_inc(ov[L]["x"], 16)
                        for n, w in enumerate(("w_gate", "w_up")):
                            sp.dma_start(w_gu[0][:, n], t_in[w][L][bass.ds(e, 1)].rearrange(
                                "o (p k) n -> (o p) k n", k=KD)).then_inc(ov[L]["w"], 16)
                        sp.dma_start(w_dn[0], t_in["w_down"][L][bass.ds(e, 1)].rearrange(
                            "o (p k) n -> (o p) k n", k=2)).then_inc(ov[L]["w"], 16)
                meet(sp, "sp")
                for i in range(TILES):
                    t = ORDER[i]
                    sp.dma_start(x7[:, i, :], xbuf[t * P:(t + 1) * P, :]).then_inc(x7_in[i], 16)
                if L < DEPTH - 1:
                    layer_loads(L + 1)
                meet(sp, "sp")

        @block.scalar
        def _(act):
            def attention(L, phase):
                units = UNITS[phase]
                base = UPL * L + UBASE[phase]

                def exps(u):
                    un, w = units[u], units[u]["n"] * P
                    act.wait_ge(nmax_done, base + u + 1)
                    if u >= 2:
                        act.wait_ge(T.full, T[("p", L, phase, u - 2)])
                    if un["kind"].startswith("swa"):
                        act.activation(stat["es"][:, u % 8:u % 8 + 1], sink[:, un["h"]:un["h"] + 1], ACT.Exp,
                                       bias=stat["nm"][:, u % 8:u % 8 + 1], scale=1.0)
                    src = sB[:, u % 2, 0:w] if "mask" in un else two(2 * (u % 2), w)
                    act.activation(pB[phase][:, u % 2, 0:w], src, ACT.Exp, bias=stat["nm"][:, u % 8:u % 8 + 1],
                                   scale=1.0, accum_out=stat["sm"][:, u % 8:u % 8 + 1]).then_inc(S[u % 2].free, 1)

                def copy(u):
                    a, d = split(units[u]["n"])
                    if d:
                        act.wait_ge(T.full, T[("p", L, phase, u)])
                        if u >= 2:
                            act.wait_ge(O.full, O[("o", L, phase, u - 2)])
                        act.activation(pT[phase][:, u % 2, a * P:(a + d) * P], ps[:, 5, 0:d * P],
                                       ACT.Copy).then_inc(T.free, 1)

                for s in range(len(units) + 1):
                    if s < len(units):
                        exps(s)
                    if s >= 1:
                        copy(s - 1)

            act.wait_ge(c_in, 32)
            act.wait_ge(zero_set, 2)
            act.activation(sc[:, :, 0:1], cc[:, 0, :].unsqueeze(2), ACT.Silu).then_inc(sc_set, 1)
            act.activation(sc[:, :, 1:2], cc[:, 1, :].unsqueeze(2), ACT.Silu).then_inc(sc_set, 1)
            act.wait_ge(const_in, 16)
            junk = junk1.bitcast(BF16)
            for L in range(DEPTH):
                for s in range(TILES + 2):
                    if s < TILES:
                        act.wait_ge(xt_in[s % 2], x_no(L, 1, s))
                        if s:
                            act.wait_ge(sq_done, norm_no(L, 1, s - 1))
                        if s > 1:
                            act.wait_ge(sq2_done, TILES * L + s - 1)
                        act.activation(junk, xt[:, s % 2, :], ACT.Square,
                                       accum_out=ssq[:, s:s + 1]).then_inc(sq_done, 1)
                        act.wait_ge(T.full, T[("h", L, s)])
                        t = ORDER[s]
                        for n in range(2):
                            cp = act.activation(hT[:, 4 * n:4 * n + 4, t * P:(t + 1) * P],
                                                ps[:, 4 + n, :].rearrange("p (k n) -> p k n", k=4), ACT.Copy)
                        cp.then_inc(T.free, 1)
                    if 1 <= s <= TILES:
                        i = s - 1
                        kv = 5 if ORDER[i] == 4 else ORDER[i]
                        act.wait_ge(S[1].full, S[1][("in", L, i)])
                        if i >= 2:
                            act.wait_ge(O.full, O[("xn", L, i - 2)])
                            if i == 2:
                                act.wait_ge(ctx_out, 96 * (L + 1))
                        act.activation(proj[:, i % 2, C_QN:C_QN + 512], ps[:, 2, :], ACT.Copy)
                        act.activation(v_loc[:, kv, :], ps[:, 3, 0:384], ACT.Copy).then_inc(S[1].free, 1)
                        act.wait_ge(S[0].free, S[0].freed[("in", L, i)])
                        act.wait_ge(sq_done, norm_no(L, 1, min(s, TILES - 1)))
                        if i:
                            act.wait_ge(sq2_done, TILES * L + i)
                        act.activation(junk[:, 0:256], proj[:, i % 2, 0:256], ACT.Square,
                                       accum_out=ssq[:, 8 + 2 * i:9 + 2 * i])
                        act.activation(junk[:, 256:384], proj[:, i % 2, C_CKV:C_CKV + 128], ACT.Square,
                                       accum_out=ssq[:, 9 + 2 * i:10 + 2 * i]).then_inc(sq2_done, 1)
                    if s >= 2 or s == TILES + 1:
                        for i in ([s - 2, 5] if s == TILES + 1 else [s - 2]):
                            kv = 4 if i == 5 else (5 if ORDER[i] == 4 else ORDER[i])
                            k0 = kv * P
                            act.wait_ge(T.full, T[("xp", L, i)])
                            if i < 5:
                                t0 = ORDER[i] * P
                                act.activation(cqT[:, :, t0:t0 + P], ps[:, 4, 0:256].rearrange("p (k n) -> p k n", k=2), ACT.Copy)
                                act.activation(ckvT[:, k0:k0 + P], ps[:, 4, 256:384], ACT.Copy)
                            else:
                                act.activation(ckvT[:, k0:k0 + P], ps[:, 4, 0:P], ACT.Copy)
                            act.activation(kpeT[0:ROPE, k0:k0 + P], ps[0:ROPE, 4, 384:512], ACT.Copy).then_inc(T.free, 1)
                            act.wait_ge(O.full, O[("xn", L, i)])
                            kn = ps[:, 6, 256:512] if i < 5 else ps[:, 6, 0:256]
                            if i < 5:
                                act.wait_ge(pad_set, 2 * L + 2)
                                act.activation(qnP[0:64, 0:4:2, t0:t0 + P],
                                               ps[0:64, 6, 0:256].rearrange("p (k n) -> p k n", k=2), ACT.Copy, scale=HEAD_SCALE)
                                act.activation(qnP[64:128, 1:4:2, t0:t0 + P],
                                               ps[64:128, 6, 0:256].rearrange("p (k n) -> p k n", k=2), ACT.Copy, scale=HEAD_SCALE)
                            act.activation(knT[:, :, k0:k0 + P], kn.rearrange("p (k n) -> p k n", k=2),
                                           ACT.Copy).then_inc(O.free, 1)
                meet(act, "act")
                attention(L, 2)
                meet(act, "act")
                for i in range(TILES + 1):
                    if i < TILES:
                        act.wait_ge(T.full, T[("uq", L, i)])
                        if i >= 2:
                            act.wait_ge(S[i % 2].full, S[i % 2][("qt", L, i - 2)])
                        act.activation(qt[:, i % 2, :], two(4, 768), ACT.Copy, scale=MLA_SCALE).then_inc(T.free, 1)
                    if i in (1, 3):
                        act.wait_ge(S[1].full, S[1][("uk", L, i)])
                        act.activation(kT[0:64, 2 * i, :], two(2, 768)[0:64], ACT.Copy)
                        act.activation(kT[0:64, 2 * i + 1, :], two(2, 768)[64:128], ACT.Copy).then_inc(S[1].free, 1)
                    if i % 2 == 0:
                        act.wait_ge(O.full, O[("uv", L, i)])
                        act.activation(v_mla[:, i, :], ps[:, 6, :], ACT.Copy).then_inc(O.free, 1)
                    if i >= 1 and (i - 1) % 2 == 0:
                        t0 = ORDER[i - 1] * P
                        act.wait_ge(S[0].full, S[0][("qt", L, i - 1)])
                        act.activation(qT[0:QK, :, t0:t0 + P], two(0)[0:QK].rearrange("p (h n) -> p h n", h=8),
                                       ACT.Copy).then_inc(S[0].free, 1)
                meet(act, "act")
                attention(L, 4)
                meet(act, "act")
                for s in range(TILES + 3):
                    if s < TILES:
                        if s >= 2:
                            act.wait_ge(S[s % 2].full, S[s % 2][("out", L, s - 2)])
                        act.wait_ge(T.full, T[("ho", L, s)])
                        act.activation(hoT[:, s % 2, 0:512], ps[:, 4, :], ACT.Copy).then_inc(T.free, 1)
                    if 2 <= s < TILES + 2:
                        act.wait_ge(res_done, TILES * L + s - 1)
                        if s > 2:
                            act.wait_ge(sq_done, norm_no(L, 5, s - 3))
                        act.activation(junk5, xt5[:, s % 2, :], ACT.Square,
                                       accum_out=ssq[:, s - 2:s - 1]).then_inc(sq_done, 1)
                    if s >= 3:
                        i = s - 3
                        if i >= 2:
                            act.wait_ge(routed, 4 * L + i - 1)
                        act.wait_ge(T.full, T[("h2", L, i)])
                        act.activation(h2T[:, i % 2, 0:512], ps[:, 4, :], ACT.Copy).then_inc(T.free, 1)
                act.wait_ge(rx1, L + 1)
                act.activation(r_ge, r_gd, ACT.Exp).then_inc(rx1_done, 1)
                act.wait_ge(rx2, L + 1)
                act.activation(r_e2, r_d2, ACT.Exp).then_inc(rx2_done, 1)
                meet(act, "act")
                n_ov = act.value_load(ctl[0:1, 0:1], min_val=0, max_val=NOVF)
                E0 = NE * L

                def x_copy(e, b, early):
                    if not early:
                        act.wait_ge(e_h, E0 + e - 1)
                    act.wait_ge(e_xT, E0 + e + 1)
                    act.activation(xgT[:, b, 0:512], ps[:, 4, :], ACT.Copy).then_inc(e_xTa, 1)

                def silu(e, b):
                    act.wait_ge(e_h, E0 + e + 1)
                    act.activation(sg[:, b, :], ps[:, b, 0:FF], ACT.Silu).then_inc(e_sg, 1)

                def y_copy(e, b, early):
                    act.wait_ge(e_d, E0 + e + 1)
                    if not early:
                        act.wait_ge(ys_out[b], 16 * (E0 // 2) + (e - b) * 8)
                    act.activation(yb[:, b, 0:512], ps[:, 2, :], ACT.Copy).then_inc(e_ya, 1)

                x_copy(0, 0, True)
                silu(0, 0)
                x_copy(1, 1, True)
                silu(1, 1)
                x_copy(2, 0, False)
                y_copy(0, 0, True)
                silu(2, 0)
                x_copy(3, 1, False)
                y_copy(1, 1, True)
                with act.Fori(3, NE - 1, 2) as e0:
                    for j in range(2):
                        e, b = e0 + j, 1 - j
                        silu(e, b)
                        x_copy(e + 1, 1 - b, False)
                        y_copy(e - 1, 1 - b, False)
                silu(15, 1)
                y_copy(14, 0, False)
                y_copy(15, 1, False)
                with act.If(n_ov > 0):
                    act.wait_ge(ys_out[0], 8 * (E0 + NE))
                    with act.Fori(0, NOVF) as c:
                        n = c + 1
                        act.wait_ge(ov[L]["xT"], n)
                        act.activation(xgT[:, 0, 0:512], ps[:, 4, :], ACT.Copy)
                        act.activation(xgT[:, 0, 512:1024], ps[:, 5, :], ACT.Copy).then_inc(ov[L]["xTe"], 1)
                        act.wait_ge(ov[L]["h"], n)
                        act.activation(sg[:, 0, :], ps[:, 0, 0:FF], ACT.Silu).then_inc(ov[L]["sg"], 1)
                        act.wait_ge(ov[L]["d"], n)
                        act.activation(yb[:, 0, :], two(2), ACT.Copy).then_inc(ov[L]["y"], 1)
                meet(act, "act")
                for i in range(TILES):
                    t = ORDER[i]
                    act.wait_ge(y_in[i], 32 * (L + 1))
                    act.activation(y1[:, i, :], y1[:, i, :], ACT.Copy, scale=wts[:, t, 0:1]).then_inc(y1_scaled, 1)
                if L == DEPTH - 1:
                    j7 = junk7.bitcast(BF16)
                    for i in range(TILES):
                        act.wait_ge(comb_done, TILES * L + i + 1)
                        if i:
                            act.wait_ge(fin_sq, i)
                        act.activation(j7, x7[:, i, :], ACT.Square,
                                       accum_out=ssq[:, 24 + i:25 + i]).then_inc(fin_sq, 1)
                meet(act, "act")

        @block.gpsimd
        def _(pool):
            def rstd(ins, outs, scale):
                then(pool, "pool", pool.tensor_scalar(outs, ins, scale, EPS, ALU.mult, ALU.add))
                w = outs.shape[-1]
                return pool.tensor_tensor(outs, outs, mhalf[:, 0:w], ALU.pow)

            def last_step(L, i):
                t = ORDER[i]
                if L < DEPTH - 1:
                    pool.wait_ge(comb_done, TILES * L + i + 1)
                    pool.dma_start(xbuf[t * P:(t + 1) * P, :], x7[:, i, :]).then_inc(x7_out, 16)
                else:
                    pool.wait_ge(fin_sq, i + 1)
                    rstd(ssq[:, 24 + i:25 + i], rsd[:, 24 + i:25 + i], 1.0 / D).then_inc(fin_rs, 1)
                    pool.wait_ge(fin_done, i + 1)
                    dst = t_out["y_prompt"] if t == 4 else t_out["y_sample"][t * P:(t + 1) * P, :]
                    pool.dma_start(dst, x7[:, i, :]).then_inc(x7_out, 16)

            pool.memset(sc[:, :, :], 0.0).then_inc(zero_set, 1)
            pool.memset(zeros[:, :], 0.0).then_inc(zero_set, 1)
            pool.memset(brow[:, :, :], 0.0).then_inc(half_set, 1)
            pool.memset(mhalf[:, :], -0.5).then_inc(half_set, 1)
            pool.wait_ge(half_set, 2)
            pool.wait_ge(zero_set, 2)
            pool.sem_inc(sc_set, 1)

            def vector_loads(L):
                bm = t_in["b_mod"][L].rearrange("(g i n) -> i g n", g=3, i=4)
                for i in range(4):
                    pool.dma_start(brow[32 * i:32 * i + 2, :, :],
                                   bm[i:i + 1].broadcast_to([2, 3, 512])).then_inc(bmod_in, 16)
                pool.dma_start(nrm[:, :], t_in["norm1"][L:L + 1, :].broadcast_to([P, D])).then_inc(nrm_in, 16)
                pool.dma_start(gqa[:, :], t_in["g_qa"][L:L + 1, :].broadcast_to([P, 256])).then_inc(vec_in, 16)
                pool.dma_start(gkva[:, :], t_in["g_kva"][L:L + 1, :].broadcast_to([P, 128])).then_inc(vec_in, 16)
                pool.dma_start(sink[:, :], t_in["swa_sink"][L:L + 1, :].broadcast_to([P, 4])).then_inc(vec_in, 16)

            vector_loads(0)
            for L in range(DEPTH):
                src = t_in["x0"] if L == 0 else xbuf

                def x_load(i):
                    t = ORDER[i]
                    pool.dma_start(xt[:, i % 2, :], src[t * P:(t + 1) * P, :]).then_inc(xt_in[i % 2], 16)

                x_load(0)
                x_load(1)
                for at, w, name in ((0, 128, "cache_mla_ckv"), (128, 32, "cache_mla_kpe"),
                                    (160, 128, "cache_swa_k"), (288, 256, "cache_na_k")):
                    pool.dma_start(ck[:, at:at + w], t_in[name][L]).then_inc(cache_in, 16)
                pool.dma_start(v_loc[:, 4, :], t_in["cache_v"][L]).then_inc(cache_in, 16)
                pool.memset(qsP, 0.0).then_inc(pad_set, 1)
                pool.memset(qnP, 0.0).then_inc(pad_set, 1)
                for s in range(TILES + 1):
                    if s < TILES:
                        pool.wait_ge(sq_done, norm_no(L, 1, s))
                        rstd(ssq[:, s:s + 1], rsd[:, s:s + 1], 1.0 / D).then_inc(rs_done, 1)
                        pool.wait_ge(hA_done, norm_no(L, 1, s))
                        pool.tensor_tensor(xt[:, s % 2, :], xt[:, s % 2, :], rowB, ALU.add).then_inc(h_done, 1)
                    if s >= 1:
                        i = s - 1
                        pool.wait_ge(sq2_done, TILES * L + i + 1)
                        a = 8 + 2 * i
                        then(pool, "pool", pool.tensor_scalar(rsd[:, a:a + 1], ssq[:, a:a + 1], 1.0 / 256, EPS, ALU.mult, ALU.add))
                        then(pool, "pool", pool.tensor_scalar(rsd[:, a + 1:a + 2], ssq[:, a + 1:a + 2], 1.0 / 128, EPS, ALU.mult, ALU.add))
                        pool.tensor_tensor(rsd[:, a:a + 2], rsd[:, a:a + 2], mhalf[:, 0:2], ALU.pow).then_inc(rs2_done, 1)
                    if s == 1:
                        pool.wait_ge(post_done, TILES * L + 1)
                        pool.wait_ge(S[1].free, S[1].freed[("in", L, 0)])
                        for name, src_ap in (("ckv", proj[:, 0, C_CKV:C_CKV + 128]), ("kpe", proj[:, 0, C_KPE:C_KPE + 32]),
                                             ("ks", proj[:, 0, C_KS:C_KS + 128]), ("kn", proj[:, 0, C_KN:C_KN + 256]),
                                             ("vs", v_loc[:, 5, 0:128]), ("vn", v_loc[:, 5, 128:384])):
                            pool.dma_start(t_out[name][L], src_ap).then_inc(ctx_out, 16)
                    if 1 <= s < TILES - 1:
                        pool.wait_ge(T.full, T[("h", L, s - 1)])
                        x_load(s + 1)
                pool.wait_ge(ctx_out, 96 * (L + 1))
                meet(pool, "pool")
                if L == 0:
                    for rows in (slots_x, slots_y[NE * P:SLOTS, :]):
                        fill = rows.shape[0] // P * D // 256
                        pool.dma_start(rows.rearrange("(p c) (a n) -> p (c a) n", p=P, n=256),
                                       zeros[:, :].unsqueeze(1).broadcast_to([P, fill, 256])).then_inc(zero_out, 16)
                pool.dma_start(nrm[:, :], t_in["norm2"][L:L + 1, :].broadcast_to([P, D])).then_inc(nrm_in, 16)
                mad = cst["madd"].unsqueeze(1).broadcast_to([P, 15, 64])
                for h in range(4):
                    pool.wait_ge(bias_mul, 4 * L + h + 1)
                    bh = bias[:, h, :].rearrange("p (j c) -> p j c", j=15)
                    pool.tensor_tensor(bh, bh, mad, ALU.add).then_inc(bias_done, 1)
                meet(pool, "pool")
                meet(pool, "pool")
                meet(pool, "pool")
                def x5_load(i):
                    t = ORDER[i]
                    pool.dma_start(xt5[:, i % 2, :], src[t * P:(t + 1) * P, :]).then_inc(xt_in[i % 2], 16)

                x5_load(0)
                x5_load(1)
                for i in range(TILES):
                    t = ORDER[i]
                    pool.wait_ge(xt_in[i % 2], x_no(L, 5, i))
                    pool.wait_ge(res_mul, TILES * L + i + 1)
                    pool.tensor_tensor(xt5[:, i % 2, :], xt5[:, i % 2, :], tmp5, ALU.add).then_inc(res_done, 1)
                    pool.wait_ge(res_done, TILES * L + i + 1)
                    pool.dma_start(xbuf[t * P:(t + 1) * P, :], xt5[:, i % 2, :]).then_inc(xs_out, 16)
                    pool.wait_ge(sq_done, norm_no(L, 5, i))
                    rstd(ssq[:, i:i + 1], rsd[:, i:i + 1], 1.0 / D).then_inc(rs_done, 1)
                    pool.wait_ge(hA_done, norm_no(L, 5, i))
                    pool.tensor_tensor(h2[:, t, :], h2[:, t, :], rowB2[:, int(t == 4), :], ALU.add).then_inc(h_done, 1)
                    if i + 2 < TILES:
                        pool.wait_ge(xs_out, 16 * (TILES * L + i + 1))
                        x5_load(i + 2)
                pool.wait_ge(xs_out, 16 * TILES * (L + 1))
                if L == 0:
                    pool.wait_ge(zero_out, 32)
                pool.wait_ge(idx_done, L + 1)
                for j in range(2):
                    for t in range(TILES):
                        pool.indirect_dma_start(slots_x, bass.IndirectOffsetOnAxis(ap=sidx[:, j * TILES + t:j * TILES + t + 1], axis=0),
                                                h2[:, t, :], None).then_inc(scat_out, 16)
                pool.wait_ge(scat_out, 160 * (L + 1))
                meet(pool, "pool")
                n_ov = pool.value_load(ctl[0:1, 0:1], min_val=0, max_val=NOVF)
                E0 = NE * L
                with pool.Fori(0, NE // 2) as pair:
                    for j in range(2):
                        e = pair * 2 + j
                        row = pair * (2 * P) + j * P
                        pool.wait_ge(e_ya, e + (E0 + 1))
                        pool.wait_ge(e_yd, e + (E0 + 1))
                        pool.dma_start(slots_y[bass.ds(row, P), :], yb[:, j, :]).then_inc(ys_out[j], 16)
                for j in range(2):
                    pool.wait_ge(ys_out[j], 16 * (E0 + NE) // 2)
                with pool.If(n_ov > 0):
                    for c in range(NOVF):
                        row = (NE + c) * P
                        pool.wait_ge(ov[L]["y"], c + 1)
                        pool.dma_start(slots_y[row:row + P, :], yb[:, 0, :]).then_inc(ov[L]["out"], 16)
                        pool.wait_ge(ov[L]["out"], 16 * (c + 1))
                meet(pool, "pool")
                for i in range(TILES):
                    t = ORDER[i]
                    for j, dst in enumerate((y1, y2)):
                        pool.indirect_dma_start(dst[:, i, :], None, slots_y,
                                                bass.IndirectOffsetOnAxis(ap=sidx[:, j * TILES + t:j * TILES + t + 1], axis=0)
                                                ).then_inc(y_in[i], 16)
                if L < DEPTH - 1:
                    vector_loads(L + 1)
                else:
                    pool.dma_start(nrm[:, :], t_in["norm_final"].unsqueeze(0).broadcast_to([P, D])).then_inc(nrm_in, 16)
                for i in range(TILES):
                    pool.wait_ge(comb, TILES * L + i + 1)
                    pool.tensor_tensor(x7[:, i, :], x7[:, i, :], y2[:, i, :], ALU.add).then_inc(comb_done, 1)
                    if L < DEPTH - 1 or i:
                        last_step(L, i - (L == DEPTH - 1))
                if L == DEPTH - 1:
                    last_step(L, TILES - 1)
                pool.wait_ge(x7_out, 16 * TILES * (L + 1))
                meet(pool, "pool")

        @block.vector
        def _(dve):
            TT, TS, STT = dve.tensor_tensor, dve.tensor_scalar, dve.scalar_tensor_tensor

            def mod_rows(L, g):
                dve.wait_ge(M.full, M[("mod", L, g)])
                if g == 0:
                    dve.wait_ge(bmod_in, 64 * (L + 1))
                TT(mrow[:, g, :], ps[:, 7, :], brow[:, g, :], ALU.add).then_inc(mods_done, 1)
                dve.wait_ge(mods_done, 3 * L + g + 1)
                dve.sem_inc(M.free, 1)

            bcn = [0]

            def row_from(L, kind, vec, half, dst, scale_norm=False):
                lane, b = ((O, 6), (M, 7))[bcn[0] % 2]
                bcn[0] += 1
                dve.wait_ge(lane.full, lane[("bc", L, kind, vec, half)])
                d = dst[:, half * 512:(half + 1) * 512]
                if scale_norm:
                    ins = STT(d, ps[:, b, :], 1.0, nrm[:, half * 512:(half + 1) * 512], ALU.add, ALU.mult)
                else:
                    ins = dve.tensor_copy(d, ps[:, b, :])
                return ins.then_inc(lane.free, 1)

            def rope(x, cos, sin, tmp, heads, dim):
                h4 = dim // 4

                def v(a):
                    return a.rearrange("p (h d) -> p h d", h=heads)

                def halves(a, j):
                    return a.rearrange("p (m s d) -> p m s d", s=2, d=h4)[:, :, j, :]

                def table(a, j):
                    return a.rearrange("p (m s d) -> p m s d", s=2, d=h4)[:, :, j, :].unsqueeze(1).broadcast_to([P, heads, 2, h4])

                n = heads * dim
                TT(v(tmp[:, 0, 0:n]), v(x), cos.unsqueeze(1).broadcast_to([P, heads, dim]), ALU.mult)
                for j in range(2):
                    o = halves(tmp[:, 1, 0:n], j).rearrange("p (h a) d -> p h a d", a=2)
                    i = halves(x, 1 - j).rearrange("p (h a) d -> p h a d", a=2)
                    last = TT(o, i, table(sin, j), ALU.mult)
                then(dve, "dve", last)
                return TT(x, tmp[:, 0, 0:n], tmp[:, 1, 0:n], ALU.add)

            def attention(L, phase):
                units = UNITS[phase]

                def maximum(u):
                    un, w = units[u], units[u]["n"] * P
                    dve.wait_ge(S[u % 2].full, S[u % 2][("s", L, phase, u)])
                    src = two(2 * (u % 2), w)
                    mx, m2, nm = (stat[n][:, u % 8:u % 8 + 1] for n in ("mx", "m2", "nm"))
                    if "mask" in un and u >= 2:
                        dve.wait_ge(S[u % 2].free, S[u % 2].freed[("s", L, phase, u - 2)])
                    if un["kind"] == "swa":
                        then(dve, "dve", dve.tensor_tensor_reduce(sB[:, u % 2, 0:w], src, un["mask"], 1.0,
                                                                  sink[:, un["h"]:un["h"] + 1], ALU.add, ALU.max, mx))
                        TS(nm, mx, -1.0, None, ALU.mult).then_inc(nmax_done, 1)
                    elif un["kind"] == "na":
                        then(dve, "dve", TS(sB[:, u % 2, 512:640], src[:, 512:640], 1.0, NEG, ALU.mult, ALU.max,
                                            accum_out=m2))
                        then(dve, "dve", dve.tensor_tensor_reduce(sB[:, u % 2, 0:512], src[:, 0:512], un["mask"], 1.0,
                                                                  m2, ALU.add, ALU.max, mx))
                        TS(nm, mx, -1.0, None, ALU.mult).then_inc(nmax_done, 1)
                    elif un["kind"] == "swa_ctx":
                        then(dve, "dve", dve.tensor_reduce(mx, src, AX.X, ALU.max))
                        TS(nm, mx, sink[:, un["h"]:un["h"] + 1], -1.0, ALU.max, ALU.mult).then_inc(nmax_done, 1)
                    else:
                        dve.tensor_reduce(nm, src, AX.X, ALU.max, negate=True).then_inc(nmax_done, 1)

                def copy(u):
                    a, d = split(units[u]["n"])
                    dve.wait_ge(T.full, T[("p", L, phase, u)])
                    if u >= 2:
                        dve.wait_ge(O.full, O[("o", L, phase, u - 2)])
                    dve.tensor_copy(pT[phase][:, u % 2, 0:a * P], ps[:, 4, 0:a * P]).then_inc(T.free, 1)

                def norm(u):
                    un = units[u]
                    sm, es, ri = (stat[n][:, u % 8:u % 8 + 1] for n in ("sm", "es", "ri"))
                    if un["kind"].startswith("swa"):
                        then(dve, "dve", TT(sm, sm, es, ALU.add))
                    then(dve, "dve", dve.reciprocal(ri, sm))
                    dve.wait_ge(O.full, O[("o", L, phase, u)])
                    TS(heads[:, un["t"], un["col"]:un["col"] + 64], ps[:, 6, 0:64], ri, None,
                       ALU.mult).then_inc(O.free, 1)

                for s in range(len(units) + 2):
                    if s < len(units):
                        maximum(s)
                    if s >= 2:
                        norm(s - 2)
                    if 1 <= s <= len(units):
                        copy(s - 1)
                    if phase == 2 and s in (18, 32):
                        mod_rows(L, 1 if s == 18 else 2)

            dve.wait_ge(const_in, 16)
            c32, s32 = (cst[n].rearrange("p (t d) -> p t d", t=4) for n in ("cos32", "sin32"))
            c64, s64 = (cst[n].rearrange("p (t d) -> p t d", t=4) for n in ("cos64", "sin64"))
            dve.wait_ge(half_set, 2)
            for L in range(DEPTH):
                if L == 0:
                    mod_rows(L, 0)
                dve.wait_ge(nrm_in, 16 * (2 * L + 1))
                dve.wait_ge(small_in, 48 * (L + 1))
                dve.wait_ge(vec_in, 48 * (L + 1))
                for s in range(TILES + 2):
                    if s < 2:
                        if s == 1:
                            dve.wait_ge(h_done, norm_no(L, 1, 0))
                        for half in range(2):
                            row_from(L, 1 - s, 0, half, rowB)
                        for half in range(2):
                            last = row_from(L, 1 - s, 1, half, rowA, True)
                        dve.wait_ge(O.free, O.freed[("bc", L, 1 - s, 1, 0)])
                        dve.wait_ge(M.free, M.freed[("bc", L, 1 - s, 1, 1)])
                    if s < TILES:
                        dve.wait_ge(rs_done, norm_no(L, 1, s))
                        STT(xt[:, s % 2, :], xt[:, s % 2, :], rsd[:, s:s + 1], rowA, ALU.mult,
                            ALU.mult).then_inc(hA_done, 1)
                    if 1 <= s <= TILES:
                        i = s - 1
                        q = proj[:, i % 2, :]
                        dve.wait_ge(S[0].full, S[0][("in", L, i)])
                        if i >= 2:
                            dve.wait_ge(T.full, T[("xp", L, i - 2)])
                            if i == 2:
                                dve.wait_ge(ctx_out, 96 * (L + 1))
                        dve.tensor_copy(q[:, 0:416], ps[:, 0, 0:416])
                        dve.tensor_copy(q[:, 416:800], ps[:, 1, 0:384]).then_inc(S[0].free, 1)
                        dve.wait_ge(S[0].free, S[0].freed[("in", L, i)])
                        a = 8 + 2 * i
                        if ORDER[i] != 4:
                            t = ORDER[i]
                            then(dve, "dve", rope(q[:, C_QS:C_QS + 384], c64[:, t, :], s64[:, t, :], rt, 6, 64))
                            then(dve, "dve", rope(q[:, C_KPE:C_KPE + 32], c32[:, t, :], s32[:, t, :], rt, 1, 32))
                        dve.wait_ge(rs2_done, TILES * L + i + 1)
                        STT(q[:, 0:256], q[:, 0:256], rsd[:, a:a + 1], gqa[:, :], ALU.mult, ALU.mult)
                        STT(q[:, C_CKV:C_CKV + 128], q[:, C_CKV:C_CKV + 128], rsd[:, a + 1:a + 2], gkva[:, :],
                            ALU.mult, ALU.mult).then_inc(post_done, 1)
                    if s >= 2:
                        for i in ([s - 2, 5] if s == TILES + 1 else [s - 2]):
                            kv = 4 if i == 5 else (5 if ORDER[i] == 4 else ORDER[i])
                            dve.wait_ge(T.full, T[("xp", L, i)])
                            if i < 5:
                                t0 = ORDER[i] * P
                                dve.wait_ge(pad_set, 2 * L + 2)
                                for lo in (0, 64):
                                    TS(qsP[lo:lo + 64, lo // 32:lo // 32 + 2, t0:t0 + P],
                                       ps[lo:lo + 64, 5, 0:256].rearrange("p (k n) -> p k n", k=2), HEAD_SCALE, None, ALU.mult)
                            ks = ps[:, 5, 256:384] if i < 5 else ps[:, 5, 0:P]
                            dve.tensor_copy(ksT[:, kv * P:(kv + 1) * P], ks).then_inc(T.free, 1)
                meet(dve, "dve")
                m01 = cst["m01"].unsqueeze(1).broadcast_to([P, 7, 64])
                for h in range(4):
                    dve.wait_ge(S[h % 2].full, S[h % 2][("bias", L, h)])
                    m01f = cst["m01"].unsqueeze(1)
                    for n in range(2):
                        bk = ps[:, 2 * (h % 2) + n, :]
                        o = bias[:, h, n * 480:(n + 1) * 480]
                        if n == 0:
                            TT(o[:, 0:448].rearrange("p (j c) -> p j c", j=7), bk[:, 0:448].rearrange("p (j c) -> p j c", j=7),
                               m01, ALU.mult)
                            TT(o[:, 448:480], bk[:, 448:480], cst["m01"][:, 0:32], ALU.mult)
                        else:
                            TT(o[:, 0:32], bk[:, 0:32], cst["m01"][:, 32:64], ALU.mult)
                            last = TT(o[:, 32:480].rearrange("p (j c) -> p j c", j=7),
                                      bk[:, 32:480].rearrange("p (j c) -> p j c", j=7), m01, ALU.mult)
                    then(dve, "dve", last)
                    dve.sem_inc(S[h % 2].free, 1)
                    dve.sem_inc(bias_mul, 1)
                attention(L, 2)
                meet(dve, "dve")
                for h in range(MLA_H):
                    dve.tensor_copy(kT[64:96, h, :], kpeT[0:ROPE, :])
                for i in range(TILES + 1):
                    if i in (0, 2):
                        dve.wait_ge(S[0].full, S[0][("uk", L, i)])
                        dve.tensor_copy(kT[0:64, 2 * i, :], two(0, 768)[0:64])
                        dve.tensor_copy(kT[0:64, 2 * i + 1, :], two(0, 768)[64:128]).then_inc(S[0].free, 1)
                    if i % 2 == 1:
                        dve.wait_ge(M.full, M[("uv", L, i)])
                        dve.tensor_copy(v_mla[:, i, :], ps[:, 7, :]).then_inc(M.free, 1)
                    if i < TILES:
                        dve.wait_ge(T.free, T.freed[("uq", L, i)])
                        t = ORDER[i]
                        if t == 4:
                            dve.sem_inc(q_done, 1)
                        else:
                            x = qt[:, i % 2, :].rearrange("p (h d) -> p h d", h=MLA_H)[:, :, NOPE:QK]
                            dve.wait_ge(q_done, TILES * L + i)
                            t1 = rq[:, 0, :].rearrange("p (h d) -> p h d", h=MLA_H)
                            t2 = rq[:, 1, :].rearrange("p (h d) -> p h d", h=MLA_H)
                            TT(t1, x, c32[:, t, :].unsqueeze(1).broadcast_to([P, MLA_H, ROPE]), ALU.mult)
                            for ax in range(2):
                                for j in range(2):
                                    o0, i0 = 16 * ax + 8 * j, 16 * ax + 8 * (1 - j)
                                    last = TT(t2[:, :, o0:o0 + 8], x[:, :, i0:i0 + 8],
                                              s32[:, t, o0:o0 + 8].unsqueeze(1).broadcast_to([P, MLA_H, 8]), ALU.mult)
                            then(dve, "dve", last)
                            TT(x, t1, t2, ALU.add).then_inc(q_done, 1)
                    if i >= 1 and (i - 1) % 2 == 1:
                        t0 = ORDER[i - 1] * P
                        dve.wait_ge(S[1].full, S[1][("qt", L, i - 1)])
                        dve.tensor_copy(qT[0:QK, :, t0:t0 + P], two(2)[0:QK].rearrange("p (h n) -> p h n", h=8)).then_inc(S[1].free, 1)
                meet(dve, "dve")
                attention(L, 4)
                meet(dve, "dve")
                dve.wait_ge(nrm_in, 16 * (2 * L + 2))
                for vec, dst in ((2, rowG1), (4, rowA2), (3, rowB2)):
                    for kind in (1, 0):
                        for half in range(2):
                            last = row_from(L, kind, vec, half, dst[:, kind, :], vec == 4)
                for lane in (O, M):
                    dve.wait_ge(lane.free, lane.freed[("bc", L, 0, 3, 0 if lane is O else 1)])

                for s in range(TILES + 3):
                    if s < TILES:
                        if s >= 2:
                            dve.wait_ge(S[s % 2].full, S[s % 2][("out", L, s - 2)])
                        dve.wait_ge(T.full, T[("ho", L, s)])
                        dve.tensor_copy(hoT[:, s % 2, 512:1024], ps[:, 5, :]).then_inc(T.free, 1)
                    if 1 <= s <= TILES:
                        i = s - 1
                        kind = int(ORDER[i] == 4)
                        dve.wait_ge(S[i % 2].full, S[i % 2][("out", L, i)])
                        if i >= 1:
                            dve.wait_ge(res_done, TILES * L + i)
                        then(dve, "dve", TT(tmp5, two(2 * (i % 2)), rowG1[:, kind, :], ALU.mult))
                        dve.sem_inc(S[i % 2].free, 1)
                        dve.sem_inc(res_mul, 1)
                    if 2 <= s < TILES + 2:
                        i = s - 2
                        dve.wait_ge(rs_done, norm_no(L, 5, i))
                        STT(h2[:, ORDER[i], :], xt5[:, i % 2, :], rsd[:, i:i + 1], rowA2[:, int(ORDER[i] == 4), :],
                            ALU.mult, ALU.mult).then_inc(hA_done, 1)
                    if s >= 3:
                        i = s - 3
                        if i >= 2:
                            dve.wait_ge(routed, 4 * L + i - 1)
                        dve.wait_ge(T.full, T[("h2", L, i)])
                        dve.tensor_copy(h2T[:, i % 2, 512:1024], ps[:, 5, :]).then_inc(T.free, 1)
                def go(ins):
                    then(dve, "dve", ins)

                def b4(a):
                    return a.unsqueeze(2).broadcast_to([P, TILES, 4])

                w4 = cst["w4"].unsqueeze(1).broadcast_to([P, TILES, 4])

                def first_max(x, m, oh):
                    go(dve.tensor_reduce(m, x, AX.X, ALU.max))
                    go(TT(r_eq, x, b4(m), ALU.is_equal))
                    go(TT(r_eq, r_eq, w4, ALU.mult))
                    go(dve.tensor_reduce(r_g, r_eq, AX.X, ALU.max))
                    go(TT(oh, r_eq, b4(r_g), ALU.is_equal))

                dve.wait_ge(O.full, O[("rt", L)])
                go(dve.tensor_copy(r_lg.rearrange("p a b -> p (a b)"), ps[:, 6, 0:100]))
                dve.sem_inc(O.free, 1)
                grp = r_lg[:, :, 0:4]
                first_max(grp, r_m, r_oh)
                go(TT(r_gd, grp, b4(r_m), ALU.subtract))
                dve.sem_inc(rx1, 1)
                elog = r_lg[:, :, 4:20].rearrange("p t (g e) -> p t g e", g=4)
                go(TT(r_prod, elog, r_oh.unsqueeze(3).broadcast_to([P, TILES, 4, 4]), ALU.mult))
                go(dve.tensor_reduce(r_sel, r_prod.rearrange("p t g e -> p t e g"), AX.X, ALU.add))
                first_max(r_sel, r_m, r_oh1)
                go(STT(r_sel, r_oh1, NEG, r_sel, ALU.mult, ALU.add))
                go(dve.tensor_copy(r_d2, r_m))
                first_max(r_sel, r_m, r_oh2)
                go(TT(r_d2, r_m, r_d2, ALU.subtract))
                dve.sem_inc(rx2, 1)
                for c, oh in ((r_c1, r_oh1), (r_c2, r_oh2)):
                    go(TT(c.rearrange("p t (g e) -> p t g e", g=4), r_oh.unsqueeze(3).broadcast_to([P, TILES, 4, 4]),
                          oh.unsqueeze(2).broadcast_to([P, TILES, 4, 4]), ALU.mult))
                TT(r_T, r_c1, r_c2, ALU.add).then_inc(pick_done, 1)
                dve.wait_ge(rx1_done, L + 1)
                go(dve.tensor_reduce(r_g, r_ge, AX.X, ALU.add))
                dve.wait_ge(rx2_done, L + 1)
                go(TS(r_m, r_e2, 1.0, None, ALU.add))
                go(TT(r_m, r_m, r_g, ALU.mult))
                go(dve.reciprocal(wts[:, :, 0], r_m))
                go(TT(wts[:, :, 1], wts[:, :, 0], r_e2, ALU.mult))
                dve.wait_ge(M.full, M[("cnt", L)])
                go(dve.tensor_copy(r_tmp.rearrange("p a b -> p (a b)"), ps[:, 7, 0:80]))
                dve.sem_inc(M.free, 1)
                dve.wait_ge(O.full, O[("pos", L)])
                go(dve.tensor_copy(r_pos.rearrange("p a b -> p (a b)"), ps[:, 6, 0:80]))
                dve.sem_inc(O.free, 1)
                go(dve.tensor_copy(r_n, r_tmp[:, 0, :]))
                for t in range(1, TILES):
                    go(TT(r_pos[:, t, :], r_pos[:, t, :], r_n, ALU.add))
                    go(TT(r_n, r_n, r_tmp[:, t, :], ALU.add))
                go(TS(r_nov, r_n, float(CAP), None, ALU.is_gt))
                for k in range(1, TILES - 1):
                    go(STT(r_nov, r_n, float(CAP + k * P), r_nov, ALU.is_gt, ALU.add))
                less = cst["less"].rearrange("p (a b) -> p a b", a=NE)
                go(TT(r_pr, r_nov.unsqueeze(1).broadcast_to([P, NE, NE]), less, ALU.mult))
                go(dve.tensor_reduce(r_ovb, r_pr, AX.X, ALU.add))
                go(STT(r_dl, r_ovb, float(P), cst["ovshift"], ALU.mult, ALU.add))
                go(TS(r_ge5, r_pos, float(CAP), None, ALU.is_ge))
                go(TT(r_ge5, r_ge5, r_dl.unsqueeze(1).broadcast_to([P, TILES, NE]), ALU.mult))
                go(TT(r_pos, r_pos, cst["ebase"].unsqueeze(1).broadcast_to([P, TILES, NE]), ALU.add))
                go(TT(r_pos, r_pos, r_ge5, ALU.add))
                for j, c in enumerate((r_c1, r_c2)):
                    go(TT(r_tmp, r_pos, c, ALU.mult))
                    go(dve.tensor_reduce(r_s[:, j, :], r_tmp, AX.X, ALU.add))
                go(dve.tensor_copy(sidx[:, :], r_s.rearrange("p a b -> p (a b)")))
                go(dve.tensor_reduce(r_ctl[:, 0:1], r_nov, AX.X, ALU.add))
                go(TT(r_ovb, r_ovb, r_nov, ALU.add))
                go(TT(r_ind, r_ovb.unsqueeze(1).broadcast_to([P, NOVF, NE]),
                      cst["chunk"].unsqueeze(2).broadcast_to([P, NOVF, NE]), ALU.is_le))
                go(dve.tensor_reduce(r_ctl[:, 1:1 + NOVF], r_ind, AX.X, ALU.add))
                go(TS(r_ctl[:, 1:1 + NOVF], r_ctl[:, 1:1 + NOVF], float(NE - 1), None, ALU.min))
                dve.tensor_copy(ctl[:, 0:1 + NOVF], r_ctl[:, 0:1 + NOVF]).then_inc(idx_done, 1)
                meet(dve, "dve")
                n_ov = dve.value_load(ctl[0:1, 0:1], min_val=0, max_val=NOVF)
                E0 = NE * L

                def x_copy(e, b, early):
                    if not early:
                        dve.wait_ge(e_h, E0 + e - 1)
                    dve.wait_ge(e_xT, E0 + e + 1)
                    dve.tensor_copy(xgT[:, b, 512:1024], ps[:, 5, :]).then_inc(e_xTd, 1)

                def gate(e, b):
                    dve.wait_ge(e_sg, E0 + e + 1)
                    TT(hid[:, b, :], sg[:, b, :], ps[:, b, FF:2 * FF], ALU.mult).then_inc(e_hid, 1)

                def hid_copy(e, b, early):
                    dve.wait_ge(e_hT, E0 + e + 1)
                    if not early:
                        dve.wait_ge(e_d, E0 + e - 1)
                    dve.tensor_copy(hidT[:, b, :], ps[:, 6, 0:FF]).then_inc(e_hTe, 1)

                def y_copy(e, b, early):
                    dve.wait_ge(e_d, E0 + e + 1)
                    if not early:
                        dve.wait_ge(ys_out[b], 8 * E0 + 8 * (e - b))
                    dve.tensor_copy(yb[:, b, 512:1024], ps[:, 3, :]).then_inc(e_yd, 1)

                x_copy(0, 0, True)
                gate(0, 0)
                x_copy(1, 1, True)
                hid_copy(0, 0, True)
                gate(1, 1)
                x_copy(2, 0, False)
                y_copy(0, 0, True)
                hid_copy(1, 1, True)
                gate(2, 0)
                x_copy(3, 1, False)
                y_copy(1, 1, True)
                hid_copy(2, 0, False)
                with dve.Fori(3, NE - 1, 2) as e0:
                    for j in range(2):
                        e, b = e0 + j, 1 - j
                        gate(e, b)
                        x_copy(e + 1, 1 - b, False)
                        y_copy(e - 1, 1 - b, False)
                        hid_copy(e, b, False)
                gate(15, 1)
                y_copy(14, 0, False)
                hid_copy(15, 1, False)
                y_copy(15, 1, False)
                with dve.If(n_ov > 0):
                    with dve.Fori(0, NOVF) as c:
                        n = c + 1
                        dve.wait_ge(ov[L]["sg"], n)
                        TT(hid[:, 0, :], sg[:, 0, :], ps[:, 0, FF:2 * FF], ALU.mult).then_inc(ov[L]["hid"], 1)
                        dve.wait_ge(ov[L]["hT"], n)
                        dve.tensor_copy(hidT[:, 0, :], ps[:, 6, 0:FF]).then_inc(ov[L]["hTe"], 1)
                meet(dve, "dve")
                def final(i):
                    if i == 0:
                        dve.wait_ge(nrm_in, 16 * (2 * DEPTH + 1))
                    dve.wait_ge(fin_rs, i + 1)
                    STT(x7[:, i, :], x7[:, i, :], rsd[:, 24 + i:25 + i], nrm[:, :], ALU.mult,
                        ALU.mult).then_inc(fin_done, 1)

                for kind in (1, 0):
                    for half in range(2):
                        row_from(L, kind, 5, half, rowG2[:, kind, :])
                for lane in (O, M):
                    dve.wait_ge(lane.free, lane.freed[("bc", L, 0, 5, 0 if lane is O else 1)])
                for i in range(TILES):
                    t = ORDER[i]
                    dve.wait_ge(y1_scaled, TILES * L + i + 1)
                    dve.wait_ge(x7_in[i], 16 * (L + 1))
                    go(STT(y2[:, i, :], y2[:, i, :], wts[:, t, 1:2], y1[:, i, :], ALU.mult, ALU.add))
                    TT(y2[:, i, :], y2[:, i, :], rowG2[:, int(t == 4), :], ALU.mult).then_inc(comb, 1)
                    if L == DEPTH - 1 and i:
                        final(i - 1)
                if L == DEPTH - 1:
                    final(TILES - 1)
                elif L < DEPTH - 1:
                    mod_rows(L + 1, 0)
                meet(dve, "dve")


CONSTS = [("ident", P), ("flip", P), ("upper", P), ("m01", 64), ("madd", 64), ("swa", 7 * P),
          ("cos32", 128), ("sin32", 128), ("cos64", 256), ("sin64", 256), ("less", NE * NE), ("w4", 4),
          ("ebase", NE), ("ovshift", NE), ("chunk", NOVF)]


def constants():
    p = np.arange(P)
    col = p % GRID_W
    start = np.clip(col - 8, 0, GRID_W - 16)
    kc = np.arange(GRID_W)
    ok = (kc[None, :] >= start[:, None]) & (kc[None, :] < start[:, None] + 16)
    key, query = p[None, :], p[:, None]
    far, none = np.float32(-1e30), np.zeros((P, P), np.float32)
    before = np.where(key >= query, 0, far)
    after = np.where(key <= query, 0, far)
    c = {
        "ident": np.eye(P), "flip": np.eye(P)[::-1], "upper": query < key,
        "m01": ok, "madd": np.where(ok, 0, far),
        "swa": np.concatenate([before, none, after, none, before, none, none], 1),
        "less": np.broadcast_to((np.arange(NE)[None, :] < np.arange(NE)[:, None]).reshape(1, -1), (P, NE * NE)),
        "w4": np.broadcast_to(np.arange(4, 0, -1), (P, 4)),
        "ebase": np.broadcast_to(np.arange(NE) * P, (P, NE)),
        "ovshift": np.broadcast_to(NE * P - CAP - np.arange(NE) * P, (P, NE)),
        "chunk": np.broadcast_to(np.arange(NOVF), (P, NOVF)),
    }
    pos = np.arange(DEC)
    for dim in (32, 64):
        half = dim // 4
        freq = (10000.0 ** (-np.arange(half, dtype=np.float32) / half)).astype(np.float32)
        cs, sn = [], []
        for x in (pos // GRID_W, pos % GRID_W):
            ang = x.astype(np.float32)[:, None] * freq[None, :]
            cs += [np.cos(ang), np.cos(ang)]
            sn += [-np.sin(ang), np.sin(ang)]
        for n, parts in (("cos", cs), ("sin", sn)):
            full = np.concatenate(parts, 1).reshape(4, P, dim)
            c[n + str(dim)] = full.transpose(1, 0, 2).reshape(P, 4 * dim)
    return np.concatenate([np.asarray(c[n], np.float32).reshape(P, w) for n, w in CONSTS], 1)


def kernel(**inputs):
    import concourse.bacc as bacc
    from concourse.bass_utils import run_bass_kernel_spmd

    x = {k: np.ascontiguousarray(v) for k, v in inputs.items()}
    w = x["w_in"]
    swa_q = w[:, :, 416:672].reshape(DEPTH, D, 4, 64)[:, :, [0, 2, 1, 3]].reshape(DEPTH, D, 256)
    w_in = np.concatenate([w[:, :, 0:416], swa_q, w[:, :, 672:800], w[:, :, 928:1440], w[:, :, 800:928],
                           w[:, :, 1440:1696]], 2)
    w_ukv = x["w_ukv"].reshape(DEPTH, 128, MLA_H, 2, 64).transpose(0, 1, 3, 2, 4).reshape(DEPTH, 128, 1024)
    rpb = np.pad(x["na_rpb"], ((0, 0), (0, 0), (0, 0), (0, RPB_ROW - 31))).reshape(DEPTH * 4, 15 * RPB_ROW)
    flat = {
        "consts": constants(),
        "x0": np.concatenate([x["x_sample"][0], x["x_prompt"][0]], 0),
        "c": x["c"], "c_ctx": x["c_ctx"], "w_mod": x["w_mod"], "b_mod": x["b_mod"],
        "norm1": x["norm1"], "norm2": x["norm2"], "norm_final": x["norm_final"],
        "w_in": w_in, "g_qa": x["g_qa"], "w_uq": x["w_uq"], "g_kva": x["g_kva"], "w_ukv": w_ukv,
        "swa_sink": x["swa_sink"], "rpb": np.pad(rpb, ((0, 0), (P, 64))),
        "w_out": x["w_out"], "w_r": np.concatenate([x["w_router_grp"], x["w_router_exp"]], 2),
        "w_gate": x["w_gate"], "w_up": x["w_up"], "w_down": x["w_down"],
        "cache_mla_ckv": x["cache_mla_ckv"][0], "cache_mla_kpe": x["cache_mla_kpe"][0],
        "cache_swa_k": x["cache_swa_k"].reshape(DEPTH, P, 128), "cache_na_k": x["cache_na_k"].reshape(DEPTH, P, 256),
        "cache_v": np.concatenate([x["cache_swa_v"].reshape(DEPTH, P, 128), x["cache_na_v"].reshape(DEPTH, P, 256)], 2),
    }
    nc = bacc.Bacc("TRN2", target_bir_lowering=False, num_devices=1)
    arrays, t_in, t_out = {}, {}, {}
    for n, a in flat.items():
        arrays["in_" + n] = a = np.ascontiguousarray(a)
        t_in[n] = nc.dram_tensor("in_" + n, a.shape, mybir.dt.from_np(a.dtype), kind="ExternalInput").ap()
    outs = {"y_prompt": (SEQ, D), "y_sample": (DEC, D), "ckv": (DEPTH, SEQ, 128), "kpe": (DEPTH, SEQ, 32),
            "ks": (DEPTH, SEQ, 128), "vs": (DEPTH, SEQ, 128), "kn": (DEPTH, SEQ, 256), "vn": (DEPTH, SEQ, 256)}
    for n, shape in outs.items():
        t_out[n] = nc.dram_tensor("out_" + n, shape, F32, kind="ExternalOutput").ap()
    program(nc, t_in, t_out)
    r = run_bass_kernel_spmd(nc, [arrays], core_ids=[0]).results[0]
    shapes = {"y_prompt": (1, SEQ, D), "y_sample": (1, DEC, D), "ckv": (1, DEPTH, SEQ, 128), "kpe": (1, DEPTH, SEQ, 32),
              "ks": (1, DEPTH, SEQ, 2, 64), "vs": (1, DEPTH, SEQ, 2, 64), "kn": (1, DEPTH, SEQ, 4, 64),
              "vn": (1, DEPTH, SEQ, 4, 64)}
    return tuple(np.asarray(r["out_" + n]).reshape(shape) for n, shape in shapes.items())
```

```python
from contextlib import ExitStack

import numpy as np

import concourse.bass as bass
from concourse import mybir

F32 = mybir.dt.float32
BF16 = mybir.dt.bfloat16
I32 = mybir.dt.int32
ALU = mybir.AluOpType
ACT = mybir.ActivationFunctionType
AX = mybir.AxisListType

P = 128
D = 1024
KD = D // P
DEPTH = 2
SEQ = 128
DEC = 512
TILES = 5
KVT = 6
TOK = TILES * P
KEYS = KVT * P
GRID_W = 64
EPS = 1e-6
NE = 16
FF = 256
MLA_H, NOPE, ROPE, MV = 8, 64, 32, 64
QK = NOPE + ROPE
NOVF = 9
CAP = P
SLOTS = (NE + NOVF) * P
MLA_SCALE = float(QK) ** -0.5
HEAD_SCALE = 0.125
NEG = -3.0e38
NEXT_MOD = 12
ORDER = [4, 0, 1, 2, 3]
CHUNKS = [(0, 416), (416, 384), (800, 512), (1312, 384)]
C_CQ, C_CKV, C_KPE, C_QS, C_KS, C_QN, C_KN = 0, 256, 384, 416, 672, 800, 1056
PW = 1312
RPB_ROW, RPB_LEN = 64, 128 + 15 * 64 + 64


def norm_no(L, phase, i):
    return TILES * (2 * L + (phase == 5)) + i + 1


def x_no(L, i):
    return 16 * ((3 - i % 2) * L + i // 2 + 1)


def ring_loads():
    out = [("mod", 0, 0)]
    for L in range(DEPTH):
        out += [("in", L), ("mod", L, 1), ("mod", L, 2)]
        out += [("mod", L + 1, 0)] if L < DEPTH - 1 else []
        out += [("out", L)]
    return out


def slot_no(i, key):
    loads = [k for k in ring_loads() if i >= 2 or k[0] != "out"]
    return 16 * (loads.index(key) + 1)


class Lane:

    def __init__(self, full, free):
        self.full, self.free = full, free
        self.number, self.freed, self.jobs, self.frees = {}, {}, 0, 0

    def take(self, pe, key, frees=1):
        if self.frees:
            pe.wait_ge(self.free, self.frees)
        self.jobs += 1
        self.frees += frees
        self.number[key] = self.jobs
        self.freed[key] = self.frees

    def __getitem__(self, key):
        return self.number[key]


def program(nc, t_in, t_out):
    with ExitStack() as ctx:
        def sb(name, shape, dt=F32):
            return ctx.enter_context(nc.sbuf_tensor(name, shape, dt))

        def sem(name):
            return ctx.enter_context(nc.semaphore(name))

        xbuf = nc.dram_tensor("x_rows", (TOK, D), F32).ap()
        slots_x = nc.dram_tensor("slots_x", (SLOTS, D), F32).ap()
        slots_y = nc.dram_tensor("slots_y", (SLOTS, D), F32).ap()

        ring = sb("ring", [P, 4 * 8 * 512])
        slot = [ring[:, i * 4096:(i + 1) * 4096].rearrange("p (k n) -> p k n", k=8) for i in range(4)]
        big = sb("big", [P, 5120])
        hT = big[:, :].rearrange("p (k n) -> p k n", k=KD)
        heads = big[:, :].rearrange("p (t n) -> p t n", t=TILES)
        mrow = sb("mrow", [P, 3, 512])
        brow = sb("brow", [P, 3, 512])
        wuq = sb("wuq", [P, 2, 768])
        wukv = sb("wukv", [P, 1024])
        wr = sb("wr", [P, KD, 20])
        gqa = sb("gqa", [P, 256])
        gkva = sb("gkva", [P, 128])
        nrm = sb("nrm", [P, D])
        sink = sb("sink", [P, 4])
        sc = sb("sc", [P, KD, 32])
        cc = sb("cc", [P, 2, KD])
        consts = sb("consts", [P, sum(w for _, w in CONSTS)])
        cst, at = {}, 0
        for name, w in CONSTS:
            cst[name] = consts[:, at:at + w]
            at += w
        ident, flip, upper = (cst[n] for n in ("ident", "flip", "upper"))
        ones = cst["w4"][:, 3:4].broadcast_to([P, P])
        mhalf = sb("mhalf", [P, 8])
        zeros = sb("zeros", [P, 256])
        ssq = sb("ssq", [P, 32])
        rsd = sb("rsd", [P, 32])
        wts = sb("wts", [P, TILES, 2])
        sidx = sb("sidx", [P, 2 * TILES], I32)
        ctl = sb("ctl", [P, 16], I32)

        ARENA = 21184
        arena = sb("arena", [P, ARENA])

        def place(at, *dims):
            n = int(np.prod(dims))
            assert at + n <= ARENA, (at, dims)
            a = arena[:, at:at + n]
            if len(dims) == 2:
                a = a.rearrange("p (a b) -> p a b", a=dims[0])
            return a, at + n

        cqT, o = place(0, 2, TOK)
        ckvT, o = place(o, KEYS)
        kpeT, A0 = place(o, KEYS)
        v_loc, o = place(A0, KVT, 384)
        qsP, o = place(o, 4, TOK)
        qnP, o = place(o, 4, TOK)
        ksT, o = place(o, KEYS)
        knT, A1 = place(o, 2, KEYS)
        proj, o = place(A1, 2, PW)
        rt, o = place(o, 2, 384)
        ck, o = place(o, 544)
        junk1, o = place(o, 192)
        BRAW = ARENA - 4 * 960
        assert o <= BRAW
        braw, o = place(BRAW, 4, 960)
        bias, o = place(A1, 4, 960)
        sB, o = place(BRAW, 2, 640)
        pB2, o = place(o, 2, 640)
        pT2, o = place(o, 2, 640)
        qT, o = place(A0, 8, TOK)
        kT, o = place(o, 8, KEYS)
        v_mla, A3 = place(o, KVT, 512)
        qt, o = place(A3, 2, 768)
        rq, o = place(o, 2, 256)
        pB4, o = place(A3, 2, 640)
        pT4, o = place(o, 2, 640)
        rowG1, o = place(0, 2, D)
        rowA2, o = place(o, 2, D)
        rowB2, o = place(o, 2, D)
        hoT, o = place(o, 2, D)
        xt5, o = place(o, 2, D)
        tmp5, o = place(o, D)
        h2, o = place(o, 5, D)
        h2T, o = place(o, 2, D)
        R0 = o
        xg, o = place(0, 2, D)
        xgT, o = place(o, 2, D)
        sg, o = place(o, 2, FF)
        hid, o = place(o, 2, FF)
        hidT, o = place(o, 2, FF)
        yb, o = place(o, 2, D)
        dn2, o = place(o, 2048)
        exp3, o = place(o, 6144)
        gu_at = [ring[:, 0:4096], ring[:, 6144:10240], ring[:, 12288:16384], exp3[:, 0:4096]]
        dn_at = [ring[:, 4096:6144], ring[:, 10240:12288], dn2, exp3[:, 4096:6144]]
        w_gu = [a.rearrange("p (g k n) -> p g k n", g=2, k=KD) for a in gu_at]
        w_dn = [a.rearrange("p (k n) -> p k n", k=2) for a in dn_at]
        rowG2, o = place(0, 2, D)
        x7, o = place(o, TILES, D)
        y1, o = place(o, TILES, D)
        y2, o = place(o, 4, D)
        rowA, o = place(o, 2, D)
        rowB, o = place(o, 2, D)
        junk7, o = place(o, 512)
        rt_at = [R0]

        def rtile(*dims):
            n = int(np.prod(dims))
            a = arena[:, rt_at[0]:rt_at[0] + n]
            rt_at[0] += n
            assert rt_at[0] <= ARENA
            if len(dims) == 2:
                a = a.rearrange("p (a b) -> p a b", a=dims[0])
            if len(dims) == 3:
                a = a.rearrange("p (a b c) -> p a b c", a=dims[0], b=dims[1])
            return a

        r_lg = rtile(TILES, 20)
        r_g, r_d2, r_e2, r_m = (rtile(TILES) for _ in range(4))
        r_gd, r_ge, r_eq, r_oh, r_sel, r_oh1, r_oh2 = (rtile(TILES, 4) for _ in range(7))
        r_prod = rtile(TILES, 4, 4)
        r_c1, r_c2, r_T, r_pos, r_ge5, r_tmp = (rtile(TILES, NE) for _ in range(6))
        r_n, r_nov, r_ovb, r_dl = (rtile(NE) for _ in range(4))
        r_pr = rtile(NE, NE)
        r_ind = rtile(NOVF, NE)
        r_s = rtile(2, TILES)
        r_ctl = rtile(16)
        junk5 = arena[:, rt_at[0]:rt_at[0] + 512].bitcast(BF16)
        assert rt_at[0] + 512 <= ARENA

        stat = {n: sb("st_" + n, [P, 8]) for n in ("mx", "m2", "nm", "sm", "es", "ri")}

        ps = ctx.enter_context(nc.psum_tensor("ps", [P, 8, 512], F32))

        def two(b, n=1024):
            return ps[:, b:b + 2, :].rearrange("p a b -> p (a b)")[:, 0:n]

        S = [Lane(sem(f"s{i}_full"), sem(f"s{i}_free")) for i in range(2)]
        T = Lane(sem("t_full"), sem("t_free"))
        O = Lane(sem("o_full"), sem("o_free"))
        M = Lane(sem("m_full"), sem("m_free"))
        met = sem("met")
        const_in, c_in, bmod_in, small_in, vec_in, nrm_in = (sem(n) for n in
                                                    ("const_in", "c_in", "bmod_in", "small_in", "vec_in", "nrm_in"))
        slot_in = [sem(f"slot{i}_in") for i in range(4)]
        mods_done = sem("mods_done")
        xt_in = [sem(f"xt{i}_in") for i in range(2)]
        cache_in, ctx_out, zero_out, zero_set = (sem(n) for n in ("cache_in", "ctx_out", "zero_out", "zero_set"))
        silu_done, sc_set, half_set = (sem(n) for n in ("silu_done", "sc_set", "half_set"))
        sq_done, rs_done = sem("sq_done"), sem("rs_done")
        sq2_done, rs2_done = sem("sq2_done"), sem("rs2_done")
        hA_done, h_done = sem("hA_done"), sem("h_done")
        rows_done = sem("rows_done")
        post_done, pad_set = sem("post_done"), sem("pad_set")
        braw_in, bias_mul, bias_done = sem("braw_in"), sem("bias_mul"), sem("bias_done")
        nmax_done, q_done, routed = sem("nmax_done"), sem("q_done"), sem("routed")
        res_mul, res_done, xs_out = (sem(n) for n in ("res_mul", "res_done", "xs_out"))
        rx1, rx1_done, rx2, rx2_done = (sem(n) for n in ("rx1", "rx1_done", "rx2", "rx2_done"))
        pick_done, idx_done, scat_out = (sem(n) for n in ("pick_done", "idx_done", "scat_out"))
        ew_in = [sem(f"ew{i}_in") for i in range(4)]
        xg_in = [sem(f"xg{i}_in") for i in range(2)]
        e_xT, e_xTa, e_xTd, e_h, e_sg, e_hid, e_hT, e_hTe, e_d, e_ya, e_yd = (sem("e_" + n) for n in (
            "xT", "xTa", "xTd", "h", "sg", "hid", "hT", "hTe", "d", "ya", "yd"))
        ys_out = [sem(f"ys{i}_out") for i in range(2)]
        ov = [{n: sem(f"ov{L}_{n}") for n in ("x", "w", "xT", "xTe", "h", "sg", "hid", "hT", "hTe", "d", "y", "out")}
              for L in range(DEPTH)]
        x7_in = [sem(f"x7{i}_in") for i in range(TILES)]
        y_in = [sem(f"y{i}_in") for i in range(TILES)]
        y1_scaled, comb_done, x7_out, fin_sq, fin_rs, fin_done = (sem(n) for n in (
            "y1_scaled", "comb_done", "x7_out", "fin_sq", "fin_rs", "fin_done"))
        step = {n: sem("step_" + n) for n in ("dve", "act", "pool")}
        steps = {n: 0 for n in step}

        def then(eng, who, ins):
            steps[who] += 1
            ins.then_inc(step[who], 1)
            eng.wait_ge(step[who], steps[who])

        meets = {}

        def meet(eng, who):
            meets[who] = meets.get(who, 0) + 1
            eng.drain().then_inc(met, 1)
            eng.wait_ge(met, 5 * meets[who])

        def unit_list(phase):
            out = []
            if phase == 2:
                for h in range(4):
                    for t in range(4):
                        lo, hi = max(t - 1, 0), min(t + 1, 3)
                        m0 = {0: 1, 1: 0, 2: 0, 3: 4}[t] * P
                        n = hi - lo + 2
                        out.append(dict(kind="swa", h=h, t=t, q=qsP[:, h, t * P:(t + 1) * P],
                                        k=[(0, ksT[:, lo * P:(hi + 1) * P]), ((n - 1) * P, ksT[:, 4 * P:5 * P])],
                                        n=n, mask=cst["swa"][:, m0:m0 + n * P],
                                        v=[v_loc[:, j, (h // 2) * 64:(h // 2) * 64 + 64] for j in [*range(lo, hi + 1), 4]],
                                        col=512 + h * 64))
                for h in range(4):
                    for t in range(4):
                        j0 = (7 - 2 * t) * 64
                        out.append(dict(kind="na", h=h, t=t, q=qnP[:, h, t * P:(t + 1) * P],
                                        k=[(0, knT[:, h // 2, 0:512]), (512, knT[:, h // 2, 512:640])],
                                        n=5, mask=bias[:, h, j0:j0 + 512],
                                        v=[v_loc[:, j, 128 + h * 64:192 + h * 64] for j in range(5)],
                                        col=768 + h * 64))
                for h in range(4):
                    out.append(dict(kind="swa_ctx", h=h, t=4, q=qsP[:, h, 512:640], k=[(0, ksT[:, 640:768])], n=1,
                                    v=[v_loc[:, 5, (h // 2) * 64:(h // 2) * 64 + 64]], col=512 + h * 64))
                for h in range(4):
                    out.append(dict(kind="ctx", h=h, t=4, q=qnP[:, h, 512:640], k=[(0, knT[:, h // 2, 640:768])],
                                    n=1, v=[v_loc[:, 5, 128 + h * 64:192 + h * 64]], col=768 + h * 64))
            else:
                for h in range(MLA_H):
                    for t in range(4):
                        out.append(dict(kind="mla", h=h, t=t, q=qT[0:QK, h, t * P:(t + 1) * P],
                                        k=[(0, kT[0:QK, h, 0:512]), (512, kT[0:QK, h, 512:640])], n=5,
                                        v=[v_mla[:, j, h * 64:h * 64 + 64] for j in range(5)], col=h * 64))
                    out.append(dict(kind="ctx", h=h, t=4, q=qT[0:QK, h, 512:640], k=[(0, kT[0:QK, h, 640:768])],
                                    n=1, v=[v_mla[:, 5, h * 64:h * 64 + 64]], col=h * 64))
            return out

        UNITS = {2: unit_list(2), 4: unit_list(4)}
        UBASE = {2: 0, 4: len(UNITS[2])}
        UPL = len(UNITS[2]) + len(UNITS[4])
        pB = {2: pB2, 4: pB4}
        pT = {2: pT2, 4: pT4}
        SINKS = sum(u["kind"].startswith("swa") for u in UNITS[2])

        def split(n):
            return (1, 0) if n == 1 else ((n + 1) // 2, n // 2)

        block = ctx.enter_context(nc.Block())

        @block.tensor
        def _(pe):
            def transpose(out, in_):
                return pe.transpose(out, in_, ident)

            def mod_group(L, g):
                for i in range(4):
                    pe.wait_ge(slot_in[i], slot_no(i, ("mod", L, g)))
                M.take(pe, ("mod", L, g))
                for k in range(KD):
                    for i in range(4):
                        mm = pe.matmul(ps[32 * i:32 * i + 32, 7, :], sc[:, k, :], slot[i][:, k, :],
                                       start=(k == 0), stop=(k == KD - 1), tile_position=(0, 32 * i))
                mm.then_inc(M.full, 1)

            bcn = [0]

            def broadcast(L, kind, vec, half):
                n = 2 * vec + half
                lane, b = ((O, 6), (M, 7))[bcn[0] % 2]
                bcn[0] += 1
                pe.wait_ge(mods_done, 3 * L + n // 4 + 1)
                lane.take(pe, ("bc", L, kind, vec, half))
                row = 32 * (n % 4) + kind
                pe.matmul(ps[:, b, :], ident[:, row:row + 1].broadcast_to([P, P]), mrow[:, n // 4, :],
                          start=True, stop=True).then_inc(lane.full, 1)

            def attention(L, phase):
                units = UNITS[phase]
                base = UPL * L + UBASE[phase]

                def scores(u):
                    un = units[u]
                    S[u % 2].take(pe, ("s", L, phase, u))
                    if phase == 2 and un["kind"] == "na" and un["t"] == 0:
                        pe.wait_ge(bias_done, 4 * L + un["h"] + 1)
                    b = 2 * (u % 2)
                    for at, k in un["k"]:
                        w = k.shape[-1]
                        mm = pe.matmul(two(b)[:, at:at + w], un["q"], k, start=(at % 512 == 0), stop=True,
                                       skip_group_check=True)
                    mm.then_inc(S[u % 2].full, 1)

                def turn(u):
                    n = units[u]["n"]
                    a, d = split(n)
                    T.take(pe, ("p", L, phase, u), frees=2 if d else 1)
                    pe.wait_ge(S[u % 2].free, S[u % 2].freed[("s", L, phase, u)])
                    for j in range(n):
                        o = ps[:, 4, j * P:(j + 1) * P] if j < a else ps[:, 5, (j - a) * P:(j - a + 1) * P]
                        mm = transpose(o, pB[phase][:, u % 2, j * P:(j + 1) * P])
                    mm.then_inc(T.full, 1)

                def values(u):
                    un = units[u]
                    O.take(pe, ("o", L, phase, u))
                    pe.wait_ge(T.free, T.freed[("p", L, phase, u)])
                    for j in range(un["n"]):
                        mm = pe.matmul(ps[:, 6, 0:64], pT[phase][:, u % 2, j * P:(j + 1) * P], un["v"][j],
                                       start=(j == 0), stop=(j == un["n"] - 1))
                    mm.then_inc(O.full, 1)

                for s in range(len(units) + 2):
                    if s < len(units):
                        scores(s)
                    if s >= 2:
                        values(s - 2)
                    if 1 <= s <= len(units):
                        turn(s - 1)
                    if phase == 2 and s in (16, 30):
                        mod_group(L, 1 if s == 16 else 2)
                    if phase == 4 and s == NEXT_MOD and L < DEPTH - 1:
                        mod_group(L + 1, 0)

            def entry(L):
                for kind in (1, 0):
                    for v in range(2):
                        for half in range(2):
                            broadcast(L, kind, v, half)
                for i in range(TILES):
                    T.take(pe, ("h", L, i))
                    pe.wait_ge(h_done, norm_no(L, 1, i))
                    for k in range(KD):
                        mm = transpose(ps[:, 4 + k // 4, (k % 4) * P:(k % 4 + 1) * P], y1[:, i, k * P:(k + 1) * P])
                    mm.then_inc(T.full, 1)

            pe.wait_ge(const_in, 16)
            pe.wait_ge(sc_set, 3)
            mod_group(0, 0)
            entry(0)
            meet(pe, "pe")
            for L in range(DEPTH):
                def turn_context():
                    T.take(pe, ("xp", L, 5), frees=2)
                    pe.wait_ge(cache_in, 80 * (L + 1))
                    transpose(ps[:, 4, 0:P], ck[:, 0:128])
                    transpose(ps[0:ROPE, 4, 384:512], ck[:, 128:160])
                    transpose(ps[:, 5, 0:P], ck[:, 160:288]).then_inc(T.full, 1)
                    O.take(pe, ("xn", L, 5))
                    transpose(ps[:, 6, 0:P], ck[:, 288:416])
                    transpose(ps[:, 6, P:2 * P], ck[:, 416:544]).then_inc(O.full, 1)

                def turn_proj(i):
                    q = proj[:, i % 2, :]
                    T.take(pe, ("xp", L, i), frees=2)
                    pe.wait_ge(post_done, TILES * L + i + 1)
                    for n, at in enumerate((C_CQ, C_CQ + P, C_CKV)):
                        transpose(ps[:, 4, n * P:(n + 1) * P], q[:, at:at + P])
                    transpose(ps[0:ROPE, 4, 384:512], q[:, C_KPE:C_KPE + ROPE])
                    for n, at in enumerate((C_QS, C_QS + P, C_KS)):
                        mm = transpose(ps[:, 5, n * P:(n + 1) * P], q[:, at:at + P])
                    mm.then_inc(T.full, 1)
                    O.take(pe, ("xn", L, i))
                    pe.wait_ge(S[1].free, S[1].freed[("in", L, i)])
                    for n, at in enumerate((C_QN, C_QN + P, C_KN, C_KN + P)):
                        mm = transpose(ps[:, 6, n * P:(n + 1) * P], q[:, at:at + P])
                    mm.then_inc(O.full, 1)

                for s in range(TILES + 1):
                    if s < TILES:
                        t = ORDER[s]
                        for half in range(2):
                            S[half].take(pe, ("in", L, s))
                            for c in (2 * half, 2 * half + 1):
                                if s == 0:
                                    pe.wait_ge(slot_in[c], slot_no(c, ("in", L)))
                                for k in range(KD):
                                    mm = pe.matmul(ps[:, c, 0:CHUNKS[c][1]], hT[:, k, t * P:(t + 1) * P],
                                                   slot[c][:, k, 0:CHUNKS[c][1]], start=(k == 0), stop=(k == KD - 1))
                            mm.then_inc(S[half].full, 1)
                    if s == 1:
                        turn_context()
                    if s >= 1:
                        turn_proj(s - 1)
                meet(pe, "pe")

                for h in range(4):
                    S[h % 2].take(pe, ("bias", L, h))
                    pe.wait_ge(braw_in, 16 * (L + 1))
                    for n in range(2):
                        mm = pe.matmul(ps[:, 2 * (h % 2) + n, 0:480], flip, braw[:, h, n * 480:(n + 1) * 480],
                                       start=True, stop=True)
                    mm.then_inc(S[h % 2].full, 1)
                attention(L, 2)
                meet(pe, "pe")

                def uq(i):
                    t = ORDER[i]
                    T.take(pe, ("uq", L, i))
                    for n, w in ((0, 512), (512, 256)):
                        for k in range(2):
                            mm = pe.matmul(ps[:, 4 + n // 512, 0:w], cqT[:, k, t * P:(t + 1) * P], wuq[:, k, n:n + w],
                                           start=(k == 0), stop=(k == 1))
                    mm.then_inc(T.full, 1)

                def qturn(i):
                    S[i % 2].take(pe, ("qt", L, i))
                    pe.wait_ge(q_done, TILES * L + i + 1)
                    for h in range(MLA_H):
                        b = 2 * (i % 2) + h // 4
                        mm = transpose(ps[0:QK, b, (h % 4) * P:(h % 4 + 1) * P], qt[:, i % 2, h * QK:(h + 1) * QK])
                    mm.then_inc(S[i % 2].full, 1)

                for i in range(TILES + 1):
                    if i < TILES:
                        uq(i)
                    if i < 4:
                        S[i % 2].take(pe, ("uk", L, i))
                        for n, w in ((0, 512), (512, 256)):
                            mm = pe.matmul(ps[:, 2 * (i % 2) + n // 512, 0:w], wukv[:, i * P:(i + 1) * P],
                                           ckvT[:, n:n + w], start=True, stop=True)
                        mm.then_inc(S[i % 2].full, 1)
                    lane, b = ((O, 6), (M, 7))[i % 2]
                    lane.take(pe, ("uv", L, i))
                    pe.matmul(ps[:, b, :], ckvT[:, i * P:(i + 1) * P], wukv[:, 512:1024],
                              start=True, stop=True).then_inc(lane.full, 1)
                    if i >= 1:
                        qturn(i - 1)
                meet(pe, "pe")

                attention(L, 4)
                meet(pe, "pe")

                for vec in (2, 4, 3):
                    for kind in (1, 0):
                        for half in range(2):
                            broadcast(L, kind, vec, half)

                def ho_turn(i):
                    t = ORDER[i]
                    T.take(pe, ("ho", L, i), frees=2)
                    for k in range(KD):
                        mm = transpose(ps[:, 4 + k // 4, (k % 4) * P:(k % 4 + 1) * P], heads[:, t, k * P:(k + 1) * P])
                    mm.then_inc(T.full, 1)

                def h2_turn(i):
                    T.take(pe, ("h2", L, i), frees=2)
                    pe.wait_ge(h_done, norm_no(L, 5, i))
                    for k in range(KD):
                        mm = transpose(ps[:, 4 + k // 4, (k % 4) * P:(k % 4 + 1) * P], h2[:, ORDER[i], k * P:(k + 1) * P])
                    mm.then_inc(T.full, 1)

                def out_proj(i):
                    S[i % 2].take(pe, ("out", L, i))
                    pe.wait_ge(T.free, T.freed[("ho", L, i)])
                    for n in range(2):
                        if i == 0:
                            pe.wait_ge(slot_in[2 + n], slot_no(2 + n, ("out", L)))
                        for k in range(KD):
                            mm = pe.matmul(ps[:, 2 * (i % 2) + n, :], hoT[:, i % 2, k * P:(k + 1) * P], slot[2 + n][:, k, :],
                                           start=(k == 0), stop=(k == KD - 1))
                    mm.then_inc(S[i % 2].full, 1)

                def route(i):
                    t = ORDER[i]
                    if i == 0:
                        O.take(pe, ("rt", L))
                    pe.wait_ge(T.free, T.freed[("h2", L, i)])
                    for k in range(KD):
                        mm = pe.matmul(ps[:, 6, t * 20:(t + 1) * 20], h2T[:, i % 2, k * P:(k + 1) * P], wr[:, k, :],
                                       start=(k == 0), stop=(k == KD - 1))
                    mm.then_inc(O.full if i == TILES - 1 else routed, 1)

                for s in range(TILES + 4):
                    if s < TILES:
                        ho_turn(s)
                    if 1 <= s <= TILES:
                        out_proj(s - 1)
                    if 3 <= s < TILES + 3:
                        h2_turn(s - 3)
                    if s >= 4:
                        route(s - 4)
                O.take(pe, ("pos", L))
                M.take(pe, ("cnt", L))
                pe.wait_ge(pick_done, L + 1)
                pe.matmul(ps[:, 6, 0:80], upper, r_T[:, :, :].rearrange("p a b -> p (a b)"), start=True,
                          stop=True).then_inc(O.full, 1)
                pe.matmul(ps[:, 7, 0:80], ones, r_T[:, :, :].rearrange("p a b -> p (a b)"), start=True,
                          stop=True).then_inc(M.full, 1)
                meet(pe, "pe")

                n_ov = pe.value_load(ctl[0:1, 0:1], min_val=0, max_val=NOVF)
                E0 = NE * L

                def x_turn(e, b, first):
                    if not first:
                        pe.wait_ge(e_xTa, E0 + e)
                        pe.wait_ge(e_xTd, E0 + e)
                    pe.wait_ge(xg_in[b], 16 * (E0 // 2) + (e - b) * 8 + 16)
                    for k in range(KD):
                        mm = transpose(ps[:, 4 + k // 4, (k % 4) * P:(k % 4 + 1) * P], xg[:, b, k:D:KD])
                    mm.then_inc(e_xT, 1)

                def up(e, q, early):
                    b = q % 2
                    pe.wait_ge(ew_in[q], 12 * E0 + (e - q) * 12 + 48)
                    pe.wait_ge(e_xTa, E0 + e + 1)
                    pe.wait_ge(e_xTd, E0 + e + 1)
                    if not early:
                        pe.wait_ge(e_hid, E0 + e - 1)
                    for k in range(KD):
                        mm = pe.matmul(ps[:, b, :], xgT[:, b, k * P:(k + 1) * P], w_gu[q][:, :, k, :],
                                       start=(k == 0), stop=(k == KD - 1))
                    mm.then_inc(e_h, 1)

                def h_turn(e, b, first):
                    if not first:
                        pe.wait_ge(e_hTe, E0 + e)
                    pe.wait_ge(e_hid, E0 + e + 1)
                    for k in range(2):
                        mm = transpose(ps[:, 6, k * P:(k + 1) * P], hid[:, b, k:FF:2])
                    mm.then_inc(e_hT, 1)

                def down(e, q, first):
                    b = q % 2
                    pe.wait_ge(e_hTe, E0 + e + 1)
                    if not first:
                        pe.wait_ge(e_ya, E0 + e)
                        pe.wait_ge(e_yd, E0 + e)
                    for n in range(2):
                        for k in range(2):
                            mm = pe.matmul(ps[:, 2 + n, :], hidT[:, b, k * P:(k + 1) * P],
                                           w_dn[q][:, k, n * 512:(n + 1) * 512], start=(k == 0), stop=(k == 1))
                    mm.then_inc(e_d, 1)

                x_turn(0, 0, True)
                up(0, 0, True)
                x_turn(1, 1, False)
                h_turn(0, 0, True)
                up(1, 1, True)
                x_turn(2, 0, False)
                down(0, 0, True)
                h_turn(1, 1, False)
                with pe.Fori(2, NE - 2, 4) as e0:
                    for j in range(4):
                        e, q = e0 + j, (2 + j) % 4
                        up(e, q, False)
                        x_turn(e + 1, 1 - j % 2, False)
                        down(e - 1, (q - 1) % 4, False)
                        h_turn(e, j % 2, False)
                up(14, 2, False)
                x_turn(15, 1, False)
                down(13, 1, False)
                h_turn(14, 0, False)
                up(15, 3, False)
                down(14, 2, False)
                h_turn(15, 1, False)
                down(15, 3, False)
                pe.wait_ge(e_ya, E0 + NE)
                pe.wait_ge(e_yd, E0 + NE)
                with pe.If(n_ov > 0):
                    with pe.Fori(0, NOVF) as c:
                        n = c + 1
                        pe.wait_ge(ov[L]["x"], n * 16)
                        for k in range(KD):
                            mm = transpose(ps[:, 4 + k // 4, (k % 4) * P:(k % 4 + 1) * P], xg[:, 0, k:D:KD])
                        mm.then_inc(ov[L]["xT"], 1)
                        pe.wait_ge(ov[L]["w"], n * 48)
                        pe.wait_ge(ov[L]["xTe"], n)
                        for k in range(KD):
                            mm = pe.matmul(ps[:, 0, :], xgT[:, 0, k * P:(k + 1) * P], w_gu[3][:, :, k, :],
                                           start=(k == 0), stop=(k == KD - 1))
                        mm.then_inc(ov[L]["h"], 1)
                        pe.wait_ge(ov[L]["hid"], n)
                        for k in range(2):
                            mm = transpose(ps[:, 6, k * P:(k + 1) * P], hid[:, 0, k:FF:2])
                        mm.then_inc(ov[L]["hT"], 1)
                        pe.wait_ge(ov[L]["hTe"], n)
                        for h in range(2):
                            for k in range(2):
                                mm = pe.matmul(ps[:, 2 + h, :], hidT[:, 0, k * P:(k + 1) * P],
                                               w_dn[3][:, k, h * 512:(h + 1) * 512], start=(k == 0), stop=(k == 1))
                        mm.then_inc(ov[L]["d"], 1)
                meet(pe, "pe")

                for kind in (1, 0):
                    for half in range(2):
                        broadcast(L, kind, 5, half)
                if L < DEPTH - 1:
                    entry(L + 1)
                meet(pe, "pe")

        @block.sync
        def _(sp):
            sp.dma_start(consts[:, :], t_in["consts"]).then_inc(const_in, 16)
            sp.dma_start(cc[:, 0, :], t_in["c"].rearrange("a (p k) -> (a p) k", k=KD)).then_inc(c_in, 16)
            sp.dma_start(cc[:, 1, :], t_in["c_ctx"].rearrange("(p k) -> p k", k=KD)).then_inc(c_in, 16)

            def mod_load(L, g):
                w_mod = t_in["w_mod"][L].rearrange("(p k) n -> p k n", k=KD)
                for i in range(4):
                    n = 4 * g + i
                    sp.dma_start(slot[i], w_mod[:, :, n * 512:(n + 1) * 512]).then_inc(slot_in[i], 16)

            def small_loads(L):
                sp.dma_start(wuq[:, :, :], t_in["w_uq"][L].rearrange("(k p) n -> p k n", p=P)).then_inc(small_in, 16)
                sp.dma_start(wukv[:, :], t_in["w_ukv"][L]).then_inc(small_in, 16)
                sp.dma_start(wr[:, :, :], t_in["w_r"][L].rearrange("(k p) n -> p k n", p=P)).then_inc(small_in, 16)

            def in_load(L, c):
                at, w = CHUNKS[c]
                w_in = t_in["w_in"][L].rearrange("(k p) n -> p k n", p=P)
                sp.dma_start(slot[c][:, :, 0:w], w_in[:, :, at:at + w]).then_inc(slot_in[c], 16)

            def x_loads(src):
                for i in range(TILES):
                    t = ORDER[i]
                    sp.dma_start(x7[:, i, :], src[t * P:(t + 1) * P, :]).then_inc(x7_in[i], 16)

            mod_load(0, 0)
            x_loads(t_in["x0"])
            small_loads(0)
            sp.wait_ge(M.full, M[("mod", 0, 0)])
            for c in range(4):
                in_load(0, c)
            meet(sp, "sp")
            for L in range(DEPTH):
                w_out = t_in["w_out"][L].rearrange("(k p) n -> p k n", p=P)
                src = bass.AP(tensor=t_in["rpb"].tensor, offset=L * 4 * RPB_LEN + 16, ap=[[1, P], [RPB_LEN, 4], [1, 960]])
                sp.dma_start(braw, src).then_inc(braw_in, 16)
                sp.wait_ge(post_done, TILES * L + 1)
                sp.wait_ge(S[1].free, S[1].freed[("in", L, 0)])
                for name, src_ap in (("ckv", proj[:, 0, C_CKV:C_CKV + 128]), ("kpe", proj[:, 0, C_KPE:C_KPE + 32]),
                                     ("ks", proj[:, 0, C_KS:C_KS + 128]), ("kn", proj[:, 0, C_KN:C_KN + 256]),
                                     ("vs", v_loc[:, 5, 0:128]), ("vn", v_loc[:, 5, 128:384])):
                    sp.dma_start(t_out[name][L], src_ap).then_inc(ctx_out, 16)
                for half in range(2):
                    sp.wait_ge(S[half].full, S[half][("in", L, TILES - 1)])
                mod_load(L, 1)
                sp.wait_ge(ctx_out, 96 * (L + 1))
                meet(sp, "sp")
                sp.wait_ge(M.full, M[("mod", L, 1)])
                mod_load(L, 2)
                sp.wait_ge(M.full, M[("mod", L, 2)])
                if L < DEPTH - 1:
                    mod_load(L + 1, 0)

                def up_load(e, q):
                    for n, w in enumerate(("w_gate", "w_up")):
                        sp.dma_start(w_gu[q][:, n], t_in[w][L][e].rearrange("(p k) n -> p k n", k=KD)).then_inc(ew_in[q], 16)

                def down_load(e, q):
                    sp.dma_start(w_dn[q], t_in["w_down"][L][e].rearrange("(p k) n -> p k n", k=2)).then_inc(ew_in[q], 16)

                def out_load():
                    for n in range(2):
                        sp.dma_start(slot[2 + n], w_out[:, :, n * 512:(n + 1) * 512]).then_inc(slot_in[2 + n], 16)
                    up_load(0, 0)
                    down_load(0, 0)

                if L == DEPTH - 1:
                    out_load()
                meet(sp, "sp")
                meet(sp, "sp")
                if L < DEPTH - 1:
                    sp.wait_ge(M.full, M[("mod", L + 1, 0)])
                    out_load()
                meet(sp, "sp")
                for i in range(2):
                    sp.wait_ge(S[i].full, S[i][("out", L, TILES - 1 - i)])
                up_load(1, 1)
                down_load(1, 1)
                up_load(2, 2)
                meet(sp, "sp")
                n_ov = sp.value_load(ctl[0:1, 0:1], min_val=0, max_val=NOVF)
                E0 = NE * L
                for e in range(2):
                    sp.dma_start(xg[:, e, :], slots_x[e * P:(e + 1) * P, :]).then_inc(xg_in[e], 16)
                down_load(2, 2)
                up_load(3, 3)
                down_load(3, 3)
                for e in range(2, 4):
                    sp.wait_ge(e_xT, E0 + e - 1)
                    sp.dma_start(xg[:, e % 2, :], slots_x[e * P:(e + 1) * P, :]).then_inc(xg_in[e % 2], 16)
                with sp.Fori(1, NE // 4) as quad:
                    for q in range(4):
                        j = q % 2
                        e = sp.snap(quad * 4 + q)
                        row = sp.snap(quad * (4 * P) + q * P)
                        sp.wait_ge(e_xT, E0 + e - 1)
                        sp.dma_start(xg[:, j, :], slots_x[bass.ds(row, P), :]).then_inc(xg_in[j], 16)
                        sp.wait_ge(e_d, E0 + e - 3)
                        for n, w in enumerate(("w_gate", "w_up")):
                            sp.dma_start(w_gu[q][:, n], t_in[w][L][bass.ds(e, 1)].rearrange(
                                "o (p k) n -> (o p) k n", k=KD)).then_inc(ew_in[q], 16)
                        sp.dma_start(w_dn[q], t_in["w_down"][L][bass.ds(e, 1)].rearrange(
                            "o (p k) n -> (o p) k n", k=2)).then_inc(ew_in[q], 16)
                if L < DEPTH - 1:
                    small_loads(L + 1)
                    for c, last_expert in enumerate((12, 13, 13, 14)):
                        sp.wait_ge(e_d, E0 + last_expert + 1)
                        in_load(L + 1, c)
                with sp.If(n_ov > 0):
                    sp.wait_ge(e_d, E0 + NE)
                    for c in range(NOVF):
                        e = sp.value_load(ctl[0:1, 1 + c:2 + c], min_val=0, max_val=NE - 1)
                        if c:
                            sp.wait_ge(ov[L]["out"], 16 * c)
                        row = (NE + c) * P
                        sp.dma_start(xg[:, 0, :], slots_x[row:row + P, :]).then_inc(ov[L]["x"], 16)
                        for n, w in enumerate(("w_gate", "w_up")):
                            sp.dma_start(w_gu[3][:, n], t_in[w][L][bass.ds(e, 1)].rearrange(
                                "o (p k) n -> (o p) k n", k=KD)).then_inc(ov[L]["w"], 16)
                        sp.dma_start(w_dn[3], t_in["w_down"][L][bass.ds(e, 1)].rearrange(
                            "o (p k) n -> (o p) k n", k=2)).then_inc(ov[L]["w"], 16)
                meet(sp, "sp")
                x_loads(xbuf)
                meet(sp, "sp")

        @block.scalar
        def _(act):
            def attention(L, phase):
                units = UNITS[phase]
                base = UPL * L + UBASE[phase]

                def exps(u):
                    un, w = units[u], units[u]["n"] * P
                    act.wait_ge(nmax_done, base + u + 1)
                    if u >= 2:
                        act.wait_ge(T.full, T[("p", L, phase, u - 2)])
                    if un["kind"].startswith("swa"):
                        act.activation(stat["es"][:, u % 8:u % 8 + 1], sink[:, un["h"]:un["h"] + 1], ACT.Exp,
                                       bias=stat["nm"][:, u % 8:u % 8 + 1], scale=1.0)
                    src = sB[:, u % 2, 0:w] if "mask" in un else two(2 * (u % 2), w)
                    act.activation(pB[phase][:, u % 2, 0:w], src, ACT.Exp, bias=stat["nm"][:, u % 8:u % 8 + 1],
                                   scale=1.0, accum_out=stat["sm"][:, u % 8:u % 8 + 1]).then_inc(S[u % 2].free, 1)

                def copy(u):
                    a, d = split(units[u]["n"])
                    if d:
                        act.wait_ge(T.full, T[("p", L, phase, u)])
                        if u >= 2:
                            act.wait_ge(O.full, O[("o", L, phase, u - 2)])
                        act.activation(pT[phase][:, u % 2, a * P:(a + d) * P], ps[:, 5, 0:d * P],
                                       ACT.Copy).then_inc(T.free, 1)

                for s in range(len(units) + 1):
                    if s < len(units):
                        exps(s)
                    if s >= 1:
                        copy(s - 1)

            act.wait_ge(c_in, 32)
            act.wait_ge(zero_set, 2)
            act.activation(sc[:, :, 0:1], cc[:, 0, :].unsqueeze(2), ACT.Silu).then_inc(sc_set, 1)
            act.activation(sc[:, :, 1:2], cc[:, 1, :].unsqueeze(2), ACT.Silu).then_inc(sc_set, 1)
            j7 = junk7.bitcast(BF16)

            def square(L, i):
                if L == 0:
                    act.wait_ge(x7_in[i], 16)
                else:
                    act.wait_ge(comb_done, TILES * (L - 1) + i + 1)
                if i:
                    act.wait_ge(sq_done, norm_no(L, 1, i - 1))
                act.activation(j7, x7[:, i, :], ACT.Square, accum_out=ssq[:, i:i + 1]).then_inc(sq_done, 1)

            def h_copy(L, i):
                act.wait_ge(T.full, T[("h", L, i)])
                t = ORDER[i]
                for n in range(2):
                    cp = act.activation(hT[:, 4 * n:4 * n + 4, t * P:(t + 1) * P],
                                        ps[:, 4 + n, :].rearrange("p (k n) -> p k n", k=4), ACT.Copy)
                cp.then_inc(T.free, 1)

            for i in range(TILES):
                square(0, i)
            for i in range(TILES):
                h_copy(0, i)
            meet(act, "act")
            junk = junk1.bitcast(BF16)
            for L in range(DEPTH):
                for s in range(TILES + 1):
                    if L == 0:
                        for rows, a, b in ((slots_x, 5 * s, min(5 * s + 5, NE + NOVF)),
                                           (slots_y, NE + 2 * s, min(NE + 2 * s + 2, NE + NOVF))):
                            if a < b:
                                act.dma_start(rows[a * P:b * P, :].rearrange("(p c) (a n) -> p (c a) n", p=P, n=256),
                                              zeros[:, :].unsqueeze(1).broadcast_to([P, (b - a) * 4, 256])
                                              ).then_inc(zero_out, 16)
                    if s < TILES:
                        i = s
                        kv = 5 if ORDER[i] == 4 else ORDER[i]
                        act.wait_ge(S[1].full, S[1][("in", L, i)])
                        if i >= 2:
                            act.wait_ge(O.full, O[("xn", L, i - 2)])
                            if i == 2:
                                act.wait_ge(ctx_out, 96 * (L + 1))
                        act.activation(proj[:, i % 2, C_QN:C_QN + 512], ps[:, 2, :], ACT.Copy)
                        act.activation(v_loc[:, kv, :], ps[:, 3, 0:384], ACT.Copy).then_inc(S[1].free, 1)
                        act.wait_ge(S[0].free, S[0].freed[("in", L, i)])
                        if i:
                            act.wait_ge(sq2_done, TILES * L + i)
                        act.activation(junk[:, 0:256], proj[:, i % 2, 0:256], ACT.Square,
                                       accum_out=ssq[:, 8 + 2 * i:9 + 2 * i])
                        act.activation(junk[:, 256:384], proj[:, i % 2, C_CKV:C_CKV + 128], ACT.Square,
                                       accum_out=ssq[:, 9 + 2 * i:10 + 2 * i]).then_inc(sq2_done, 1)
                    if s >= 1:
                        for i in ([5, 0] if s == 1 else [s - 1]):
                            kv = 4 if i == 5 else (5 if ORDER[i] == 4 else ORDER[i])
                            k0 = kv * P
                            act.wait_ge(T.full, T[("xp", L, i)])
                            if i < 5:
                                t0 = ORDER[i] * P
                                act.activation(cqT[:, :, t0:t0 + P], ps[:, 4, 0:256].rearrange("p (k n) -> p k n", k=2), ACT.Copy)
                                act.activation(ckvT[:, k0:k0 + P], ps[:, 4, 256:384], ACT.Copy)
                            else:
                                act.activation(ckvT[:, k0:k0 + P], ps[:, 4, 0:P], ACT.Copy)
                            act.activation(kpeT[0:ROPE, k0:k0 + P], ps[0:ROPE, 4, 384:512], ACT.Copy).then_inc(T.free, 1)
                            act.wait_ge(O.full, O[("xn", L, i)])
                            kn = ps[:, 6, 256:512] if i < 5 else ps[:, 6, 0:256]
                            if i < 5:
                                act.wait_ge(pad_set, 2 * L + 2)
                                act.activation(qnP[0:64, 0:4:2, t0:t0 + P],
                                               ps[0:64, 6, 0:256].rearrange("p (k n) -> p k n", k=2), ACT.Copy, scale=HEAD_SCALE)
                                act.activation(qnP[64:128, 1:4:2, t0:t0 + P],
                                               ps[64:128, 6, 0:256].rearrange("p (k n) -> p k n", k=2), ACT.Copy, scale=HEAD_SCALE)
                            act.activation(knT[:, :, k0:k0 + P], kn.rearrange("p (k n) -> p k n", k=2),
                                           ACT.Copy).then_inc(O.free, 1)
                meet(act, "act")
                attention(L, 2)
                meet(act, "act")
                for i in range(TILES + 1):
                    if i < TILES:
                        act.wait_ge(T.full, T[("uq", L, i)])
                        if i >= 2:
                            act.wait_ge(S[i % 2].full, S[i % 2][("qt", L, i - 2)])
                        act.activation(qt[:, i % 2, :], two(4, 768), ACT.Copy, scale=MLA_SCALE).then_inc(T.free, 1)
                    if i in (1, 3):
                        act.wait_ge(S[1].full, S[1][("uk", L, i)])
                        act.activation(kT[0:64, 2 * i, :], two(2, 768)[0:64], ACT.Copy)
                        act.activation(kT[0:64, 2 * i + 1, :], two(2, 768)[64:128], ACT.Copy).then_inc(S[1].free, 1)
                    if i % 2 == 0:
                        act.wait_ge(O.full, O[("uv", L, i)])
                        act.activation(v_mla[:, i, :], ps[:, 6, :], ACT.Copy).then_inc(O.free, 1)
                    if i >= 1 and (i - 1) % 2 == 0:
                        t0 = ORDER[i - 1] * P
                        act.wait_ge(S[0].full, S[0][("qt", L, i - 1)])
                        act.activation(qT[0:QK, :, t0:t0 + P], two(0)[0:QK].rearrange("p (h n) -> p h n", h=8),
                                       ACT.Copy).then_inc(S[0].free, 1)
                meet(act, "act")
                attention(L, 4)
                meet(act, "act")
                for s in range(TILES + 3):
                    if s < TILES:
                        if s >= 2:
                            act.wait_ge(S[s % 2].full, S[s % 2][("out", L, s - 2)])
                        act.wait_ge(T.full, T[("ho", L, s)])
                        act.activation(hoT[:, s % 2, 0:512], ps[:, 4, :], ACT.Copy).then_inc(T.free, 1)
                    if 2 <= s < TILES + 2:
                        act.wait_ge(res_done, TILES * L + s - 1)
                        if s > 2:
                            act.wait_ge(sq_done, norm_no(L, 5, s - 3))
                        act.activation(junk5, xt5[:, s % 2, :], ACT.Square,
                                       accum_out=ssq[:, s - 2:s - 1]).then_inc(sq_done, 1)
                    if s >= 3:
                        i = s - 3
                        if i >= 2:
                            act.wait_ge(routed, 4 * L + i - 1)
                        act.wait_ge(T.full, T[("h2", L, i)])
                        act.activation(h2T[:, i % 2, 0:512], ps[:, 4, :], ACT.Copy).then_inc(T.free, 1)
                act.wait_ge(rx1, L + 1)
                act.activation(r_ge, r_gd, ACT.Exp).then_inc(rx1_done, 1)
                act.wait_ge(rx2, L + 1)
                act.activation(r_e2, r_d2, ACT.Exp).then_inc(rx2_done, 1)
                meet(act, "act")
                n_ov = act.value_load(ctl[0:1, 0:1], min_val=0, max_val=NOVF)
                E0 = NE * L

                def x_copy(e, b, early):
                    if not early:
                        act.wait_ge(e_h, E0 + e - 1)
                    act.wait_ge(e_xT, E0 + e + 1)
                    act.activation(xgT[:, b, 0:512], ps[:, 4, :], ACT.Copy).then_inc(e_xTa, 1)

                def silu(e, b):
                    act.wait_ge(e_h, E0 + e + 1)
                    act.activation(sg[:, b, :], ps[:, b, 0:FF], ACT.Silu).then_inc(e_sg, 1)

                def y_copy(e, b, early):
                    act.wait_ge(e_d, E0 + e + 1)
                    if not early:
                        act.wait_ge(ys_out[b], 16 * (E0 // 2) + (e - b) * 8)
                    act.activation(yb[:, b, 0:512], ps[:, 2, :], ACT.Copy).then_inc(e_ya, 1)

                x_copy(0, 0, True)
                silu(0, 0)
                x_copy(1, 1, True)
                silu(1, 1)
                x_copy(2, 0, False)
                y_copy(0, 0, True)
                silu(2, 0)
                x_copy(3, 1, False)
                y_copy(1, 1, True)
                with act.Fori(3, NE - 1, 2) as e0:
                    for j in range(2):
                        e, b = e0 + j, 1 - j
                        silu(e, b)
                        x_copy(e + 1, 1 - b, False)
                        y_copy(e - 1, 1 - b, False)
                silu(15, 1)
                y_copy(14, 0, False)
                y_copy(15, 1, False)
                with act.If(n_ov > 0):
                    act.wait_ge(ys_out[0], 8 * (E0 + NE))
                    with act.Fori(0, NOVF) as c:
                        n = c + 1
                        act.wait_ge(ov[L]["xT"], n)
                        act.activation(xgT[:, 0, 0:512], ps[:, 4, :], ACT.Copy)
                        act.activation(xgT[:, 0, 512:1024], ps[:, 5, :], ACT.Copy).then_inc(ov[L]["xTe"], 1)
                        act.wait_ge(ov[L]["h"], n)
                        act.activation(sg[:, 0, :], ps[:, 0, 0:FF], ACT.Silu).then_inc(ov[L]["sg"], 1)
                        act.wait_ge(ov[L]["d"], n)
                        act.activation(yb[:, 0, :], two(2), ACT.Copy).then_inc(ov[L]["y"], 1)
                meet(act, "act")
                def y1_scale(i):
                    act.wait_ge(y_in[i], 32 * (L + 1))
                    act.activation(y1[:, i, :], y1[:, i, :], ACT.Copy,
                                   scale=wts[:, ORDER[i], 0:1]).then_inc(y1_scaled, 1)

                if L < DEPTH - 1:
                    for s in range(TILES + 2):
                        if s < TILES:
                            y1_scale(s)
                        if 1 <= s <= TILES:
                            square(L + 1, s - 1)
                            t = ORDER[s - 1]
                            act.dma_start(xbuf[t * P:(t + 1) * P, :], x7[:, s - 1, :]).then_inc(x7_out, 16)
                        if s >= 2:
                            h_copy(L + 1, s - 2)
                else:
                    for s in range(TILES + 2):
                        if s < TILES:
                            y1_scale(s)
                        if 1 <= s <= TILES:
                            i = s - 1
                            act.wait_ge(comb_done, TILES * L + i + 1)
                            if i:
                                act.wait_ge(fin_sq, i)
                            act.activation(j7, x7[:, i, :], ACT.Square,
                                           accum_out=ssq[:, 24 + i:25 + i]).then_inc(fin_sq, 1)
                        if s >= 2:
                            t = ORDER[s - 2]
                            act.wait_ge(fin_done, s - 1)
                            dst = t_out["y_prompt"] if t == 4 else t_out["y_sample"][t * P:(t + 1) * P, :]
                            act.dma_start(dst, x7[:, s - 2, :]).then_inc(x7_out, 16)
                act.wait_ge(x7_out, 16 * TILES * (L + 1))
                meet(act, "act")

        @block.gpsimd
        def _(pool):
            def rstd(ins, outs, scale):
                then(pool, "pool", pool.tensor_scalar(outs, ins, scale, EPS, ALU.mult, ALU.add))
                w = outs.shape[-1]
                return pool.tensor_tensor(outs, outs, mhalf[:, 0:w], ALU.pow)

            def entry(L, i):
                pool.wait_ge(sq_done, norm_no(L, 1, i))
                rstd(ssq[:, i:i + 1], rsd[:, i:i + 1], 1.0 / D).then_inc(rs_done, 1)
                pool.wait_ge(hA_done, norm_no(L, 1, i))
                pool.tensor_tensor(y1[:, i, :], y1[:, i, :], rowB[:, int(ORDER[i] == 4), :], ALU.add).then_inc(h_done, 1)

            pool.memset(sc[:, :, :], 0.0).then_inc(zero_set, 1)
            pool.memset(zeros[:, :], 0.0).then_inc(zero_set, 1)
            pool.memset(brow[:, :, :], 0.0).then_inc(half_set, 1)
            pool.memset(mhalf[:, :], -0.5).then_inc(half_set, 1)
            pool.wait_ge(half_set, 2)
            pool.wait_ge(zero_set, 2)
            pool.sem_inc(sc_set, 1)

            def bias_loads(L):
                bm = t_in["b_mod"][L].rearrange("(g i n) -> i g n", g=3, i=4)
                for i in range(4):
                    pool.dma_start(brow[32 * i:32 * i + 2, :, :],
                                   bm[i:i + 1].broadcast_to([2, 3, 512])).then_inc(bmod_in, 16)

            def vector_loads(L):
                pool.dma_start(nrm[:, :], t_in["norm1"][L:L + 1, :].broadcast_to([P, D])).then_inc(nrm_in, 16)
                pool.dma_start(gqa[:, :], t_in["g_qa"][L:L + 1, :].broadcast_to([P, 256])).then_inc(vec_in, 16)
                pool.dma_start(gkva[:, :], t_in["g_kva"][L:L + 1, :].broadcast_to([P, 128])).then_inc(vec_in, 16)
                pool.dma_start(sink[:, :], t_in["swa_sink"][L:L + 1, :].broadcast_to([P, 4])).then_inc(vec_in, 16)

            bias_loads(0)
            vector_loads(0)
            for i in range(TILES):
                entry(0, i)
            meet(pool, "pool")
            for L in range(DEPTH):
                src = t_in["x0"] if L == 0 else xbuf
                for at, w, name in ((0, 128, "cache_mla_ckv"), (128, 32, "cache_mla_kpe"),
                                    (160, 128, "cache_swa_k"), (288, 256, "cache_na_k")):
                    pool.dma_start(ck[:, at:at + w], t_in[name][L]).then_inc(cache_in, 16)
                pool.dma_start(v_loc[:, 4, :], t_in["cache_v"][L]).then_inc(cache_in, 16)
                pool.memset(qsP, 0.0).then_inc(pad_set, 1)
                pool.memset(qnP, 0.0).then_inc(pad_set, 1)
                for i in range(TILES):
                    pool.wait_ge(sq2_done, TILES * L + i + 1)
                    a = 8 + 2 * i
                    then(pool, "pool", pool.tensor_scalar(rsd[:, a:a + 1], ssq[:, a:a + 1], 1.0 / 256, EPS, ALU.mult, ALU.add))
                    then(pool, "pool", pool.tensor_scalar(rsd[:, a + 1:a + 2], ssq[:, a + 1:a + 2], 1.0 / 128, EPS, ALU.mult, ALU.add))
                    pool.tensor_tensor(rsd[:, a:a + 2], rsd[:, a:a + 2], mhalf[:, 0:2], ALU.pow).then_inc(rs2_done, 1)
                meet(pool, "pool")
                pool.dma_start(nrm[:, :], t_in["norm2"][L:L + 1, :].broadcast_to([P, D])).then_inc(nrm_in, 16)
                mad = cst["madd"].unsqueeze(1).broadcast_to([P, 15, 64])
                for h in range(4):
                    pool.wait_ge(bias_mul, 4 * L + h + 1)
                    bh = bias[:, h, :].rearrange("p (j c) -> p j c", j=15)
                    pool.tensor_tensor(bh, bh, mad, ALU.add).then_inc(bias_done, 1)
                meet(pool, "pool")
                if L < DEPTH - 1:
                    bias_loads(L + 1)
                meet(pool, "pool")
                meet(pool, "pool")
                def x5_load(i):
                    t = ORDER[i]
                    pool.dma_start(xt5[:, i % 2, :], src[t * P:(t + 1) * P, :]).then_inc(xt_in[i % 2], 16)

                x5_load(0)
                x5_load(1)
                for i in range(TILES):
                    t = ORDER[i]
                    pool.wait_ge(xt_in[i % 2], x_no(L, i))
                    pool.wait_ge(res_mul, TILES * L + i + 1)
                    pool.tensor_tensor(xt5[:, i % 2, :], xt5[:, i % 2, :], tmp5, ALU.add).then_inc(res_done, 1)
                    pool.wait_ge(res_done, TILES * L + i + 1)
                    pool.dma_start(xbuf[t * P:(t + 1) * P, :], xt5[:, i % 2, :]).then_inc(xs_out, 16)
                    pool.wait_ge(sq_done, norm_no(L, 5, i))
                    rstd(ssq[:, i:i + 1], rsd[:, i:i + 1], 1.0 / D).then_inc(rs_done, 1)
                    pool.wait_ge(hA_done, norm_no(L, 5, i))
                    pool.tensor_tensor(h2[:, t, :], h2[:, t, :], rowB2[:, int(t == 4), :], ALU.add).then_inc(h_done, 1)
                    if i + 2 < TILES:
                        pool.wait_ge(xs_out, 16 * (TILES * L + i + 1))
                        x5_load(i + 2)
                pool.wait_ge(xs_out, 16 * TILES * (L + 1))
                if L == 0:
                    pool.wait_ge(zero_out, 16 * 10)
                pool.wait_ge(idx_done, L + 1)
                for j in range(2):
                    for t in range(TILES):
                        pool.indirect_dma_start(slots_x, bass.IndirectOffsetOnAxis(ap=sidx[:, j * TILES + t:j * TILES + t + 1], axis=0),
                                                h2[:, t, :], None).then_inc(scat_out, 16)
                pool.wait_ge(scat_out, 160 * (L + 1))
                meet(pool, "pool")
                n_ov = pool.value_load(ctl[0:1, 0:1], min_val=0, max_val=NOVF)
                E0 = NE * L
                if L < DEPTH - 1:
                    vector_loads(L + 1)
                else:
                    pool.dma_start(nrm[:, :], t_in["norm_final"].unsqueeze(0).broadcast_to([P, D])).then_inc(nrm_in, 16)
                with pool.Fori(0, NE // 2) as pair:
                    for j in range(2):
                        e = pair * 2 + j
                        row = pair * (2 * P) + j * P
                        pool.wait_ge(e_ya, e + (E0 + 1))
                        pool.wait_ge(e_yd, e + (E0 + 1))
                        pool.dma_start(slots_y[bass.ds(row, P), :], yb[:, j, :]).then_inc(ys_out[j], 16)
                for j in range(2):
                    pool.wait_ge(ys_out[j], 16 * (E0 + NE) // 2)
                with pool.If(n_ov > 0):
                    for c in range(NOVF):
                        row = (NE + c) * P
                        pool.wait_ge(ov[L]["y"], c + 1)
                        pool.dma_start(slots_y[row:row + P, :], yb[:, 0, :]).then_inc(ov[L]["out"], 16)
                        pool.wait_ge(ov[L]["out"], 16 * (c + 1))
                meet(pool, "pool")
                def gather(dst, j, i):
                    at = j * TILES + ORDER[i]
                    pool.indirect_dma_start(dst, None, slots_y,
                                            bass.IndirectOffsetOnAxis(ap=sidx[:, at:at + 1], axis=0)).then_inc(y_in[i], 16)

                for i in range(TILES):
                    gather(y1[:, i, :], 0, i)
                    if i == TILES - 1:
                        pool.wait_ge(comb_done, TILES * L + 1)
                    gather(y2[:, i % 4, :], 1, i)
                for i in range(TILES):
                    if L < DEPTH - 1:
                        entry(L + 1, i)
                    else:
                        pool.wait_ge(fin_sq, i + 1)
                        rstd(ssq[:, 24 + i:25 + i], rsd[:, 24 + i:25 + i], 1.0 / D).then_inc(fin_rs, 1)
                meet(pool, "pool")

        @block.vector
        def _(dve):
            TT, TS, STT = dve.tensor_tensor, dve.tensor_scalar, dve.scalar_tensor_tensor

            def mod_rows(L, g):
                dve.wait_ge(M.full, M[("mod", L, g)])
                if g == 0:
                    dve.wait_ge(bmod_in, 64 * (L + 1))
                TT(mrow[:, g, :], ps[:, 7, :], brow[:, g, :], ALU.add).then_inc(mods_done, 1)
                dve.wait_ge(mods_done, 3 * L + g + 1)
                dve.sem_inc(M.free, 1)

            bcn = [0]

            def row_from(L, kind, vec, half, dst, scale_norm=False):
                lane, b = ((O, 6), (M, 7))[bcn[0] % 2]
                bcn[0] += 1
                dve.wait_ge(lane.full, lane[("bc", L, kind, vec, half)])
                d = dst[:, half * 512:(half + 1) * 512]
                if scale_norm:
                    ins = STT(d, ps[:, b, :], 1.0, nrm[:, half * 512:(half + 1) * 512], ALU.add, ALU.mult)
                else:
                    ins = dve.tensor_copy(d, ps[:, b, :])
                return ins.then_inc(lane.free, 1)

            def rope(x, cos, sin, tmp, heads, dim):
                h4 = dim // 4

                def v(a):
                    return a.rearrange("p (h d) -> p h d", h=heads)

                def halves(a, j):
                    return a.rearrange("p (m s d) -> p m s d", s=2, d=h4)[:, :, j, :]

                def table(a, j):
                    return a.rearrange("p (m s d) -> p m s d", s=2, d=h4)[:, :, j, :].unsqueeze(1).broadcast_to([P, heads, 2, h4])

                n = heads * dim
                TT(v(tmp[:, 0, 0:n]), v(x), cos.unsqueeze(1).broadcast_to([P, heads, dim]), ALU.mult)
                for j in range(2):
                    o = halves(tmp[:, 1, 0:n], j).rearrange("p (h a) d -> p h a d", a=2)
                    i = halves(x, 1 - j).rearrange("p (h a) d -> p h a d", a=2)
                    last = TT(o, i, table(sin, j), ALU.mult)
                then(dve, "dve", last)
                return TT(x, tmp[:, 0, 0:n], tmp[:, 1, 0:n], ALU.add)

            def attention(L, phase):
                units = UNITS[phase]

                def maximum(u):
                    un, w = units[u], units[u]["n"] * P
                    dve.wait_ge(S[u % 2].full, S[u % 2][("s", L, phase, u)])
                    src = two(2 * (u % 2), w)
                    mx, m2, nm = (stat[n][:, u % 8:u % 8 + 1] for n in ("mx", "m2", "nm"))
                    if "mask" in un and u >= 2:
                        dve.wait_ge(S[u % 2].free, S[u % 2].freed[("s", L, phase, u - 2)])
                    if un["kind"] == "swa":
                        then(dve, "dve", dve.tensor_tensor_reduce(sB[:, u % 2, 0:w], src, un["mask"], 1.0,
                                                                  sink[:, un["h"]:un["h"] + 1], ALU.add, ALU.max, mx))
                        TS(nm, mx, -1.0, None, ALU.mult).then_inc(nmax_done, 1)
                    elif un["kind"] == "na":
                        then(dve, "dve", TS(sB[:, u % 2, 512:640], src[:, 512:640], 1.0, NEG, ALU.mult, ALU.max,
                                            accum_out=m2))
                        then(dve, "dve", dve.tensor_tensor_reduce(sB[:, u % 2, 0:512], src[:, 0:512], un["mask"], 1.0,
                                                                  m2, ALU.add, ALU.max, mx))
                        TS(nm, mx, -1.0, None, ALU.mult).then_inc(nmax_done, 1)
                    elif un["kind"] == "swa_ctx":
                        then(dve, "dve", dve.tensor_reduce(mx, src, AX.X, ALU.max))
                        TS(nm, mx, sink[:, un["h"]:un["h"] + 1], -1.0, ALU.max, ALU.mult).then_inc(nmax_done, 1)
                    else:
                        dve.tensor_reduce(nm, src, AX.X, ALU.max, negate=True).then_inc(nmax_done, 1)

                def copy(u):
                    a, d = split(units[u]["n"])
                    dve.wait_ge(T.full, T[("p", L, phase, u)])
                    if u >= 2:
                        dve.wait_ge(O.full, O[("o", L, phase, u - 2)])
                    dve.tensor_copy(pT[phase][:, u % 2, 0:a * P], ps[:, 4, 0:a * P]).then_inc(T.free, 1)

                def norm(u):
                    un = units[u]
                    sm, es, ri = (stat[n][:, u % 8:u % 8 + 1] for n in ("sm", "es", "ri"))
                    if un["kind"].startswith("swa"):
                        then(dve, "dve", TT(sm, sm, es, ALU.add))
                    then(dve, "dve", dve.reciprocal(ri, sm))
                    dve.wait_ge(O.full, O[("o", L, phase, u)])
                    TS(heads[:, un["t"], un["col"]:un["col"] + 64], ps[:, 6, 0:64], ri, None,
                       ALU.mult).then_inc(O.free, 1)

                for s in range(len(units) + 2):
                    if s < len(units):
                        maximum(s)
                    if s >= 2:
                        norm(s - 2)
                    if 1 <= s <= len(units):
                        copy(s - 1)
                    if phase == 2 and s in (18, 32):
                        mod_rows(L, 1 if s == 18 else 2)
                    if phase == 4 and s == NEXT_MOD + 2 and L < DEPTH - 1:
                        mod_rows(L + 1, 0)

            def entry_rows(L):
                dve.wait_ge(nrm_in, 16 * (2 * L + 1))
                for kind in (1, 0):
                    for v, dst in ((0, rowB), (1, rowA)):
                        for half in range(2):
                            row_from(L, kind, v, half, dst[:, kind, :], v == 1)
                for lane in (O, M):
                    dve.wait_ge(lane.free, lane.freed[("bc", L, 0, 1, 0 if lane is O else 1)])

            def entry(L, i):
                dve.wait_ge(rs_done, norm_no(L, 1, i))
                STT(y1[:, i, :], x7[:, i, :], rsd[:, i:i + 1], rowA[:, int(ORDER[i] == 4), :], ALU.mult,
                    ALU.mult).then_inc(hA_done, 1)

            dve.wait_ge(const_in, 16)
            c32, s32 = (cst[n].rearrange("p (t d) -> p t d", t=4) for n in ("cos32", "sin32"))
            c64, s64 = (cst[n].rearrange("p (t d) -> p t d", t=4) for n in ("cos64", "sin64"))
            dve.wait_ge(half_set, 2)
            mod_rows(0, 0)
            entry_rows(0)
            for i in range(TILES):
                entry(0, i)
            meet(dve, "dve")
            for L in range(DEPTH):
                dve.wait_ge(small_in, 48 * (L + 1))
                dve.wait_ge(vec_in, 48 * (L + 1))
                for s in range(TILES + 1):
                    if s < TILES:
                        i = s
                        q = proj[:, i % 2, :]
                        dve.wait_ge(S[0].full, S[0][("in", L, i)])
                        if i >= 2:
                            dve.wait_ge(T.full, T[("xp", L, i - 2)])
                            if i == 2:
                                dve.wait_ge(ctx_out, 96 * (L + 1))
                        dve.tensor_copy(q[:, 0:416], ps[:, 0, 0:416])
                        dve.tensor_copy(q[:, 416:800], ps[:, 1, 0:384]).then_inc(S[0].free, 1)
                        dve.wait_ge(S[0].free, S[0].freed[("in", L, i)])
                        a = 8 + 2 * i
                        if ORDER[i] != 4:
                            t = ORDER[i]
                            then(dve, "dve", rope(q[:, C_QS:C_QS + 384], c64[:, t, :], s64[:, t, :], rt, 6, 64))
                            then(dve, "dve", rope(q[:, C_KPE:C_KPE + 32], c32[:, t, :], s32[:, t, :], rt, 1, 32))
                        dve.wait_ge(rs2_done, TILES * L + i + 1)
                        STT(q[:, 0:256], q[:, 0:256], rsd[:, a:a + 1], gqa[:, :], ALU.mult, ALU.mult)
                        STT(q[:, C_CKV:C_CKV + 128], q[:, C_CKV:C_CKV + 128], rsd[:, a + 1:a + 2], gkva[:, :],
                            ALU.mult, ALU.mult).then_inc(post_done, 1)
                    if s >= 1:
                        for i in ([5, 0] if s == 1 else [s - 1]):
                            kv = 4 if i == 5 else (5 if ORDER[i] == 4 else ORDER[i])
                            dve.wait_ge(T.full, T[("xp", L, i)])
                            if i < 5:
                                t0 = ORDER[i] * P
                                dve.wait_ge(pad_set, 2 * L + 2)
                                for lo in (0, 64):
                                    TS(qsP[lo:lo + 64, lo // 32:lo // 32 + 2, t0:t0 + P],
                                       ps[lo:lo + 64, 5, 0:256].rearrange("p (k n) -> p k n", k=2), HEAD_SCALE, None, ALU.mult)
                            ks = ps[:, 5, 256:384] if i < 5 else ps[:, 5, 0:P]
                            dve.tensor_copy(ksT[:, kv * P:(kv + 1) * P], ks).then_inc(T.free, 1)
                meet(dve, "dve")
                m01 = cst["m01"].unsqueeze(1).broadcast_to([P, 7, 64])
                for h in range(4):
                    dve.wait_ge(S[h % 2].full, S[h % 2][("bias", L, h)])
                    m01f = cst["m01"].unsqueeze(1)
                    for n in range(2):
                        bk = ps[:, 2 * (h % 2) + n, :]
                        o = bias[:, h, n * 480:(n + 1) * 480]
                        if n == 0:
                            TT(o[:, 0:448].rearrange("p (j c) -> p j c", j=7), bk[:, 0:448].rearrange("p (j c) -> p j c", j=7),
                               m01, ALU.mult)
                            TT(o[:, 448:480], bk[:, 448:480], cst["m01"][:, 0:32], ALU.mult)
                        else:
                            TT(o[:, 0:32], bk[:, 0:32], cst["m01"][:, 32:64], ALU.mult)
                            last = TT(o[:, 32:480].rearrange("p (j c) -> p j c", j=7),
                                      bk[:, 32:480].rearrange("p (j c) -> p j c", j=7), m01, ALU.mult)
                    then(dve, "dve", last)
                    dve.sem_inc(S[h % 2].free, 1)
                    dve.sem_inc(bias_mul, 1)
                attention(L, 2)
                meet(dve, "dve")
                for h in range(MLA_H):
                    dve.tensor_copy(kT[64:96, h, :], kpeT[0:ROPE, :])
                for i in range(TILES + 1):
                    if i in (0, 2):
                        dve.wait_ge(S[0].full, S[0][("uk", L, i)])
                        dve.tensor_copy(kT[0:64, 2 * i, :], two(0, 768)[0:64])
                        dve.tensor_copy(kT[0:64, 2 * i + 1, :], two(0, 768)[64:128]).then_inc(S[0].free, 1)
                    if i % 2 == 1:
                        dve.wait_ge(M.full, M[("uv", L, i)])
                        dve.tensor_copy(v_mla[:, i, :], ps[:, 7, :]).then_inc(M.free, 1)
                    if i < TILES:
                        dve.wait_ge(T.free, T.freed[("uq", L, i)])
                        t = ORDER[i]
                        if t == 4:
                            dve.sem_inc(q_done, 1)
                        else:
                            x = qt[:, i % 2, :].rearrange("p (h d) -> p h d", h=MLA_H)[:, :, NOPE:QK]
                            dve.wait_ge(q_done, TILES * L + i)
                            t1 = rq[:, 0, :].rearrange("p (h d) -> p h d", h=MLA_H)
                            t2 = rq[:, 1, :].rearrange("p (h d) -> p h d", h=MLA_H)
                            TT(t1, x, c32[:, t, :].unsqueeze(1).broadcast_to([P, MLA_H, ROPE]), ALU.mult)
                            for ax in range(2):
                                for j in range(2):
                                    o0, i0 = 16 * ax + 8 * j, 16 * ax + 8 * (1 - j)
                                    last = TT(t2[:, :, o0:o0 + 8], x[:, :, i0:i0 + 8],
                                              s32[:, t, o0:o0 + 8].unsqueeze(1).broadcast_to([P, MLA_H, 8]), ALU.mult)
                            then(dve, "dve", last)
                            TT(x, t1, t2, ALU.add).then_inc(q_done, 1)
                    if i >= 1 and (i - 1) % 2 == 1:
                        t0 = ORDER[i - 1] * P
                        dve.wait_ge(S[1].full, S[1][("qt", L, i - 1)])
                        dve.tensor_copy(qT[0:QK, :, t0:t0 + P], two(2)[0:QK].rearrange("p (h n) -> p h n", h=8)).then_inc(S[1].free, 1)
                meet(dve, "dve")
                attention(L, 4)
                meet(dve, "dve")
                dve.wait_ge(nrm_in, 16 * (2 * L + 2))
                for vec, dst in ((2, rowG1), (4, rowA2), (3, rowB2)):
                    for kind in (1, 0):
                        for half in range(2):
                            last = row_from(L, kind, vec, half, dst[:, kind, :], vec == 4)
                for lane in (O, M):
                    dve.wait_ge(lane.free, lane.freed[("bc", L, 0, 3, 0 if lane is O else 1)])

                for s in range(TILES + 3):
                    if s < TILES:
                        if s >= 2:
                            dve.wait_ge(S[s % 2].full, S[s % 2][("out", L, s - 2)])
                        dve.wait_ge(T.full, T[("ho", L, s)])
                        dve.tensor_copy(hoT[:, s % 2, 512:1024], ps[:, 5, :]).then_inc(T.free, 1)
                    if 1 <= s <= TILES:
                        i = s - 1
                        kind = int(ORDER[i] == 4)
                        dve.wait_ge(S[i % 2].full, S[i % 2][("out", L, i)])
                        if i >= 1:
                            dve.wait_ge(res_done, TILES * L + i)
                        then(dve, "dve", TT(tmp5, two(2 * (i % 2)), rowG1[:, kind, :], ALU.mult))
                        dve.sem_inc(S[i % 2].free, 1)
                        dve.sem_inc(res_mul, 1)
                    if 2 <= s < TILES + 2:
                        i = s - 2
                        dve.wait_ge(rs_done, norm_no(L, 5, i))
                        STT(h2[:, ORDER[i], :], xt5[:, i % 2, :], rsd[:, i:i + 1], rowA2[:, int(ORDER[i] == 4), :],
                            ALU.mult, ALU.mult).then_inc(hA_done, 1)
                    if s >= 3:
                        i = s - 3
                        if i >= 2:
                            dve.wait_ge(routed, 4 * L + i - 1)
                        dve.wait_ge(T.full, T[("h2", L, i)])
                        dve.tensor_copy(h2T[:, i % 2, 512:1024], ps[:, 5, :]).then_inc(T.free, 1)
                def go(ins):
                    then(dve, "dve", ins)

                def b4(a):
                    return a.unsqueeze(2).broadcast_to([P, TILES, 4])

                w4 = cst["w4"].unsqueeze(1).broadcast_to([P, TILES, 4])

                def first_max(x, m, oh):
                    go(dve.tensor_reduce(m, x, AX.X, ALU.max))
                    go(TT(r_eq, x, b4(m), ALU.is_equal))
                    go(TT(r_eq, r_eq, w4, ALU.mult))
                    go(dve.tensor_reduce(r_g, r_eq, AX.X, ALU.max))
                    go(TT(oh, r_eq, b4(r_g), ALU.is_equal))

                dve.wait_ge(O.full, O[("rt", L)])
                go(dve.tensor_copy(r_lg.rearrange("p a b -> p (a b)"), ps[:, 6, 0:100]))
                dve.sem_inc(O.free, 1)
                grp = r_lg[:, :, 0:4]
                first_max(grp, r_m, r_oh)
                go(TT(r_gd, grp, b4(r_m), ALU.subtract))
                dve.sem_inc(rx1, 1)
                elog = r_lg[:, :, 4:20].rearrange("p t (g e) -> p t g e", g=4)
                go(TT(r_prod, elog, r_oh.unsqueeze(3).broadcast_to([P, TILES, 4, 4]), ALU.mult))
                go(dve.tensor_reduce(r_sel, r_prod.rearrange("p t g e -> p t e g"), AX.X, ALU.add))
                first_max(r_sel, r_m, r_oh1)
                go(STT(r_sel, r_oh1, NEG, r_sel, ALU.mult, ALU.add))
                go(dve.tensor_copy(r_d2, r_m))
                first_max(r_sel, r_m, r_oh2)
                go(TT(r_d2, r_m, r_d2, ALU.subtract))
                dve.sem_inc(rx2, 1)
                for c, oh in ((r_c1, r_oh1), (r_c2, r_oh2)):
                    go(TT(c.rearrange("p t (g e) -> p t g e", g=4), r_oh.unsqueeze(3).broadcast_to([P, TILES, 4, 4]),
                          oh.unsqueeze(2).broadcast_to([P, TILES, 4, 4]), ALU.mult))
                TT(r_T, r_c1, r_c2, ALU.add).then_inc(pick_done, 1)
                dve.wait_ge(rx1_done, L + 1)
                go(dve.tensor_reduce(r_g, r_ge, AX.X, ALU.add))
                dve.wait_ge(rx2_done, L + 1)
                go(TS(r_m, r_e2, 1.0, None, ALU.add))
                go(TT(r_m, r_m, r_g, ALU.mult))
                go(dve.reciprocal(wts[:, :, 0], r_m))
                go(TT(wts[:, :, 1], wts[:, :, 0], r_e2, ALU.mult))
                dve.wait_ge(M.full, M[("cnt", L)])
                go(dve.tensor_copy(r_tmp.rearrange("p a b -> p (a b)"), ps[:, 7, 0:80]))
                dve.sem_inc(M.free, 1)
                dve.wait_ge(O.full, O[("pos", L)])
                go(dve.tensor_copy(r_pos.rearrange("p a b -> p (a b)"), ps[:, 6, 0:80]))
                dve.sem_inc(O.free, 1)
                go(dve.tensor_copy(r_n, r_tmp[:, 0, :]))
                for t in range(1, TILES):
                    go(TT(r_pos[:, t, :], r_pos[:, t, :], r_n, ALU.add))
                    go(TT(r_n, r_n, r_tmp[:, t, :], ALU.add))
                go(TS(r_nov, r_n, float(CAP), None, ALU.is_gt))
                for k in range(1, TILES - 1):
                    go(STT(r_nov, r_n, float(CAP + k * P), r_nov, ALU.is_gt, ALU.add))
                less = cst["less"].rearrange("p (a b) -> p a b", a=NE)
                go(TT(r_pr, r_nov.unsqueeze(1).broadcast_to([P, NE, NE]), less, ALU.mult))
                go(dve.tensor_reduce(r_ovb, r_pr, AX.X, ALU.add))
                go(STT(r_dl, r_ovb, float(P), cst["ovshift"], ALU.mult, ALU.add))
                go(TS(r_ge5, r_pos, float(CAP), None, ALU.is_ge))
                go(TT(r_ge5, r_ge5, r_dl.unsqueeze(1).broadcast_to([P, TILES, NE]), ALU.mult))
                go(TT(r_pos, r_pos, cst["ebase"].unsqueeze(1).broadcast_to([P, TILES, NE]), ALU.add))
                go(TT(r_pos, r_pos, r_ge5, ALU.add))
                for j, c in enumerate((r_c1, r_c2)):
                    go(TT(r_tmp, r_pos, c, ALU.mult))
                    go(dve.tensor_reduce(r_s[:, j, :], r_tmp, AX.X, ALU.add))
                go(dve.tensor_copy(sidx[:, :], r_s.rearrange("p a b -> p (a b)")))
                go(dve.tensor_reduce(r_ctl[:, 0:1], r_nov, AX.X, ALU.add))
                go(TT(r_ovb, r_ovb, r_nov, ALU.add))
                go(TT(r_ind, r_ovb.unsqueeze(1).broadcast_to([P, NOVF, NE]),
                      cst["chunk"].unsqueeze(2).broadcast_to([P, NOVF, NE]), ALU.is_le))
                go(dve.tensor_reduce(r_ctl[:, 1:1 + NOVF], r_ind, AX.X, ALU.add))
                go(TS(r_ctl[:, 1:1 + NOVF], r_ctl[:, 1:1 + NOVF], float(NE - 1), None, ALU.min))
                dve.tensor_copy(ctl[:, 0:1 + NOVF], r_ctl[:, 0:1 + NOVF]).then_inc(idx_done, 1)
                meet(dve, "dve")
                n_ov = dve.value_load(ctl[0:1, 0:1], min_val=0, max_val=NOVF)
                E0 = NE * L

                def x_copy(e, b, early):
                    if not early:
                        dve.wait_ge(e_h, E0 + e - 1)
                    dve.wait_ge(e_xT, E0 + e + 1)
                    dve.tensor_copy(xgT[:, b, 512:1024], ps[:, 5, :]).then_inc(e_xTd, 1)

                def gate(e, b):
                    dve.wait_ge(e_sg, E0 + e + 1)
                    TT(hid[:, b, :], sg[:, b, :], ps[:, b, FF:2 * FF], ALU.mult).then_inc(e_hid, 1)

                def hid_copy(e, b, early):
                    dve.wait_ge(e_hT, E0 + e + 1)
                    if not early:
                        dve.wait_ge(e_d, E0 + e - 1)
                    dve.tensor_copy(hidT[:, b, :], ps[:, 6, 0:FF]).then_inc(e_hTe, 1)

                def y_copy(e, b, early):
                    dve.wait_ge(e_d, E0 + e + 1)
                    if not early:
                        dve.wait_ge(ys_out[b], 8 * E0 + 8 * (e - b))
                    dve.tensor_copy(yb[:, b, 512:1024], ps[:, 3, :]).then_inc(e_yd, 1)

                x_copy(0, 0, True)
                gate(0, 0)
                x_copy(1, 1, True)
                hid_copy(0, 0, True)
                gate(1, 1)
                x_copy(2, 0, False)
                y_copy(0, 0, True)
                hid_copy(1, 1, True)
                gate(2, 0)
                x_copy(3, 1, False)
                y_copy(1, 1, True)
                hid_copy(2, 0, False)
                with dve.Fori(3, NE - 1, 2) as e0:
                    for j in range(2):
                        e, b = e0 + j, 1 - j
                        gate(e, b)
                        x_copy(e + 1, 1 - b, False)
                        y_copy(e - 1, 1 - b, False)
                        hid_copy(e, b, False)
                gate(15, 1)
                y_copy(14, 0, False)
                hid_copy(15, 1, False)
                y_copy(15, 1, False)
                with dve.If(n_ov > 0):
                    with dve.Fori(0, NOVF) as c:
                        n = c + 1
                        dve.wait_ge(ov[L]["sg"], n)
                        TT(hid[:, 0, :], sg[:, 0, :], ps[:, 0, FF:2 * FF], ALU.mult).then_inc(ov[L]["hid"], 1)
                        dve.wait_ge(ov[L]["hT"], n)
                        dve.tensor_copy(hidT[:, 0, :], ps[:, 6, 0:FF]).then_inc(ov[L]["hTe"], 1)
                meet(dve, "dve")
                def final(i):
                    if i == 0:
                        dve.wait_ge(nrm_in, 16 * (2 * DEPTH + 1))
                    dve.wait_ge(fin_rs, i + 1)
                    STT(x7[:, i, :], x7[:, i, :], rsd[:, 24 + i:25 + i], nrm[:, :], ALU.mult,
                        ALU.mult).then_inc(fin_done, 1)

                for kind in (1, 0):
                    for half in range(2):
                        row_from(L, kind, 5, half, rowG2[:, kind, :])
                for lane in (O, M):
                    dve.wait_ge(lane.free, lane.freed[("bc", L, 0, 5, 0 if lane is O else 1)])
                if L < DEPTH - 1:
                    entry_rows(L + 1)
                for s in range(TILES + 1):
                    if s < TILES:
                        t = ORDER[s]
                        y = y2[:, s % 4, :]
                        dve.wait_ge(y1_scaled, TILES * L + s + 1)
                        dve.wait_ge(x7_in[s], 16 * (L + 2))
                        go(STT(y, y, wts[:, t, 1:2], y1[:, s, :], ALU.mult, ALU.add))
                        go(TT(y, y, rowG2[:, int(t == 4), :], ALU.mult))
                        TT(x7[:, s, :], x7[:, s, :], y, ALU.add).then_inc(comb_done, 1)
                    if s >= 1:
                        if L < DEPTH - 1:
                            entry(L + 1, s - 1)
                        else:
                            final(s - 1)
                meet(dve, "dve")


CONSTS = [("ident", P), ("flip", P), ("upper", P), ("m01", 64), ("madd", 64), ("swa", 7 * P),
          ("cos32", 128), ("sin32", 128), ("cos64", 256), ("sin64", 256), ("less", NE * NE), ("w4", 4),
          ("ebase", NE), ("ovshift", NE), ("chunk", NOVF)]


def constants():
    p = np.arange(P)
    col = p % GRID_W
    start = np.clip(col - 8, 0, GRID_W - 16)
    kc = np.arange(GRID_W)
    ok = (kc[None, :] >= start[:, None]) & (kc[None, :] < start[:, None] + 16)
    key, query = p[None, :], p[:, None]
    far, none = np.float32(-1e30), np.zeros((P, P), np.float32)
    before = np.where(key >= query, 0, far)
    after = np.where(key <= query, 0, far)
    c = {
        "ident": np.eye(P), "flip": np.eye(P)[::-1], "upper": query < key,
        "m01": ok, "madd": np.where(ok, 0, far),
        "swa": np.concatenate([before, none, after, none, before, none, none], 1),
        "less": np.broadcast_to((np.arange(NE)[None, :] < np.arange(NE)[:, None]).reshape(1, -1), (P, NE * NE)),
        "w4": np.broadcast_to(np.arange(4, 0, -1), (P, 4)),
        "ebase": np.broadcast_to(np.arange(NE) * P, (P, NE)),
        "ovshift": np.broadcast_to(NE * P - CAP - np.arange(NE) * P, (P, NE)),
        "chunk": np.broadcast_to(np.arange(NOVF), (P, NOVF)),
    }
    pos = np.arange(DEC)
    for dim in (32, 64):
        half = dim // 4
        freq = (10000.0 ** (-np.arange(half, dtype=np.float32) / half)).astype(np.float32)
        cs, sn = [], []
        for x in (pos // GRID_W, pos % GRID_W):
            ang = x.astype(np.float32)[:, None] * freq[None, :]
            cs += [np.cos(ang), np.cos(ang)]
            sn += [-np.sin(ang), np.sin(ang)]
        for n, parts in (("cos", cs), ("sin", sn)):
            full = np.concatenate(parts, 1).reshape(4, P, dim)
            c[n + str(dim)] = full.transpose(1, 0, 2).reshape(P, 4 * dim)
    return np.concatenate([np.asarray(c[n], np.float32).reshape(P, w) for n, w in CONSTS], 1)


def kernel(**inputs):
    import concourse.bacc as bacc
    from concourse.bass_utils import run_bass_kernel_spmd

    x = {k: np.ascontiguousarray(v) for k, v in inputs.items()}
    w = x["w_in"]
    swa_q = w[:, :, 416:672].reshape(DEPTH, D, 4, 64)[:, :, [0, 2, 1, 3]].reshape(DEPTH, D, 256)
    w_in = np.concatenate([w[:, :, 0:416], swa_q, w[:, :, 672:800], w[:, :, 928:1440], w[:, :, 800:928],
                           w[:, :, 1440:1696]], 2)
    w_ukv = x["w_ukv"].reshape(DEPTH, 128, MLA_H, 2, 64).transpose(0, 1, 3, 2, 4).reshape(DEPTH, 128, 1024)
    rpb = np.pad(x["na_rpb"], ((0, 0), (0, 0), (0, 0), (0, RPB_ROW - 31))).reshape(DEPTH * 4, 15 * RPB_ROW)
    flat = {
        "consts": constants(),
        "x0": np.concatenate([x["x_sample"][0], x["x_prompt"][0]], 0),
        "c": x["c"], "c_ctx": x["c_ctx"], "w_mod": x["w_mod"], "b_mod": x["b_mod"],
        "norm1": x["norm1"], "norm2": x["norm2"], "norm_final": x["norm_final"],
        "w_in": w_in, "g_qa": x["g_qa"], "w_uq": x["w_uq"], "g_kva": x["g_kva"], "w_ukv": w_ukv,
        "swa_sink": x["swa_sink"], "rpb": np.pad(rpb, ((0, 0), (P, 64))),
        "w_out": x["w_out"], "w_r": np.concatenate([x["w_router_grp"], x["w_router_exp"]], 2),
        "w_gate": x["w_gate"], "w_up": x["w_up"], "w_down": x["w_down"],
        "cache_mla_ckv": x["cache_mla_ckv"][0], "cache_mla_kpe": x["cache_mla_kpe"][0],
        "cache_swa_k": x["cache_swa_k"].reshape(DEPTH, P, 128), "cache_na_k": x["cache_na_k"].reshape(DEPTH, P, 256),
        "cache_v": np.concatenate([x["cache_swa_v"].reshape(DEPTH, P, 128), x["cache_na_v"].reshape(DEPTH, P, 256)], 2),
    }
    nc = bacc.Bacc("TRN2", target_bir_lowering=False, num_devices=1)
    arrays, t_in, t_out = {}, {}, {}
    for n, a in flat.items():
        arrays["in_" + n] = a = np.ascontiguousarray(a)
        t_in[n] = nc.dram_tensor("in_" + n, a.shape, mybir.dt.from_np(a.dtype), kind="ExternalInput").ap()
    outs = {"y_prompt": (SEQ, D), "y_sample": (DEC, D), "ckv": (DEPTH, SEQ, 128), "kpe": (DEPTH, SEQ, 32),
            "ks": (DEPTH, SEQ, 128), "vs": (DEPTH, SEQ, 128), "kn": (DEPTH, SEQ, 256), "vn": (DEPTH, SEQ, 256)}
    for n, shape in outs.items():
        t_out[n] = nc.dram_tensor("out_" + n, shape, F32, kind="ExternalOutput").ap()
    program(nc, t_in, t_out)
    r = run_bass_kernel_spmd(nc, [arrays], core_ids=[0]).results[0]
    shapes = {"y_prompt": (1, SEQ, D), "y_sample": (1, DEC, D), "ckv": (1, DEPTH, SEQ, 128), "kpe": (1, DEPTH, SEQ, 32),
              "ks": (1, DEPTH, SEQ, 2, 64), "vs": (1, DEPTH, SEQ, 2, 64), "kn": (1, DEPTH, SEQ, 4, 64),
              "vn": (1, DEPTH, SEQ, 4, 64)}
    return tuple(np.asarray(r["out_" + n]).reshape(shape) for n, shape in shapes.items())
```

```python
from contextlib import ExitStack

import numpy as np

import concourse.bass as bass
from concourse import mybir

F32 = mybir.dt.float32
BF16 = mybir.dt.bfloat16
I32 = mybir.dt.int32
ALU = mybir.AluOpType
ACT = mybir.ActivationFunctionType
AX = mybir.AxisListType

P = 128
D = 1024
KD = D // P
DEPTH = 2
SEQ = 128
DEC = 512
TILES = 5
KVT = 6
TOK = TILES * P
KEYS = KVT * P
GRID_W = 64
EPS = 1e-6
NE = 16
FF = 256
MLA_H, NOPE, ROPE, MV = 8, 64, 32, 64
QK = NOPE + ROPE
NOVF = 9
CAP = P
SLOTS = (NE + NOVF) * P
MLA_SCALE = float(QK) ** -0.5
HEAD_SCALE = 0.125
NEG = -3.0e38
NEXT_MOD = 1
PROJ = [8 * i + 10 for i in range(TILES)]
HO, OUT, NORM, H2, ROUTE = 0, 2, 5, 12, 14
ORDER = [4, 0, 1, 2, 3]
CHUNKS = [(0, 416), (416, 384), (800, 512), (1312, 384)]
C_CQ, C_CKV, C_KPE, C_QS, C_KS, C_QN, C_KN = 0, 256, 384, 416, 672, 800, 1056
PW = 1312
RPB_ROW, RPB_LEN = 64, 128 + 15 * 64 + 64


def norm_no(L, which, i):
    return TILES * (2 * L + (which - 1)) + i + 1


def ring_loads():
    out = [("mod", 0, 0)]
    for L in range(DEPTH):
        out += [("in", L), ("mod", L, 1), ("mod", L, 2)]
        out += [("mod", L + 1, 0)] if L < DEPTH - 1 else []
        out += [("out", L)]
    return out


def slot_no(i, key):
    loads = [k for k in ring_loads() if i >= 2 or k[0] != "out"]
    return 16 * (loads.index(key) + 1)


class Lane:

    def __init__(self, full, free):
        self.full, self.free = full, free
        self.number, self.freed, self.jobs, self.frees = {}, {}, 0, 0

    def take(self, pe, key, frees=1):
        if self.frees:
            pe.wait_ge(self.free, self.frees)
        self.jobs += 1
        self.frees += frees
        self.number[key] = self.jobs
        self.freed[key] = self.frees

    def __getitem__(self, key):
        return self.number[key]


def program(nc, t_in, t_out):
    with ExitStack() as ctx:
        def sb(name, shape, dt=F32):
            return ctx.enter_context(nc.sbuf_tensor(name, shape, dt))

        def sem(name):
            return ctx.enter_context(nc.semaphore(name))

        xbuf = nc.dram_tensor("x_rows", (TOK, D), F32).ap()
        mods = nc.dram_tensor("mods", (2, 6 * D), F32).ap()
        slots_x = nc.dram_tensor("slots_x", (SLOTS, D), F32).ap()
        slots_y = nc.dram_tensor("slots_y", (SLOTS, D), F32).ap()

        ring = sb("ring", [P, 4 * 8 * 512])
        slot = [ring[:, i * 4096:(i + 1) * 4096].rearrange("p (k n) -> p k n", k=8) for i in range(4)]
        big = sb("big", [P, 5120])
        hT = big[:, :].rearrange("p (k n) -> p k n", k=KD)
        heads = big[:, :].rearrange("p (t n) -> p t n", t=TILES)
        mrow = sb("mrow", [P, 3, 512])
        brow = sb("brow", [P, 3, 512])
        wuq = sb("wuq", [P, 2, 768])
        wukv = sb("wukv", [P, 1024])
        wr = sb("wr", [P, KD, 20])
        gqa = sb("gqa", [P, 256])
        gkva = sb("gkva", [P, 128])
        nrm = sb("nrm", [P, D])
        sink = sb("sink", [P, 4])
        sc = sb("sc", [P, KD, 32])
        cc = sb("cc", [P, 2, KD])
        consts = sb("consts", [P, sum(w for _, w in CONSTS)])
        cst, at = {}, 0
        for name, w in CONSTS:
            cst[name] = consts[:, at:at + w]
            at += w
        ident, flip, upper = (cst[n] for n in ("ident", "flip", "upper"))
        ones = cst["w4"][:, 3:4].broadcast_to([P, P])
        mhalf = sb("mhalf", [P, 8])
        zeros = sb("zeros", [P, 256])
        ssq = sb("ssq", [P, 32])
        rsd = sb("rsd", [P, 32])
        wts = sb("wts", [P, TILES, 2])
        sidx = sb("sidx", [P, 2 * TILES], I32)
        ctl = sb("ctl", [P, 16], I32)

        ARENA = 21184
        arena = sb("arena", [P, ARENA])

        def place(at, *dims):
            n = int(np.prod(dims))
            assert at + n <= ARENA, (at, dims)
            a = arena[:, at:at + n]
            if len(dims) == 2:
                a = a.rearrange("p (a b) -> p a b", a=dims[0])
            return a, at + n

        cqT, o = place(0, 2, TOK)
        ckvT, o = place(o, KEYS)
        kpeT, A0 = place(o, KEYS)
        v_loc, o = place(A0, KVT, 384)
        qsP, o = place(o, 4, TOK)
        qnP, o = place(o, 4, TOK)
        ksT, o = place(o, KEYS)
        knT, A1 = place(o, 2, KEYS)
        proj, o = place(A1, 2, PW)
        rt, o = place(o, 2, 384)
        ck, o = place(o, 544)
        junk1, o = place(o, 192)
        BRAW = ARENA - 4 * 960
        assert o <= BRAW
        braw, o = place(BRAW, 4, 960)
        bias, o = place(A1, 4, 960)
        sB, o = place(BRAW, 2, 640)
        pB2, o = place(o, 2, 640)
        pT2, o = place(o, 2, 640)
        qT, o = place(A0, 8, TOK)
        kT, o = place(o, 8, KEYS)
        v_mla, A3 = place(o, KVT, 512)
        qt, o = place(A3, 2, 768)
        rq, o = place(o, 2, 256)
        pB4, o = place(A3, 2, 640)
        pT4, o = place(o, 2, 640)
        hoT, o = place(o, D)
        junk4, o = place(o, 256)
        rowG1, o = place(0, 2, D)
        xh, o = place(o, 512)
        r_lg, o = place(o, TILES, 20)
        assert o <= A0
        rowA2 = ring[:, 6144:8192].rearrange("p (a b) -> p a b", a=2)
        rowB2 = [wukv[:, :], wuq[:, :, :].rearrange("p a b -> p (a b)")[:, 0:D]]
        R0 = A0
        WEIGHTS = ARENA - 2048 - 6144
        dn2, o = place(WEIGHTS, 2048)
        exp3, o = place(o, 6144)
        xg, o = place(0, 2, D)
        xgT, o = place(o, 2, D)
        sg, o = place(o, 2, FF)
        hid, o = place(o, 2, FF)
        hidT, o = place(o, 2, FF)
        yb, o = place(o, 2, D)
        P6_END = o
        gu_at = [ring[:, 0:4096], ring[:, 6144:10240], ring[:, 12288:16384], exp3[:, 0:4096]]
        dn_at = [ring[:, 4096:6144], ring[:, 10240:12288], dn2, exp3[:, 4096:6144]]
        w_gu = [a.rearrange("p (g k n) -> p g k n", g=2, k=KD) for a in gu_at]
        w_dn = [a.rearrange("p (k n) -> p k n", k=2) for a in dn_at]
        rowG2, o = place(0, 2, D)
        y1, o = place(o, TILES, D)
        junk7, o = place(o, 512)
        assert P6_END <= o
        x7, o = place(o, TILES, D)
        assert o <= WEIGHTS
        y2, o = place(WEIGHTS, 4, D)
        rowA, o = place(o, 2, D)
        rowB, o = place(o, 2, D)
        rt_at = [R0]

        def rtile(*dims):
            n = int(np.prod(dims))
            a = arena[:, rt_at[0]:rt_at[0] + n]
            rt_at[0] += n
            assert rt_at[0] <= WEIGHTS
            if len(dims) == 2:
                a = a.rearrange("p (a b) -> p a b", a=dims[0])
            if len(dims) == 3:
                a = a.rearrange("p (a b c) -> p a b c", a=dims[0], b=dims[1])
            return a

        r_g, r_d2, r_e2, r_m = (rtile(TILES) for _ in range(4))
        r_gd, r_ge, r_eq, r_oh, r_sel, r_oh1, r_oh2 = (rtile(TILES, 4) for _ in range(7))
        r_prod = rtile(TILES, 4, 4)
        r_T = rtile(TILES + 1, NE)
        r_slot, r_ge5 = (rtile(TILES, NE) for _ in range(2))
        r_c, r_pick = (rtile(2, TILES, NE) for _ in range(2))
        r_cmp = rtile(NE, 4)
        r_nov, r_ovb, r_dl = (rtile(NE) for _ in range(3))
        r_pr = rtile(NE, NE)
        r_ind = rtile(NOVF, NE)
        r_s = rtile(2, TILES)
        r_ctl = rtile(16)

        stat = {n: sb("st_" + n, [P, 8]) for n in ("mx", "m2", "nm", "sm", "es", "ri")}

        ps = ctx.enter_context(nc.psum_tensor("ps", [P, 8, 512], F32))

        def two(b, n=1024):
            return ps[:, b:b + 2, :].rearrange("p a b -> p (a b)")[:, 0:n]

        S = [Lane(sem(f"s{i}_full"), sem(f"s{i}_free")) for i in range(2)]
        T = Lane(sem("t_full"), sem("t_free"))
        O = Lane(sem("o_full"), sem("o_free"))
        M = Lane(sem("m_full"), sem("m_free"))
        met = sem("met")
        const_in, c_in, bmod_in, small_in, vec_in, nrm_in = (sem(n) for n in
                                                    ("const_in", "c_in", "bmod_in", "small_in", "vec_in", "nrm_in"))
        slot_in = [sem(f"slot{i}_in") for i in range(4)]
        mods_done = sem("mods_done")
        xh_in = sem("xh_in")
        cache_in, ctx_out, zero_out, zero_set = (sem(n) for n in ("cache_in", "ctx_out", "zero_out", "zero_set"))
        sc_set, half_set = sem("sc_set"), sem("half_set")
        sq_done, rs_done = sem("sq_done"), sem("rs_done")
        sq2_done, rs2_done = sem("sq2_done"), sem("rs2_done")
        hA_done, h_done = sem("hA_done"), sem("h_done")
        mods_out, rows_in = sem("mods_out"), sem("rows_in")
        post_done, pad_set = sem("post_done"), sem("pad_set")
        braw_in, bias_mul, bias_done = sem("braw_in"), sem("bias_mul"), sem("bias_done")
        nmax_done, q_done = sem("nmax_done"), sem("q_done")
        res_done, xs_out = sem("res_done"), sem("xs_out")
        rx1, rx1_done, rx2, rx2_done = (sem(n) for n in ("rx1", "rx1_done", "rx2", "rx2_done"))
        pick_done, idx_done, scat_out = (sem(n) for n in ("pick_done", "idx_done", "scat_out"))
        ew_in = [sem(f"ew{i}_in") for i in range(4)]
        xg_in = [sem(f"xg{i}_in") for i in range(2)]
        e_xT, e_xTa, e_xTd, e_h, e_sg, e_hid, e_hT, e_hTe, e_d, e_ya, e_yd = (sem("e_" + n) for n in (
            "xT", "xTa", "xTd", "h", "sg", "hid", "hT", "hTe", "d", "ya", "yd"))
        ys_out = [sem(f"ys{i}_out") for i in range(2)]
        ov = [{n: sem(f"ov{L}_{n}") for n in ("x", "w", "xT", "xTe", "h", "sg", "hid", "hT", "hTe", "d", "y", "out")}
              for L in range(DEPTH)]
        x7_in = [sem(f"x7{i}_in") for i in range(TILES)]
        y_in = [sem(f"y{i}_in") for i in range(TILES)]
        y1_scaled, comb_done, x7_out, fin_sq, fin_rs, fin_done = (sem(n) for n in (
            "y1_scaled", "comb_done", "x7_out", "fin_sq", "fin_rs", "fin_done"))
        step = {n: sem("step_" + n) for n in ("dve", "act", "pool")}
        steps = {n: 0 for n in step}

        def then(eng, who, ins):
            steps[who] += 1
            ins.then_inc(step[who], 1)
            eng.wait_ge(step[who], steps[who])

        meets = {}

        def meet(eng, who):
            meets[who] = meets.get(who, 0) + 1
            eng.drain().then_inc(met, 1)
            eng.wait_ge(met, 5 * meets[who])

        def row_bank(key):
            return (O, 6) if key in O.number else (M, 7)

        def unit_list(phase):
            out = []
            if phase == 2:
                for h in range(4):
                    for t in range(4):
                        lo, hi = max(t - 1, 0), min(t + 1, 3)
                        m0 = {0: 1, 1: 0, 2: 0, 3: 4}[t] * P
                        n = hi - lo + 2
                        out.append(dict(kind="swa", h=h, t=t, q=qsP[:, h, t * P:(t + 1) * P],
                                        k=[(0, ksT[:, lo * P:(hi + 1) * P]), ((n - 1) * P, ksT[:, 4 * P:5 * P])],
                                        n=n, mask=cst["swa"][:, m0:m0 + n * P],
                                        v=[v_loc[:, j, (h // 2) * 64:(h // 2) * 64 + 64] for j in [*range(lo, hi + 1), 4]],
                                        col=512 + h * 64))
                for h in range(4):
                    for t in range(4):
                        j0 = (7 - 2 * t) * 64
                        out.append(dict(kind="na", h=h, t=t, q=qnP[:, h, t * P:(t + 1) * P],
                                        k=[(0, knT[:, h // 2, 0:512]), (512, knT[:, h // 2, 512:640])],
                                        n=5, mask=bias[:, h, j0:j0 + 512],
                                        v=[v_loc[:, j, 128 + h * 64:192 + h * 64] for j in range(5)],
                                        col=768 + h * 64))
                for h in range(4):
                    out.append(dict(kind="swa_ctx", h=h, t=4, q=qsP[:, h, 512:640], k=[(0, ksT[:, 640:768])], n=1,
                                    v=[v_loc[:, 5, (h // 2) * 64:(h // 2) * 64 + 64]], col=512 + h * 64))
                for h in range(4):
                    out.append(dict(kind="ctx", h=h, t=4, q=qnP[:, h, 512:640], k=[(0, knT[:, h // 2, 640:768])],
                                    n=1, v=[v_loc[:, 5, 128 + h * 64:192 + h * 64]], col=768 + h * 64))
            else:
                for t in ORDER:
                    for h in range(MLA_H):
                        if t == 4:
                            out.append(dict(kind="ctx", h=h, t=4, q=qT[0:QK, h, 512:640], k=[(0, kT[0:QK, h, 640:768])],
                                            n=1, v=[v_mla[:, 5, h * 64:h * 64 + 64]], col=h * 64))
                            continue
                        out.append(dict(kind="mla", h=h, t=t, q=qT[0:QK, h, t * P:(t + 1) * P],
                                        k=[(0, kT[0:QK, h, 0:512]), (512, kT[0:QK, h, 512:640])], n=5,
                                        v=[v_mla[:, j, h * 64:h * 64 + 64] for j in range(5)], col=h * 64))
            return out

        UNITS = {2: unit_list(2), 4: unit_list(4)}
        UBASE = {2: 0, 4: len(UNITS[2])}
        UPL = len(UNITS[2]) + len(UNITS[4])
        STEPS = {2: len(UNITS[2]) + 2, 4: PROJ[-1] + ROUTE + 1}
        pB = {2: pB2, 4: pB4}
        pT = {2: pT2, 4: pT4}

        def split(n):
            return (1, 0) if n == 1 else ((n + 1) // 2, n // 2)

        block = ctx.enter_context(nc.Block())

        @block.tensor
        def _(pe):
            def transpose(out, in_):
                return pe.transpose(out, in_, ident)

            def mod_group(L, g):
                for i in range(4):
                    pe.wait_ge(slot_in[i], slot_no(i, ("mod", L, g)))
                M.take(pe, ("mod", L, g))
                for k in range(KD):
                    for i in range(4):
                        mm = pe.matmul(ps[32 * i:32 * i + 32, 7, :], sc[:, k, :], slot[i][:, k, :],
                                       start=(k == 0), stop=(k == KD - 1), tile_position=(0, 32 * i))
                mm.then_inc(M.full, 1)

            bcn = [0]

            def broadcast(L, kind, vec, half):
                n = 2 * vec + half
                lane, b = ((O, 6), (M, 7))[bcn[0] % 2]
                bcn[0] += 1
                pe.wait_ge(mods_done, 3 * L + n // 4 + 1)
                lane.take(pe, ("bc", L, kind, vec, half))
                row = 32 * (n % 4) + kind
                pe.matmul(ps[:, b, :], ident[:, row:row + 1].broadcast_to([P, P]), mrow[:, n // 4, :],
                          start=True, stop=True).then_inc(lane.full, 1)

            def attention(L, phase):
                units = UNITS[phase]
                base = UPL * L + UBASE[phase]

                def scores(u):
                    un = units[u]
                    S[u % 2].take(pe, ("s", L, phase, u))
                    if phase == 2 and un["kind"] == "na" and un["t"] == 0:
                        pe.wait_ge(bias_done, 4 * L + un["h"] + 1)
                    b = 2 * (u % 2)
                    for at, k in un["k"]:
                        w = k.shape[-1]
                        mm = pe.matmul(two(b)[:, at:at + w], un["q"], k, start=(at % 512 == 0), stop=True,
                                       skip_group_check=True)
                    mm.then_inc(S[u % 2].full, 1)

                def turn(u):
                    n = units[u]["n"]
                    a, d = split(n)
                    T.take(pe, ("p", L, phase, u), frees=2 if d else 1)
                    pe.wait_ge(S[u % 2].free, S[u % 2].freed[("s", L, phase, u)])
                    for j in range(n):
                        o = ps[:, 4, j * P:(j + 1) * P] if j < a else ps[:, 5, (j - a) * P:(j - a + 1) * P]
                        mm = transpose(o, pB[phase][:, u % 2, j * P:(j + 1) * P])
                    mm.then_inc(T.full, 1)

                def values(u):
                    un = units[u]
                    O.take(pe, ("o", L, phase, u))
                    pe.wait_ge(T.free, T.freed[("p", L, phase, u)])
                    for j in range(un["n"]):
                        mm = pe.matmul(ps[:, 6, 0:64], pT[phase][:, u % 2, j * P:(j + 1) * P], un["v"][j],
                                       start=(j == 0), stop=(j == un["n"] - 1))
                    mm.then_inc(O.full, 1)

                for s in range(STEPS[phase]):
                    if s < len(units):
                        scores(s)
                    if 2 <= s < len(units) + 2:
                        values(s - 2)
                    if phase == 2 and s in (16, 30):
                        mod_group(L, 1 if s == 16 else 2)
                    if 1 <= s <= len(units):
                        turn(s - 1)
                    if phase == 4:
                        beside(L, s)

            def beside(L, s):
                if s == NEXT_MOD and L < DEPTH - 1:
                    mod_group(L + 1, 0)
                for i in range(TILES):
                    t, n = ORDER[i], s - PROJ[i]
                    if n in (HO, HO + 1, H2, H2 + 1):
                        half, key = (n - HO, "ho") if n < H2 else (n - H2, "h2")
                        M.take(pe, (key, L, i, half))
                        if key == "ho":
                            last = 8 * i + MLA_H - 1
                            assert UNITS[4][last]["t"] == t
                            pe.wait_ge(O.free, O.freed[("o", L, 4, last)])
                        else:
                            pe.wait_ge(h_done, norm_no(L, 2, i))
                        for k in range(4):
                            mm = transpose(ps[:, 7, k * P:(k + 1) * P],
                                           heads[:, t, (4 * half + k) * P:(4 * half + k + 1) * P])
                        mm.then_inc(M.full, 1)
                    if n in (OUT, OUT + 1):
                        half = n - OUT
                        M.take(pe, ("out", L, i, half))
                        if i == 0:
                            pe.wait_ge(slot_in[2 + half], slot_no(2 + half, ("out", L)))
                        for k in range(KD):
                            mm = pe.matmul(ps[:, 7, :], hoT[:, k * P:(k + 1) * P], slot[2 + half][:, k, :],
                                           start=(k == 0), stop=(k == KD - 1))
                        mm.then_inc(M.full, 1)
                    if n == ROUTE:
                        M.take(pe, ("rt", L, i))
                        for k in range(KD):
                            mm = pe.matmul(ps[:, 7, 0:20], hoT[:, k * P:(k + 1) * P], wr[:, k, :],
                                           start=(k == 0), stop=(k == KD - 1))
                        mm.then_inc(M.full, 1)

            def entry(L):
                for kind in (1, 0):
                    for v in range(2):
                        for half in range(2):
                            broadcast(L, kind, v, half)
                for i in range(TILES):
                    T.take(pe, ("h", L, i))
                    pe.wait_ge(h_done, norm_no(L, 1, i))
                    for k in range(KD):
                        mm = transpose(ps[:, 4 + k // 4, (k % 4) * P:(k % 4 + 1) * P], y1[:, i, k * P:(k + 1) * P])
                    mm.then_inc(T.full, 1)

            pe.wait_ge(sc_set, 3)
            mod_group(0, 0)
            pe.wait_ge(const_in, 16)
            entry(0)
            meet(pe, "pe")
            for L in range(DEPTH):
                def turn_context():
                    T.take(pe, ("xp", L, 5), frees=2)
                    pe.wait_ge(cache_in, 80 * (L + 1))
                    transpose(ps[:, 4, 0:P], ck[:, 0:128])
                    transpose(ps[0:ROPE, 4, 384:512], ck[:, 128:160])
                    transpose(ps[:, 5, 0:P], ck[:, 160:288]).then_inc(T.full, 1)
                    O.take(pe, ("xn", L, 5))
                    transpose(ps[:, 6, 0:P], ck[:, 288:416])
                    transpose(ps[:, 6, P:2 * P], ck[:, 416:544]).then_inc(O.full, 1)

                def turn_proj(i):
                    q = proj[:, i % 2, :]
                    T.take(pe, ("xp", L, i), frees=2)
                    pe.wait_ge(post_done, TILES * L + i + 1)
                    for n, at in enumerate((C_CQ, C_CQ + P, C_CKV)):
                        transpose(ps[:, 4, n * P:(n + 1) * P], q[:, at:at + P])
                    transpose(ps[0:ROPE, 4, 384:512], q[:, C_KPE:C_KPE + ROPE])
                    for n, at in enumerate((C_QS, C_QS + P, C_KS)):
                        mm = transpose(ps[:, 5, n * P:(n + 1) * P], q[:, at:at + P])
                    mm.then_inc(T.full, 1)
                    O.take(pe, ("xn", L, i))
                    pe.wait_ge(S[1].free, S[1].freed[("in", L, i)])
                    for n, at in enumerate((C_QN, C_QN + P, C_KN, C_KN + P)):
                        mm = transpose(ps[:, 6, n * P:(n + 1) * P], q[:, at:at + P])
                    mm.then_inc(O.full, 1)

                for s in range(TILES + 1):
                    if s < TILES:
                        t = ORDER[s]
                        for half in range(2):
                            S[half].take(pe, ("in", L, s))
                            for c in (2 * half, 2 * half + 1):
                                if s == 0:
                                    pe.wait_ge(slot_in[c], slot_no(c, ("in", L)))
                                for k in range(KD):
                                    mm = pe.matmul(ps[:, c, 0:CHUNKS[c][1]], hT[:, k, t * P:(t + 1) * P],
                                                   slot[c][:, k, 0:CHUNKS[c][1]], start=(k == 0), stop=(k == KD - 1))
                            mm.then_inc(S[half].full, 1)
                    if s == 1:
                        turn_context()
                    if s >= 1:
                        turn_proj(s - 1)
                meet(pe, "pe")

                for h in range(4):
                    S[h % 2].take(pe, ("bias", L, h))
                    pe.wait_ge(braw_in, 16 * (L + 1))
                    for n in range(2):
                        mm = pe.matmul(ps[:, 2 * (h % 2) + n, 0:480], flip, braw[:, h, n * 480:(n + 1) * 480],
                                       start=True, stop=True)
                    mm.then_inc(S[h % 2].full, 1)
                attention(L, 2)
                meet(pe, "pe")

                def uq(i):
                    t = ORDER[i]
                    T.take(pe, ("uq", L, i))
                    for n, w in ((0, 512), (512, 256)):
                        for k in range(2):
                            mm = pe.matmul(ps[:, 4 + n // 512, 0:w], cqT[:, k, t * P:(t + 1) * P], wuq[:, k, n:n + w],
                                           start=(k == 0), stop=(k == 1))
                    mm.then_inc(T.full, 1)

                def qturn(i):
                    S[i % 2].take(pe, ("qt", L, i))
                    pe.wait_ge(q_done, TILES * L + i + 1)
                    for h in range(MLA_H):
                        b = 2 * (i % 2) + h // 4
                        mm = transpose(ps[0:QK, b, (h % 4) * P:(h % 4 + 1) * P], qt[:, i % 2, h * QK:(h + 1) * QK])
                    mm.then_inc(S[i % 2].full, 1)

                for i in range(TILES + 1):
                    if i < TILES:
                        uq(i)
                    if i < 4:
                        S[i % 2].take(pe, ("uk", L, i))
                        for n, w in ((0, 512), (512, 256)):
                            mm = pe.matmul(ps[:, 2 * (i % 2) + n // 512, 0:w], wukv[:, i * P:(i + 1) * P],
                                           ckvT[:, n:n + w], start=True, stop=True)
                        mm.then_inc(S[i % 2].full, 1)
                    lane, b = ((O, 6), (M, 7))[i % 2]
                    lane.take(pe, ("uv", L, i))
                    pe.matmul(ps[:, b, :], ckvT[:, i * P:(i + 1) * P], wukv[:, 512:1024],
                              start=True, stop=True).then_inc(lane.full, 1)
                    if i >= 1:
                        qturn(i - 1)
                meet(pe, "pe")

                attention(L, 4)
                meet(pe, "pe")

                O.take(pe, ("pos", L))
                pe.wait_ge(pick_done, L + 1)
                pe.matmul(ps[:, 6, 0:96], upper, r_T.rearrange("p a b -> p (a b)"), start=True, stop=False,
                          skip_group_check=True)
                for t in range(TILES):
                    mm = pe.matmul(ps[:, 6, (t + 1) * NE:96].rearrange("p (a b) -> p a b", b=NE), ones,
                                   r_T[:, t:t + 1, :].broadcast_to([P, TILES - t, NE]), start=False,
                                   stop=(t == TILES - 1), skip_group_check=True)
                mm.then_inc(O.full, 1)
                meet(pe, "pe")

                n_ov = pe.value_load(ctl[0:1, 0:1], min_val=0, max_val=NOVF)
                E0 = NE * L

                def x_turn(e, b, first):
                    if not first:
                        pe.wait_ge(e_xTa, E0 + e)
                        pe.wait_ge(e_xTd, E0 + e)
                    pe.wait_ge(xg_in[b], 16 * (E0 // 2) + (e - b) * 8 + 16)
                    for k in range(KD):
                        mm = transpose(ps[:, 4 + k // 4, (k % 4) * P:(k % 4 + 1) * P], xg[:, b, k:D:KD])
                    mm.then_inc(e_xT, 1)

                def up(e, q, early):
                    b = q % 2
                    pe.wait_ge(ew_in[q], 12 * E0 + (e - q) * 12 + 48)
                    pe.wait_ge(e_xTa, E0 + e + 1)
                    pe.wait_ge(e_xTd, E0 + e + 1)
                    if not early:
                        pe.wait_ge(e_hid, E0 + e - 1)
                    for k in range(KD):
                        mm = pe.matmul(ps[:, b, :], xgT[:, b, k * P:(k + 1) * P], w_gu[q][:, :, k, :],
                                       start=(k == 0), stop=(k == KD - 1))
                    mm.then_inc(e_h, 1)

                def h_turn(e, b, first):
                    if not first:
                        pe.wait_ge(e_hTe, E0 + e)
                    pe.wait_ge(e_hid, E0 + e + 1)
                    for k in range(2):
                        mm = transpose(ps[:, 6, k * P:(k + 1) * P], hid[:, b, k:FF:2])
                    mm.then_inc(e_hT, 1)

                def down(e, q, first):
                    b = q % 2
                    pe.wait_ge(e_hTe, E0 + e + 1)
                    if not first:
                        pe.wait_ge(e_ya, E0 + e)
                        pe.wait_ge(e_yd, E0 + e)
                    for n in range(2):
                        for k in range(2):
                            mm = pe.matmul(ps[:, 2 + n, :], hidT[:, b, k * P:(k + 1) * P],
                                           w_dn[q][:, k, n * 512:(n + 1) * 512], start=(k == 0), stop=(k == 1))
                    mm.then_inc(e_d, 1)

                x_turn(0, 0, True)
                up(0, 0, True)
                x_turn(1, 1, False)
                h_turn(0, 0, True)
                up(1, 1, True)
                x_turn(2, 0, False)
                down(0, 0, True)
                h_turn(1, 1, False)
                with pe.Fori(2, NE - 2, 4) as e0:
                    for j in range(4):
                        e, q = e0 + j, (2 + j) % 4
                        up(e, q, False)
                        x_turn(e + 1, 1 - j % 2, False)
                        down(e - 1, (q - 1) % 4, False)
                        h_turn(e, j % 2, False)
                up(14, 2, False)
                x_turn(15, 1, False)
                down(13, 1, False)
                h_turn(14, 0, False)
                up(15, 3, False)
                down(14, 2, False)
                h_turn(15, 1, False)
                down(15, 3, False)
                pe.wait_ge(e_ya, E0 + NE)
                pe.wait_ge(e_yd, E0 + NE)
                with pe.If(n_ov > 0):
                    with pe.Fori(0, NOVF) as c:
                        n = c + 1
                        pe.wait_ge(ov[L]["x"], n * 16)
                        for k in range(KD):
                            mm = transpose(ps[:, 4 + k // 4, (k % 4) * P:(k % 4 + 1) * P], xg[:, 0, k:D:KD])
                        mm.then_inc(ov[L]["xT"], 1)
                        pe.wait_ge(ov[L]["w"], n * 48)
                        pe.wait_ge(ov[L]["xTe"], n)
                        for k in range(KD):
                            mm = pe.matmul(ps[:, 0, :], xgT[:, 0, k * P:(k + 1) * P], w_gu[3][:, :, k, :],
                                           start=(k == 0), stop=(k == KD - 1))
                        mm.then_inc(ov[L]["h"], 1)
                        pe.wait_ge(ov[L]["hid"], n)
                        for k in range(2):
                            mm = transpose(ps[:, 6, k * P:(k + 1) * P], hid[:, 0, k:FF:2])
                        mm.then_inc(ov[L]["hT"], 1)
                        pe.wait_ge(ov[L]["hTe"], n)
                        for h in range(2):
                            for k in range(2):
                                mm = pe.matmul(ps[:, 2 + h, :], hidT[:, 0, k * P:(k + 1) * P],
                                               w_dn[3][:, k, h * 512:(h + 1) * 512], start=(k == 0), stop=(k == 1))
                        mm.then_inc(ov[L]["d"], 1)
                meet(pe, "pe")

                for kind in (1, 0):
                    for half in range(2):
                        broadcast(L, kind, 5, half)
                if L < DEPTH - 1:
                    entry(L + 1)
                meet(pe, "pe")

        @block.sync
        def _(sp):
            sp.dma_start(cc[:, 0, :], t_in["c"].rearrange("a (p k) -> (a p) k", k=KD)).then_inc(c_in, 16)
            sp.dma_start(cc[:, 1, :], t_in["c_ctx"].rearrange("(p k) -> p k", k=KD)).then_inc(c_in, 16)

            def mod_load(L, g):
                w_mod = t_in["w_mod"][L].rearrange("(p k) n -> p k n", k=KD)
                for i in range(4):
                    n = 4 * g + i
                    sp.dma_start(slot[i], w_mod[:, :, n * 512:(n + 1) * 512]).then_inc(slot_in[i], 16)

            def small_loads(L):
                sp.dma_start(wuq[:, :, :], t_in["w_uq"][L].rearrange("(k p) n -> p k n", p=P)).then_inc(small_in, 16)
                sp.dma_start(wukv[:, :], t_in["w_ukv"][L]).then_inc(small_in, 16)
                sp.dma_start(wr[:, :, :], t_in["w_r"][L].rearrange("(k p) n -> p k n", p=P)).then_inc(small_in, 16)

            def in_load(L, c):
                at, w = CHUNKS[c]
                w_in = t_in["w_in"][L].rearrange("(k p) n -> p k n", p=P)
                sp.dma_start(slot[c][:, :, 0:w], w_in[:, :, at:at + w]).then_inc(slot_in[c], 16)

            def x_loads(src):
                for i in range(TILES):
                    t = ORDER[i]
                    sp.dma_start(x7[:, i, :], src[t * P:(t + 1) * P, :]).then_inc(x7_in[i], 16)

            mod_load(0, 0)
            sp.dma_start(consts[:, :], t_in["consts"]).then_inc(const_in, 16)
            x_loads(t_in["x0"])
            small_loads(0)
            sp.wait_ge(M.full, M[("mod", 0, 0)])
            for c in range(4):
                in_load(0, c)
            meet(sp, "sp")
            for L in range(DEPTH):
                w_out = t_in["w_out"][L].rearrange("(k p) n -> p k n", p=P)
                src = bass.AP(tensor=t_in["rpb"].tensor, offset=L * 4 * RPB_LEN + 16, ap=[[1, P], [RPB_LEN, 4], [1, 960]])
                sp.dma_start(braw, src).then_inc(braw_in, 16)
                sp.wait_ge(post_done, TILES * L + 1)
                sp.wait_ge(S[1].free, S[1].freed[("in", L, 0)])
                for name, src_ap in (("ckv", proj[:, 0, C_CKV:C_CKV + 128]), ("kpe", proj[:, 0, C_KPE:C_KPE + 32]),
                                     ("ks", proj[:, 0, C_KS:C_KS + 128]), ("kn", proj[:, 0, C_KN:C_KN + 256]),
                                     ("vs", v_loc[:, 5, 0:128]), ("vn", v_loc[:, 5, 128:384])):
                    sp.dma_start(t_out[name][L], src_ap).then_inc(ctx_out, 16)
                for half in range(2):
                    sp.wait_ge(S[half].full, S[half][("in", L, TILES - 1)])
                mod_load(L, 1)
                sp.wait_ge(ctx_out, 96 * (L + 1))
                meet(sp, "sp")
                sp.wait_ge(M.full, M[("mod", L, 1)])
                mod_load(L, 2)
                sp.wait_ge(M.full, M[("mod", L, 2)])
                sp.wait_ge(mods_done, 3 * L + 3)
                for kind in range(2):
                    sp.dma_start(mods[kind, 2 * D:6 * D].rearrange("(g i n) -> i g n", g=2, i=4),
                                 mrow[kind:kind + 97:32, 1:3, :]).then_inc(mods_out, 16)
                if L < DEPTH - 1:
                    mod_load(L + 1, 0)

                def half_up_load(e, q, n):
                    w = ("w_gate", "w_up")[n]
                    sp.dma_start(w_gu[q][:, n], t_in[w][L][e].rearrange("(p k) n -> p k n", k=KD)).then_inc(ew_in[q], 16)

                def up_load(e, q):
                    for n in range(2):
                        half_up_load(e, q, n)

                def down_load(e, q):
                    sp.dma_start(w_dn[q], t_in["w_down"][L][e].rearrange("(p k) n -> p k n", k=2)).then_inc(ew_in[q], 16)

                def out_load():
                    for n in range(2):
                        sp.dma_start(slot[2 + n], w_out[:, :, n * 512:(n + 1) * 512]).then_inc(slot_in[2 + n], 16)
                    up_load(0, 0)
                    down_load(0, 0)

                if L == DEPTH - 1:
                    out_load()
                sp.wait_ge(mods_out, 32 * (L + 1))
                meet(sp, "sp")
                meet(sp, "sp")
                def row_load(dst, vec, kind):
                    sp.dma_start(dst, mods[kind:kind + 1, vec * D:(vec + 1) * D].broadcast_to([P, D])).then_inc(rows_in, 16)

                for kind in (1, 0):
                    row_load(rowG1[:, kind, :], 2, kind)
                    row_load(rowB2[kind], 3, kind)
                if L < DEPTH - 1:
                    sp.wait_ge(M.full, M[("mod", L + 1, 0)])
                    out_load()
                for kind in (1, 0):
                    row_load(rowA2[:, kind, :], 4, kind)
                src = t_in["x0"] if L == 0 else xbuf
                for i in range(TILES):
                    t = ORDER[i]
                    for half in range(2):
                        n = 2 * (TILES * L + i) + half
                        if i or half:
                            sp.wait_ge(res_done, n)
                        sp.dma_start(xh, src[t * P:(t + 1) * P, half * 512:(half + 1) * 512]).then_inc(xh_in, 16)
                    sp.wait_ge(res_done, 2 * (TILES * L + i + 1))
                    sp.dma_start(xbuf[t * P:(t + 1) * P, :], heads[:, t, :]).then_inc(xs_out, 16)
                meet(sp, "sp")
                up_load(1, 1)
                down_load(1, 1)
                half_up_load(2, 2, 0)
                meet(sp, "sp")
                n_ov = sp.value_load(ctl[0:1, 0:1], min_val=0, max_val=NOVF)
                E0 = NE * L
                for e in range(2):
                    sp.dma_start(xg[:, e, :], slots_x[e * P:(e + 1) * P, :]).then_inc(xg_in[e], 16)
                half_up_load(2, 2, 1)
                down_load(2, 2)
                up_load(3, 3)
                down_load(3, 3)
                for e in range(2, 4):
                    sp.wait_ge(e_xT, E0 + e - 1)
                    sp.dma_start(xg[:, e % 2, :], slots_x[e * P:(e + 1) * P, :]).then_inc(xg_in[e % 2], 16)
                with sp.Fori(1, NE // 4) as quad:
                    for q in range(4):
                        j = q % 2
                        e = sp.snap(quad * 4 + q)
                        row = sp.snap(quad * (4 * P) + q * P)
                        sp.wait_ge(e_xT, E0 + e - 1)
                        sp.dma_start(xg[:, j, :], slots_x[bass.ds(row, P), :]).then_inc(xg_in[j], 16)
                        sp.wait_ge(e_d, E0 + e - 3)
                        for n, w in enumerate(("w_gate", "w_up")):
                            sp.dma_start(w_gu[q][:, n], t_in[w][L][bass.ds(e, 1)].rearrange(
                                "o (p k) n -> (o p) k n", k=KD)).then_inc(ew_in[q], 16)
                        sp.dma_start(w_dn[q], t_in["w_down"][L][bass.ds(e, 1)].rearrange(
                            "o (p k) n -> (o p) k n", k=2)).then_inc(ew_in[q], 16)
                x_loads(xbuf)
                if L < DEPTH - 1:
                    small_loads(L + 1)
                    sp.wait_ge(e_d, E0 + 13)
                    in_load(L + 1, 0)
                with sp.If(n_ov > 0):
                    sp.wait_ge(e_d, E0 + NE)
                    for c in range(NOVF):
                        e = sp.value_load(ctl[0:1, 1 + c:2 + c], min_val=0, max_val=NE - 1)
                        if c:
                            sp.wait_ge(ov[L]["out"], 16 * c)
                        row = (NE + c) * P
                        sp.dma_start(xg[:, 0, :], slots_x[row:row + P, :]).then_inc(ov[L]["x"], 16)
                        for n, w in enumerate(("w_gate", "w_up")):
                            sp.dma_start(w_gu[3][:, n], t_in[w][L][bass.ds(e, 1)].rearrange(
                                "o (p k) n -> (o p) k n", k=KD)).then_inc(ov[L]["w"], 16)
                        sp.dma_start(w_dn[3], t_in["w_down"][L][bass.ds(e, 1)].rearrange(
                            "o (p k) n -> (o p) k n", k=2)).then_inc(ov[L]["w"], 16)
                meet(sp, "sp")
                if L < DEPTH - 1:
                    sp.wait_ge(y_in[TILES - 1], 32 * (L + 1))
                    for c in range(1, 4):
                        in_load(L + 1, c)
                meet(sp, "sp")

        @block.scalar
        def _(act):
            def attention(L, phase):
                units = UNITS[phase]
                base = UPL * L + UBASE[phase]

                def exps(u):
                    un, w = units[u], units[u]["n"] * P
                    act.wait_ge(nmax_done, base + u + 1)
                    if u >= 2:
                        act.wait_ge(T.full, T[("p", L, phase, u - 2)])
                    if un["kind"].startswith("swa"):
                        act.activation(stat["es"][:, u % 8:u % 8 + 1], sink[:, un["h"]:un["h"] + 1], ACT.Exp,
                                       bias=stat["nm"][:, u % 8:u % 8 + 1], scale=1.0)
                    src = sB[:, u % 2, 0:w] if "mask" in un else two(2 * (u % 2), w)
                    act.activation(pB[phase][:, u % 2, 0:w], src, ACT.Exp, bias=stat["nm"][:, u % 8:u % 8 + 1],
                                   scale=1.0, accum_out=stat["sm"][:, u % 8:u % 8 + 1]).then_inc(S[u % 2].free, 1)

                def copy(u):
                    a, d = split(units[u]["n"])
                    if d:
                        act.wait_ge(T.full, T[("p", L, phase, u)])
                        if u >= 2:
                            act.wait_ge(O.full, O[("o", L, phase, u - 2)])
                        act.activation(pT[phase][:, u % 2, a * P:(a + d) * P], ps[:, 5, 0:d * P],
                                       ACT.Copy).then_inc(T.free, 1)

                for s in range(STEPS[phase]):
                    if s < len(units):
                        exps(s)
                    if 1 <= s <= len(units):
                        copy(s - 1)
                    if phase == 4:
                        beside(L, s)

            def beside(L, s):
                for i in range(TILES):
                    n = s - PROJ[i]
                    if n in (HO, HO + 1, H2, H2 + 1):
                        key = ("ho", L, i, n - HO) if n < H2 else ("h2", L, i, n - H2)
                        act.wait_ge(M.full, M[key])
                        act.activation(hoT[:, key[3] * 512:(key[3] + 1) * 512], ps[:, 7, :],
                                       ACT.Copy).then_inc(M.free, 1)
                    if n in (OUT + 1, OUT + 2):
                        half = n - OUT - 1
                        at = 18 * half + i
                        act.wait_ge(res_done, 2 * (TILES * L + i) + half + 1)
                        then(act, "act", act.activation(junk4.bitcast(BF16)[:, 0:512],
                                                        heads[:, ORDER[i], half * 512:(half + 1) * 512], ACT.Square,
                                                        accum_out=ssq[:, at:at + 1]))
                        if half:
                            act.sem_inc(sq_done, 1)

            act.wait_ge(c_in, 32)
            act.wait_ge(zero_set, 2)
            act.activation(sc[:, :, 0:1], cc[:, 0, :].unsqueeze(2), ACT.Silu).then_inc(sc_set, 1)
            act.activation(sc[:, :, 1:2], cc[:, 1, :].unsqueeze(2), ACT.Silu).then_inc(sc_set, 1)
            j7 = junk7.bitcast(BF16)

            def square(L, i):
                if L == 0:
                    act.wait_ge(x7_in[i], 16)
                else:
                    act.wait_ge(comb_done, TILES * (L - 1) + i + 1)
                if i:
                    act.wait_ge(sq_done, norm_no(L, 1, i - 1))
                act.activation(j7, x7[:, i, :], ACT.Square, accum_out=ssq[:, i:i + 1]).then_inc(sq_done, 1)

            def h_copy(L, i):
                act.wait_ge(T.full, T[("h", L, i)])
                t = ORDER[i]
                for n in range(2):
                    cp = act.activation(hT[:, 4 * n:4 * n + 4, t * P:(t + 1) * P],
                                        ps[:, 4 + n, :].rearrange("p (k n) -> p k n", k=4), ACT.Copy)
                cp.then_inc(T.free, 1)

            for i in range(TILES):
                square(0, i)
            for i in range(TILES):
                h_copy(0, i)
            meet(act, "act")
            junk = junk1.bitcast(BF16)
            for L in range(DEPTH):
                for s in range(TILES + 1):
                    if L == 0:
                        for rows, a, b in ((slots_x, 5 * s, min(5 * s + 5, NE + NOVF)),
                                           (slots_y, NE + 2 * s, min(NE + 2 * s + 2, NE + NOVF))):
                            if a < b:
                                act.dma_start(rows[a * P:b * P, :].rearrange("(p c) (a n) -> p (c a) n", p=P, n=256),
                                              zeros[:, :].unsqueeze(1).broadcast_to([P, (b - a) * 4, 256])
                                              ).then_inc(zero_out, 16)
                    if s < TILES:
                        i = s
                        kv = 5 if ORDER[i] == 4 else ORDER[i]
                        act.wait_ge(S[1].full, S[1][("in", L, i)])
                        if i >= 2:
                            act.wait_ge(O.full, O[("xn", L, i - 2)])
                            if i == 2:
                                act.wait_ge(ctx_out, 96 * (L + 1))
                        act.activation(proj[:, i % 2, C_QN:C_QN + 512], ps[:, 2, :], ACT.Copy)
                        act.activation(v_loc[:, kv, :], ps[:, 3, 0:384], ACT.Copy).then_inc(S[1].free, 1)
                        act.wait_ge(S[0].free, S[0].freed[("in", L, i)])
                        if i:
                            act.wait_ge(sq2_done, TILES * L + i)
                        act.activation(junk[:, 0:256], proj[:, i % 2, 0:256], ACT.Square,
                                       accum_out=ssq[:, 8 + 2 * i:9 + 2 * i])
                        act.activation(junk[:, 256:384], proj[:, i % 2, C_CKV:C_CKV + 128], ACT.Square,
                                       accum_out=ssq[:, 9 + 2 * i:10 + 2 * i]).then_inc(sq2_done, 1)
                    if s >= 1:
                        for i in ([5, 0] if s == 1 else [s - 1]):
                            kv = 4 if i == 5 else (5 if ORDER[i] == 4 else ORDER[i])
                            k0 = kv * P
                            act.wait_ge(T.full, T[("xp", L, i)])
                            if i < 5:
                                t0 = ORDER[i] * P
                                act.activation(cqT[:, :, t0:t0 + P], ps[:, 4, 0:256].rearrange("p (k n) -> p k n", k=2), ACT.Copy)
                                act.activation(ckvT[:, k0:k0 + P], ps[:, 4, 256:384], ACT.Copy)
                            else:
                                act.activation(ckvT[:, k0:k0 + P], ps[:, 4, 0:P], ACT.Copy)
                            act.activation(kpeT[0:ROPE, k0:k0 + P], ps[0:ROPE, 4, 384:512], ACT.Copy).then_inc(T.free, 1)
                            act.wait_ge(O.full, O[("xn", L, i)])
                            kn = ps[:, 6, 256:512] if i < 5 else ps[:, 6, 0:256]
                            if i < 5:
                                act.wait_ge(pad_set, 2 * L + 2)
                                act.activation(qnP[0:64, 0:4:2, t0:t0 + P],
                                               ps[0:64, 6, 0:256].rearrange("p (k n) -> p k n", k=2), ACT.Copy, scale=HEAD_SCALE)
                                act.activation(qnP[64:128, 1:4:2, t0:t0 + P],
                                               ps[64:128, 6, 0:256].rearrange("p (k n) -> p k n", k=2), ACT.Copy, scale=HEAD_SCALE)
                            act.activation(knT[:, :, k0:k0 + P], kn.rearrange("p (k n) -> p k n", k=2),
                                           ACT.Copy).then_inc(O.free, 1)
                meet(act, "act")
                attention(L, 2)
                meet(act, "act")
                for i in range(TILES + 1):
                    if i < TILES:
                        act.wait_ge(T.full, T[("uq", L, i)])
                        if i >= 2:
                            act.wait_ge(S[i % 2].full, S[i % 2][("qt", L, i - 2)])
                        act.activation(qt[:, i % 2, :], two(4, 768), ACT.Copy, scale=MLA_SCALE).then_inc(T.free, 1)
                    if i in (1, 3):
                        act.wait_ge(S[1].full, S[1][("uk", L, i)])
                        act.activation(kT[0:64, 2 * i, :], two(2, 768)[0:64], ACT.Copy)
                        act.activation(kT[0:64, 2 * i + 1, :], two(2, 768)[64:128], ACT.Copy).then_inc(S[1].free, 1)
                    if i % 2 == 0:
                        act.wait_ge(O.full, O[("uv", L, i)])
                        act.activation(v_mla[:, i, :], ps[:, 6, :], ACT.Copy).then_inc(O.free, 1)
                    if i >= 1 and (i - 1) % 2 == 0:
                        t0 = ORDER[i - 1] * P
                        act.wait_ge(S[0].full, S[0][("qt", L, i - 1)])
                        act.activation(qT[0:QK, :, t0:t0 + P], two(0)[0:QK].rearrange("p (h n) -> p h n", h=8),
                                       ACT.Copy).then_inc(S[0].free, 1)
                meet(act, "act")
                attention(L, 4)
                meet(act, "act")
                act.wait_ge(rx1, L + 1)
                act.activation(r_ge, r_gd, ACT.Exp).then_inc(rx1_done, 1)
                act.wait_ge(rx2, L + 1)
                act.activation(r_e2, r_d2, ACT.Exp).then_inc(rx2_done, 1)
                meet(act, "act")
                n_ov = act.value_load(ctl[0:1, 0:1], min_val=0, max_val=NOVF)
                E0 = NE * L

                def x_copy(e, b, early):
                    if not early:
                        act.wait_ge(e_h, E0 + e - 1)
                    act.wait_ge(e_xT, E0 + e + 1)
                    act.activation(xgT[:, b, 0:512], ps[:, 4, :], ACT.Copy).then_inc(e_xTa, 1)

                def silu(e, b):
                    act.wait_ge(e_h, E0 + e + 1)
                    act.activation(sg[:, b, :], ps[:, b, 0:FF], ACT.Silu).then_inc(e_sg, 1)

                def y_copy(e, b, early):
                    act.wait_ge(e_d, E0 + e + 1)
                    if not early:
                        act.wait_ge(ys_out[b], 16 * (E0 // 2) + (e - b) * 8)
                    act.activation(yb[:, b, 0:512], ps[:, 2, :], ACT.Copy).then_inc(e_ya, 1)

                x_copy(0, 0, True)
                silu(0, 0)
                x_copy(1, 1, True)
                silu(1, 1)
                x_copy(2, 0, False)
                y_copy(0, 0, True)
                silu(2, 0)
                x_copy(3, 1, False)
                y_copy(1, 1, True)
                with act.Fori(3, NE - 1, 2) as e0:
                    for j in range(2):
                        e, b = e0 + j, 1 - j
                        silu(e, b)
                        x_copy(e + 1, 1 - b, False)
                        y_copy(e - 1, 1 - b, False)
                silu(15, 1)
                y_copy(14, 0, False)
                y_copy(15, 1, False)
                with act.If(n_ov > 0):
                    act.wait_ge(ys_out[0], 8 * (E0 + NE))
                    with act.Fori(0, NOVF) as c:
                        n = c + 1
                        act.wait_ge(ov[L]["xT"], n)
                        act.activation(xgT[:, 0, 0:512], ps[:, 4, :], ACT.Copy)
                        act.activation(xgT[:, 0, 512:1024], ps[:, 5, :], ACT.Copy).then_inc(ov[L]["xTe"], 1)
                        act.wait_ge(ov[L]["h"], n)
                        act.activation(sg[:, 0, :], ps[:, 0, 0:FF], ACT.Silu).then_inc(ov[L]["sg"], 1)
                        act.wait_ge(ov[L]["d"], n)
                        act.activation(yb[:, 0, :], two(2), ACT.Copy).then_inc(ov[L]["y"], 1)
                meet(act, "act")
                for kind in (1, 0):
                    for half in range(2):
                        lane, b = row_bank(("bc", L, kind, 5, half))
                        act.wait_ge(lane.full, lane[("bc", L, kind, 5, half)])
                        act.activation(rowG2[:, kind, half * 512:(half + 1) * 512], ps[:, b, :],
                                       ACT.Copy).then_inc(lane.free, 1)

                def y1_scale(i):
                    act.wait_ge(y_in[i], 32 * (L + 1))
                    act.activation(y1[:, i, :], y1[:, i, :], ACT.Copy,
                                   scale=wts[:, ORDER[i], 0:1]).then_inc(y1_scaled, 1)

                if L < DEPTH - 1:
                    y1_scale(0)
                    y1_scale(1)
                    for s in range(TILES + 2):
                        if s + 2 < TILES:
                            y1_scale(s + 2)
                        if 1 <= s <= TILES:
                            square(L + 1, s - 1)
                            t = ORDER[s - 1]
                            act.dma_start(xbuf[t * P:(t + 1) * P, :], x7[:, s - 1, :]).then_inc(x7_out, 16)
                        if s >= 2:
                            h_copy(L + 1, s - 2)
                else:
                    for s in range(TILES + 2):
                        if s < TILES:
                            y1_scale(s)
                        if 1 <= s <= TILES:
                            i = s - 1
                            act.wait_ge(comb_done, TILES * L + i + 1)
                            if i:
                                act.wait_ge(fin_sq, i)
                            act.activation(j7, x7[:, i, :], ACT.Square,
                                           accum_out=ssq[:, 24 + i:25 + i]).then_inc(fin_sq, 1)
                        if s >= 2:
                            t = ORDER[s - 2]
                            act.wait_ge(fin_done, s - 1)
                            dst = t_out["y_prompt"] if t == 4 else t_out["y_sample"][t * P:(t + 1) * P, :]
                            act.dma_start(dst, x7[:, s - 2, :]).then_inc(x7_out, 16)
                act.wait_ge(x7_out, 16 * TILES * (L + 1))
                meet(act, "act")

        @block.gpsimd
        def _(pool):
            def rstd(ins, outs, scale):
                then(pool, "pool", pool.tensor_scalar(outs, ins, scale, EPS, ALU.mult, ALU.add))
                w = outs.shape[-1]
                return pool.tensor_tensor(outs, outs, mhalf[:, 0:w], ALU.pow)

            def entry(L, i):
                pool.wait_ge(sq_done, norm_no(L, 1, i))
                rstd(ssq[:, i:i + 1], rsd[:, i:i + 1], 1.0 / D).then_inc(rs_done, 1)
                pool.wait_ge(hA_done, norm_no(L, 1, i))
                pool.tensor_tensor(y1[:, i, :], y1[:, i, :], rowB[:, int(ORDER[i] == 4), :], ALU.add).then_inc(h_done, 1)

            pool.memset(sc[:, :, :], 0.0).then_inc(zero_set, 1)
            pool.memset(zeros[:, :], 0.0).then_inc(zero_set, 1)
            pool.memset(brow[:, :, :], 0.0).then_inc(half_set, 1)
            pool.memset(mhalf[:, :], -0.5).then_inc(half_set, 1)
            pool.wait_ge(half_set, 2)
            pool.wait_ge(zero_set, 2)
            pool.sem_inc(sc_set, 1)

            def bias_loads(L):
                bm = t_in["b_mod"][L].rearrange("(g i n) -> i g n", g=3, i=4)
                for i in range(4):
                    pool.dma_start(brow[32 * i:32 * i + 2, :, :],
                                   bm[i:i + 1].broadcast_to([2, 3, 512])).then_inc(bmod_in, 16)

            def vector_loads(L):
                pool.dma_start(nrm[:, :], t_in["norm1"][L:L + 1, :].broadcast_to([P, D])).then_inc(nrm_in, 16)
                pool.dma_start(gqa[:, :], t_in["g_qa"][L:L + 1, :].broadcast_to([P, 256])).then_inc(vec_in, 16)
                pool.dma_start(gkva[:, :], t_in["g_kva"][L:L + 1, :].broadcast_to([P, 128])).then_inc(vec_in, 16)
                pool.dma_start(sink[:, :], t_in["swa_sink"][L:L + 1, :].broadcast_to([P, 4])).then_inc(vec_in, 16)

            bias_loads(0)
            vector_loads(0)
            for i in range(TILES):
                entry(0, i)
            meet(pool, "pool")
            for L in range(DEPTH):
                src = t_in["x0"] if L == 0 else xbuf
                for at, w, name in ((0, 128, "cache_mla_ckv"), (128, 32, "cache_mla_kpe"),
                                    (160, 128, "cache_swa_k"), (288, 256, "cache_na_k")):
                    pool.dma_start(ck[:, at:at + w], t_in[name][L]).then_inc(cache_in, 16)
                pool.dma_start(v_loc[:, 4, :], t_in["cache_v"][L]).then_inc(cache_in, 16)
                pool.memset(qsP, 0.0).then_inc(pad_set, 1)
                pool.memset(qnP, 0.0).then_inc(pad_set, 1)
                for i in range(TILES):
                    pool.wait_ge(sq2_done, TILES * L + i + 1)
                    a = 8 + 2 * i
                    then(pool, "pool", pool.tensor_scalar(rsd[:, a:a + 1], ssq[:, a:a + 1], 1.0 / 256, EPS, ALU.mult, ALU.add))
                    then(pool, "pool", pool.tensor_scalar(rsd[:, a + 1:a + 2], ssq[:, a + 1:a + 2], 1.0 / 128, EPS, ALU.mult, ALU.add))
                    pool.tensor_tensor(rsd[:, a:a + 2], rsd[:, a:a + 2], mhalf[:, 0:2], ALU.pow).then_inc(rs2_done, 1)
                meet(pool, "pool")
                pool.dma_start(nrm[:, :], t_in["norm2"][L:L + 1, :].broadcast_to([P, D])).then_inc(nrm_in, 16)
                mad = cst["madd"].unsqueeze(1).broadcast_to([P, 15, 64])
                for h in range(4):
                    pool.wait_ge(bias_mul, 4 * L + h + 1)
                    bh = bias[:, h, :].rearrange("p (j c) -> p j c", j=15)
                    pool.tensor_tensor(bh, bh, mad, ALU.add).then_inc(bias_done, 1)
                meet(pool, "pool")
                if L < DEPTH - 1:
                    bias_loads(L + 1)
                meet(pool, "pool")
                for i in range(TILES):
                    pool.wait_ge(sq_done, norm_no(L, 2, i))
                    then(pool, "pool", pool.tensor_tensor(ssq[:, i:i + 1], ssq[:, i:i + 1], ssq[:, 18 + i:19 + i], ALU.add))
                    rstd(ssq[:, i:i + 1], rsd[:, i:i + 1], 1.0 / D).then_inc(rs_done, 1)
                meet(pool, "pool")
                pool.wait_ge(xs_out, 16 * TILES * (L + 1))
                if L == 0:
                    pool.wait_ge(zero_out, 16 * 10)
                pool.wait_ge(idx_done, L + 1)
                for j in range(2):
                    for t in range(TILES):
                        pool.indirect_dma_start(slots_x, bass.IndirectOffsetOnAxis(ap=sidx[:, j * TILES + t:j * TILES + t + 1], axis=0),
                                                heads[:, t, :], None).then_inc(scat_out, 16)
                pool.wait_ge(scat_out, 160 * (L + 1))
                meet(pool, "pool")
                n_ov = pool.value_load(ctl[0:1, 0:1], min_val=0, max_val=NOVF)
                E0 = NE * L
                if L < DEPTH - 1:
                    vector_loads(L + 1)
                else:
                    pool.dma_start(nrm[:, :], t_in["norm_final"].unsqueeze(0).broadcast_to([P, D])).then_inc(nrm_in, 16)
                with pool.Fori(0, NE // 2) as pair:
                    for j in range(2):
                        e = pair * 2 + j
                        row = pair * (2 * P) + j * P
                        pool.wait_ge(e_ya, e + (E0 + 1))
                        pool.wait_ge(e_yd, e + (E0 + 1))
                        pool.dma_start(slots_y[bass.ds(row, P), :], yb[:, j, :]).then_inc(ys_out[j], 16)
                for j in range(2):
                    pool.wait_ge(ys_out[j], 16 * (E0 + NE) // 2)
                with pool.If(n_ov > 0):
                    for c in range(NOVF):
                        row = (NE + c) * P
                        pool.wait_ge(ov[L]["y"], c + 1)
                        pool.dma_start(slots_y[row:row + P, :], yb[:, 0, :]).then_inc(ov[L]["out"], 16)
                        pool.wait_ge(ov[L]["out"], 16 * (c + 1))
                meet(pool, "pool")
                def gather(dst, j, i):
                    at = j * TILES + ORDER[i]
                    pool.indirect_dma_start(dst, None, slots_y,
                                            bass.IndirectOffsetOnAxis(ap=sidx[:, at:at + 1], axis=0)).then_inc(y_in[i], 16)

                for i in range(TILES):
                    gather(y1[:, i, :], 0, i)
                    if i == TILES - 1:
                        pool.wait_ge(comb_done, TILES * L + 1)
                    gather(y2[:, i % 4, :], 1, i)
                for i in range(TILES):
                    if L < DEPTH - 1:
                        entry(L + 1, i)
                    else:
                        pool.wait_ge(fin_sq, i + 1)
                        rstd(ssq[:, 24 + i:25 + i], rsd[:, 24 + i:25 + i], 1.0 / D).then_inc(fin_rs, 1)
                meet(pool, "pool")

        @block.vector
        def _(dve):
            TT, TS, STT = dve.tensor_tensor, dve.tensor_scalar, dve.scalar_tensor_tensor

            def mod_rows(L, g):
                dve.wait_ge(M.full, M[("mod", L, g)])
                if g == 0:
                    dve.wait_ge(bmod_in, 64 * (L + 1))
                TT(mrow[:, g, :], ps[:, 7, :], brow[:, g, :], ALU.add).then_inc(mods_done, 1)
                dve.wait_ge(mods_done, 3 * L + g + 1)
                dve.sem_inc(M.free, 1)

            def row_from(L, kind, vec, half, dst, scale_norm=False):
                lane, b = row_bank(("bc", L, kind, vec, half))
                dve.wait_ge(lane.full, lane[("bc", L, kind, vec, half)])
                d = dst[:, half * 512:(half + 1) * 512]
                if scale_norm:
                    ins = STT(d, ps[:, b, :], 1.0, nrm[:, half * 512:(half + 1) * 512], ALU.add, ALU.mult)
                else:
                    ins = dve.tensor_copy(d, ps[:, b, :])
                return ins.then_inc(lane.free, 1)

            def rope(x, cos, sin, tmp, heads, dim):
                h4 = dim // 4

                def v(a):
                    return a.rearrange("p (h d) -> p h d", h=heads)

                def halves(a, j):
                    return a.rearrange("p (m s d) -> p m s d", s=2, d=h4)[:, :, j, :]

                def table(a, j):
                    return a.rearrange("p (m s d) -> p m s d", s=2, d=h4)[:, :, j, :].unsqueeze(1).broadcast_to([P, heads, 2, h4])

                n = heads * dim
                TT(v(tmp[:, 0, 0:n]), v(x), cos.unsqueeze(1).broadcast_to([P, heads, dim]), ALU.mult)
                for j in range(2):
                    o = halves(tmp[:, 1, 0:n], j).rearrange("p (h a) d -> p h a d", a=2)
                    i = halves(x, 1 - j).rearrange("p (h a) d -> p h a d", a=2)
                    last = TT(o, i, table(sin, j), ALU.mult)
                then(dve, "dve", last)
                return TT(x, tmp[:, 0, 0:n], tmp[:, 1, 0:n], ALU.add)

            def attention(L, phase):
                units = UNITS[phase]

                def maximum(u):
                    un, w = units[u], units[u]["n"] * P
                    dve.wait_ge(S[u % 2].full, S[u % 2][("s", L, phase, u)])
                    src = two(2 * (u % 2), w)
                    mx, m2, nm = (stat[n][:, u % 8:u % 8 + 1] for n in ("mx", "m2", "nm"))
                    if "mask" in un and u >= 2:
                        dve.wait_ge(S[u % 2].free, S[u % 2].freed[("s", L, phase, u - 2)])
                    if un["kind"] == "swa":
                        then(dve, "dve", dve.tensor_tensor_reduce(sB[:, u % 2, 0:w], src, un["mask"], 1.0,
                                                                  sink[:, un["h"]:un["h"] + 1], ALU.add, ALU.max, mx))
                        TS(nm, mx, -1.0, None, ALU.mult).then_inc(nmax_done, 1)
                    elif un["kind"] == "na":
                        then(dve, "dve", TS(sB[:, u % 2, 512:640], src[:, 512:640], 1.0, NEG, ALU.mult, ALU.max,
                                            accum_out=m2))
                        then(dve, "dve", dve.tensor_tensor_reduce(sB[:, u % 2, 0:512], src[:, 0:512], un["mask"], 1.0,
                                                                  m2, ALU.add, ALU.max, mx))
                        TS(nm, mx, -1.0, None, ALU.mult).then_inc(nmax_done, 1)
                    elif un["kind"] == "swa_ctx":
                        then(dve, "dve", dve.tensor_reduce(mx, src, AX.X, ALU.max))
                        TS(nm, mx, sink[:, un["h"]:un["h"] + 1], -1.0, ALU.max, ALU.mult).then_inc(nmax_done, 1)
                    else:
                        dve.tensor_reduce(nm, src, AX.X, ALU.max, negate=True).then_inc(nmax_done, 1)

                def copy(u):
                    a, d = split(units[u]["n"])
                    dve.wait_ge(T.full, T[("p", L, phase, u)])
                    if u >= 2:
                        dve.wait_ge(O.full, O[("o", L, phase, u - 2)])
                    dve.tensor_copy(pT[phase][:, u % 2, 0:a * P], ps[:, 4, 0:a * P]).then_inc(T.free, 1)

                def norm(u):
                    un = units[u]
                    sm, es, ri = (stat[n][:, u % 8:u % 8 + 1] for n in ("sm", "es", "ri"))
                    if un["kind"].startswith("swa"):
                        then(dve, "dve", TT(sm, sm, es, ALU.add))
                    then(dve, "dve", dve.reciprocal(ri, sm))
                    dve.wait_ge(O.full, O[("o", L, phase, u)])
                    TS(heads[:, un["t"], un["col"]:un["col"] + 64], ps[:, 6, 0:64], ri, None,
                       ALU.mult).then_inc(O.free, 1)

                for s in range(STEPS[phase]):
                    if s < len(units):
                        maximum(s)
                    if 2 <= s < len(units) + 2:
                        norm(s - 2)
                    if 1 <= s <= len(units):
                        copy(s - 1)
                    if phase == 4:
                        beside(L, s)
                    if phase == 2 and s in (18, 32):
                        mod_rows(L, 1 if s == 18 else 2)

            def beside(L, s):
                if s == NEXT_MOD + 1 and L < DEPTH - 1:
                    mod_rows(L + 1, 0)
                if s == PROJ[0] + HO + 1:
                    dve.wait_ge(rows_in, 96 * (L + 1))
                    dve.wait_ge(nrm_in, 16 * (2 * L + 2))
                    then(dve, "dve", STT(rowA2, rowA2, 1.0, nrm[:, :].unsqueeze(1).broadcast_to([P, 2, D]), ALU.add, ALU.mult))
                for i in range(TILES):
                    t, n = ORDER[i], s - PROJ[i]
                    kind = int(t == 4)
                    if n in (OUT, OUT + 1):
                        half = n - OUT
                        cols = slice(half * 512, (half + 1) * 512)
                        dve.wait_ge(M.full, M[("out", L, i, half)])
                        then(dve, "dve", TT(heads[:, t, cols], ps[:, 7, :], rowG1[:, kind, cols], ALU.mult))
                        dve.sem_inc(M.free, 1)
                        dve.wait_ge(xh_in, 16 * (2 * (TILES * L + i) + half + 1))
                        TT(heads[:, t, cols], heads[:, t, cols], xh, ALU.add).then_inc(res_done, 1)
                    if n == NORM:
                        dve.wait_ge(rs_done, norm_no(L, 2, i))
                        dve.wait_ge(xs_out, 16 * (TILES * L + i + 1))
                        STT(heads[:, t, :], heads[:, t, :], rsd[:, i:i + 1], rowA2[:, kind, :],
                            ALU.mult, ALU.mult).then_inc(hA_done, 1)
                    if n == NORM + 1:
                        dve.wait_ge(hA_done, norm_no(L, 2, i))
                        TT(heads[:, t, :], heads[:, t, :], rowB2[kind], ALU.add).then_inc(h_done, 1)
                    if n == ROUTE:
                        dve.wait_ge(M.full, M[("rt", L, i)])
                        dve.tensor_copy(r_lg[:, t, :], ps[:, 7, 0:20]).then_inc(M.free, 1)

            def entry_rows(L, kind):
                dve.wait_ge(nrm_in, 16 * (2 * L + 1))
                for v, dst in ((0, rowB), (1, rowA)):
                    for half in range(2):
                        row_from(L, kind, v, half, dst[:, kind, :], v == 1)
                for lane in (O, M):
                    dve.wait_ge(lane.free, lane.freed[("bc", L, kind, 1, 0 if lane is O else 1)])

            def entry(L, i):
                dve.wait_ge(rs_done, norm_no(L, 1, i))
                STT(y1[:, i, :], x7[:, i, :], rsd[:, i:i + 1], rowA[:, int(ORDER[i] == 4), :], ALU.mult,
                    ALU.mult).then_inc(hA_done, 1)

            dve.wait_ge(const_in, 16)
            c32, s32 = (cst[n].rearrange("p (t d) -> p t d", t=4) for n in ("cos32", "sin32"))
            c64, s64 = (cst[n].rearrange("p (t d) -> p t d", t=4) for n in ("cos64", "sin64"))
            dve.wait_ge(half_set, 2)
            mod_rows(0, 0)
            entry_rows(0, 1)
            entry_rows(0, 0)
            for i in range(TILES):
                entry(0, i)
            meet(dve, "dve")
            for L in range(DEPTH):
                dve.wait_ge(small_in, 48 * (L + 1))
                dve.wait_ge(vec_in, 48 * (L + 1))
                for s in range(TILES + 1):
                    if s < TILES:
                        i = s
                        q = proj[:, i % 2, :]
                        dve.wait_ge(S[0].full, S[0][("in", L, i)])
                        if i >= 2:
                            dve.wait_ge(T.full, T[("xp", L, i - 2)])
                            if i == 2:
                                dve.wait_ge(ctx_out, 96 * (L + 1))
                        dve.tensor_copy(q[:, 0:416], ps[:, 0, 0:416])
                        dve.tensor_copy(q[:, 416:800], ps[:, 1, 0:384]).then_inc(S[0].free, 1)
                        dve.wait_ge(S[0].free, S[0].freed[("in", L, i)])
                        a = 8 + 2 * i
                        if ORDER[i] != 4:
                            t = ORDER[i]
                            then(dve, "dve", rope(q[:, C_QS:C_QS + 384], c64[:, t, :], s64[:, t, :], rt, 6, 64))
                            then(dve, "dve", rope(q[:, C_KPE:C_KPE + 32], c32[:, t, :], s32[:, t, :], rt, 1, 32))
                        dve.wait_ge(rs2_done, TILES * L + i + 1)
                        STT(q[:, 0:256], q[:, 0:256], rsd[:, a:a + 1], gqa[:, :], ALU.mult, ALU.mult)
                        STT(q[:, C_CKV:C_CKV + 128], q[:, C_CKV:C_CKV + 128], rsd[:, a + 1:a + 2], gkva[:, :],
                            ALU.mult, ALU.mult).then_inc(post_done, 1)
                    if s >= 1:
                        for i in ([5, 0] if s == 1 else [s - 1]):
                            kv = 4 if i == 5 else (5 if ORDER[i] == 4 else ORDER[i])
                            dve.wait_ge(T.full, T[("xp", L, i)])
                            if i < 5:
                                t0 = ORDER[i] * P
                                dve.wait_ge(pad_set, 2 * L + 2)
                                for lo in (0, 64):
                                    TS(qsP[lo:lo + 64, lo // 32:lo // 32 + 2, t0:t0 + P],
                                       ps[lo:lo + 64, 5, 0:256].rearrange("p (k n) -> p k n", k=2), HEAD_SCALE, None, ALU.mult)
                            ks = ps[:, 5, 256:384] if i < 5 else ps[:, 5, 0:P]
                            dve.tensor_copy(ksT[:, kv * P:(kv + 1) * P], ks).then_inc(T.free, 1)
                meet(dve, "dve")
                m01 = cst["m01"].unsqueeze(1).broadcast_to([P, 7, 64])
                for h in range(4):
                    dve.wait_ge(S[h % 2].full, S[h % 2][("bias", L, h)])
                    for n in range(2):
                        bk = ps[:, 2 * (h % 2) + n, :]
                        o = bias[:, h, n * 480:(n + 1) * 480]
                        if n == 0:
                            TT(o[:, 0:448].rearrange("p (j c) -> p j c", j=7), bk[:, 0:448].rearrange("p (j c) -> p j c", j=7),
                               m01, ALU.mult)
                            TT(o[:, 448:480], bk[:, 448:480], cst["m01"][:, 0:32], ALU.mult)
                        else:
                            TT(o[:, 0:32], bk[:, 0:32], cst["m01"][:, 32:64], ALU.mult)
                            last = TT(o[:, 32:480].rearrange("p (j c) -> p j c", j=7),
                                      bk[:, 32:480].rearrange("p (j c) -> p j c", j=7), m01, ALU.mult)
                    then(dve, "dve", last)
                    dve.sem_inc(S[h % 2].free, 1)
                    dve.sem_inc(bias_mul, 1)
                attention(L, 2)
                meet(dve, "dve")
                for h in range(MLA_H):
                    dve.tensor_copy(kT[64:96, h, :], kpeT[0:ROPE, :])
                for i in range(TILES + 1):
                    if i in (0, 2):
                        dve.wait_ge(S[0].full, S[0][("uk", L, i)])
                        dve.tensor_copy(kT[0:64, 2 * i, :], two(0, 768)[0:64])
                        dve.tensor_copy(kT[0:64, 2 * i + 1, :], two(0, 768)[64:128]).then_inc(S[0].free, 1)
                    if i % 2 == 1:
                        dve.wait_ge(M.full, M[("uv", L, i)])
                        dve.tensor_copy(v_mla[:, i, :], ps[:, 7, :]).then_inc(M.free, 1)
                    if i < TILES:
                        dve.wait_ge(T.free, T.freed[("uq", L, i)])
                        t = ORDER[i]
                        if t == 4:
                            dve.sem_inc(q_done, 1)
                        else:
                            x = qt[:, i % 2, :].rearrange("p (h d) -> p h d", h=MLA_H)[:, :, NOPE:QK]
                            dve.wait_ge(q_done, TILES * L + i)
                            t1 = rq[:, 0, :].rearrange("p (h d) -> p h d", h=MLA_H)
                            t2 = rq[:, 1, :].rearrange("p (h d) -> p h d", h=MLA_H)
                            TT(t1, x, c32[:, t, :].unsqueeze(1).broadcast_to([P, MLA_H, ROPE]), ALU.mult)
                            for ax in range(2):
                                for j in range(2):
                                    o0, i0 = 16 * ax + 8 * j, 16 * ax + 8 * (1 - j)
                                    last = TT(t2[:, :, o0:o0 + 8], x[:, :, i0:i0 + 8],
                                              s32[:, t, o0:o0 + 8].unsqueeze(1).broadcast_to([P, MLA_H, 8]), ALU.mult)
                            then(dve, "dve", last)
                            TT(x, t1, t2, ALU.add).then_inc(q_done, 1)
                    if i >= 1 and (i - 1) % 2 == 1:
                        t0 = ORDER[i - 1] * P
                        dve.wait_ge(S[1].full, S[1][("qt", L, i - 1)])
                        dve.tensor_copy(qT[0:QK, :, t0:t0 + P], two(2)[0:QK].rearrange("p (h n) -> p h n", h=8)).then_inc(S[1].free, 1)
                meet(dve, "dve")
                attention(L, 4)
                meet(dve, "dve")
                def go(ins):
                    then(dve, "dve", ins)

                def b4(a):
                    return a.unsqueeze(2).broadcast_to([P, TILES, 4])

                w4 = cst["w4"].unsqueeze(1).broadcast_to([P, TILES, 4])

                def first_max(x, m, oh):
                    go(dve.tensor_reduce(m, x, AX.X, ALU.max))
                    go(TT(r_eq, x, b4(m), ALU.is_equal))
                    go(TT(r_eq, r_eq, w4, ALU.mult))
                    go(dve.tensor_reduce(r_g, r_eq, AX.X, ALU.max))
                    go(TT(oh, r_eq, b4(r_g), ALU.is_equal))

                grp = r_lg[:, :, 0:4]
                dve.memset(r_T[:, TILES, :], 0.0)
                first_max(grp, r_m, r_oh)
                go(TT(r_gd, grp, b4(r_m), ALU.subtract))
                dve.sem_inc(rx1, 1)
                elog = r_lg[:, :, 4:20].rearrange("p t (g e) -> p t g e", g=4)
                go(TT(r_prod, elog, r_oh.unsqueeze(3).broadcast_to([P, TILES, 4, 4]), ALU.mult))
                go(dve.tensor_reduce(r_sel, r_prod.rearrange("p t g e -> p t e g"), AX.X, ALU.add))
                first_max(r_sel, r_m, r_oh1)
                go(STT(r_sel, r_oh1, NEG, r_sel, ALU.mult, ALU.add))
                go(dve.tensor_copy(r_d2, r_m))
                first_max(r_sel, r_m, r_oh2)
                go(TT(r_d2, r_m, r_d2, ALU.subtract))
                dve.sem_inc(rx2, 1)
                for j, oh in enumerate((r_oh1, r_oh2)):
                    last = TT(r_c[:, j].rearrange("p t (g e) -> p t g e", g=4),
                              r_oh.unsqueeze(3).broadcast_to([P, TILES, 4, 4]),
                              oh.unsqueeze(2).broadcast_to([P, TILES, 4, 4]), ALU.mult)
                go(last)
                TT(r_T[:, 0:TILES, :], r_c[:, 0], r_c[:, 1], ALU.add).then_inc(pick_done, 1)
                dve.wait_ge(O.full, O[("pos", L)])
                pos = ps[:, 6, 0:TILES * NE].rearrange("p (t e) -> p t e", t=TILES)
                total = ps[:, 6, TILES * NE:(TILES + 1) * NE]
                TT(r_slot, pos, cst["ebase"].unsqueeze(1).broadcast_to([P, TILES, NE]), ALU.add)
                go(TT(r_cmp, total.unsqueeze(2).broadcast_to([P, NE, 4]),
                      cst["chunk_at"].unsqueeze(1).broadcast_to([P, NE, 4]), ALU.is_gt))
                go(dve.tensor_reduce(r_nov, r_cmp, AX.X, ALU.add))
                less = cst["less"].rearrange("p (a b) -> p a b", a=NE)
                go(TT(r_pr, r_nov.unsqueeze(1).broadcast_to([P, NE, NE]), less, ALU.mult))
                go(dve.tensor_reduce(r_ovb, r_pr, AX.X, ALU.add))
                go(STT(r_dl, r_ovb, float(P), cst["ovshift"], ALU.mult, ALU.add))
                go(STT(r_ge5, pos, float(CAP), r_dl.unsqueeze(1).broadcast_to([P, TILES, NE]), ALU.is_ge, ALU.mult))
                dve.sem_inc(O.free, 1)
                go(TT(r_slot, r_slot, r_ge5, ALU.add))
                for j in range(2):
                    last = TT(r_pick[:, j], r_slot, r_c[:, j], ALU.mult)
                go(last)
                go(dve.tensor_reduce(r_s, r_pick, AX.X, ALU.add))
                dve.tensor_copy(sidx[:, :], r_s.rearrange("p a b -> p (a b)")).then_inc(idx_done, 1)
                dve.wait_ge(rx1_done, L + 1)
                go(dve.tensor_reduce(r_g, r_ge, AX.X, ALU.add))
                dve.wait_ge(rx2_done, L + 1)
                go(TS(r_m, r_e2, 1.0, None, ALU.add))
                go(TT(r_m, r_m, r_g, ALU.mult))
                go(dve.reciprocal(wts[:, :, 0], r_m))
                go(TT(wts[:, :, 1], wts[:, :, 0], r_e2, ALU.mult))
                go(dve.tensor_reduce(r_ctl[:, 0:1], r_nov, AX.X, ALU.add))
                go(TT(r_ovb, r_ovb, r_nov, ALU.add))
                go(TT(r_ind, r_ovb.unsqueeze(1).broadcast_to([P, NOVF, NE]),
                      cst["chunk"].unsqueeze(2).broadcast_to([P, NOVF, NE]), ALU.is_le))
                go(dve.tensor_reduce(r_ctl[:, 1:1 + NOVF], r_ind, AX.X, ALU.add))
                go(TS(r_ctl[:, 1:1 + NOVF], r_ctl[:, 1:1 + NOVF], float(NE - 1), None, ALU.min))
                go(dve.tensor_copy(ctl[:, 0:1 + NOVF], r_ctl[:, 0:1 + NOVF]))
                meet(dve, "dve")
                n_ov = dve.value_load(ctl[0:1, 0:1], min_val=0, max_val=NOVF)
                E0 = NE * L

                def x_copy(e, b, early):
                    if not early:
                        dve.wait_ge(e_h, E0 + e - 1)
                    dve.wait_ge(e_xT, E0 + e + 1)
                    dve.tensor_copy(xgT[:, b, 512:1024], ps[:, 5, :]).then_inc(e_xTd, 1)

                def gate(e, b):
                    dve.wait_ge(e_sg, E0 + e + 1)
                    TT(hid[:, b, :], sg[:, b, :], ps[:, b, FF:2 * FF], ALU.mult).then_inc(e_hid, 1)

                def hid_copy(e, b, early):
                    dve.wait_ge(e_hT, E0 + e + 1)
                    if not early:
                        dve.wait_ge(e_d, E0 + e - 1)
                    dve.tensor_copy(hidT[:, b, :], ps[:, 6, 0:FF]).then_inc(e_hTe, 1)

                def y_copy(e, b, early):
                    dve.wait_ge(e_d, E0 + e + 1)
                    if not early:
                        dve.wait_ge(ys_out[b], 8 * E0 + 8 * (e - b))
                    dve.tensor_copy(yb[:, b, 512:1024], ps[:, 3, :]).then_inc(e_yd, 1)

                x_copy(0, 0, True)
                gate(0, 0)
                x_copy(1, 1, True)
                hid_copy(0, 0, True)
                gate(1, 1)
                x_copy(2, 0, False)
                y_copy(0, 0, True)
                hid_copy(1, 1, True)
                gate(2, 0)
                x_copy(3, 1, False)
                y_copy(1, 1, True)
                hid_copy(2, 0, False)
                with dve.Fori(3, NE - 1, 2) as e0:
                    for j in range(2):
                        e, b = e0 + j, 1 - j
                        gate(e, b)
                        x_copy(e + 1, 1 - b, False)
                        y_copy(e - 1, 1 - b, False)
                        hid_copy(e, b, False)
                gate(15, 1)
                y_copy(14, 0, False)
                hid_copy(15, 1, False)
                y_copy(15, 1, False)
                with dve.If(n_ov > 0):
                    with dve.Fori(0, NOVF) as c:
                        n = c + 1
                        dve.wait_ge(ov[L]["sg"], n)
                        TT(hid[:, 0, :], sg[:, 0, :], ps[:, 0, FF:2 * FF], ALU.mult).then_inc(ov[L]["hid"], 1)
                        dve.wait_ge(ov[L]["hT"], n)
                        dve.tensor_copy(hidT[:, 0, :], ps[:, 6, 0:FF]).then_inc(ov[L]["hTe"], 1)
                meet(dve, "dve")
                def final(i):
                    if i == 0:
                        dve.wait_ge(nrm_in, 16 * (2 * DEPTH + 1))
                    dve.wait_ge(fin_rs, i + 1)
                    STT(x7[:, i, :], x7[:, i, :], rsd[:, 24 + i:25 + i], nrm[:, :], ALU.mult,
                        ALU.mult).then_inc(fin_done, 1)

                for lane in (O, M):
                    dve.wait_ge(lane.free, lane.freed[("bc", L, 0, 5, 0 if lane is O else 1)])
                for s in range(TILES + 1):
                    if s < TILES:
                        t = ORDER[s]
                        y = y2[:, s % 4, :]
                        dve.wait_ge(y1_scaled, TILES * L + s + 1)
                        dve.wait_ge(x7_in[s], 16 * (L + 2))
                        go(STT(y, y, wts[:, t, 1:2], y1[:, s, :], ALU.mult, ALU.add))
                        go(TT(y, y, rowG2[:, int(t == 4), :], ALU.mult))
                        TT(x7[:, s, :], x7[:, s, :], y, ALU.add).then_inc(comb_done, 1)
                    if s <= 1 and L < DEPTH - 1:
                        entry_rows(L + 1, 1 - s)
                    if s >= 1:
                        if L < DEPTH - 1:
                            entry(L + 1, s - 1)
                        else:
                            final(s - 1)
                meet(dve, "dve")


CONSTS = [("ident", P), ("flip", P), ("upper", P), ("m01", 64), ("madd", 64), ("swa", 7 * P),
          ("cos32", 128), ("sin32", 128), ("cos64", 256), ("sin64", 256), ("less", NE * NE), ("w4", 4),
          ("ebase", NE), ("ovshift", NE), ("chunk", NOVF), ("chunk_at", 4)]


def constants():
    p = np.arange(P)
    col = p % GRID_W
    start = np.clip(col - 8, 0, GRID_W - 16)
    kc = np.arange(GRID_W)
    ok = (kc[None, :] >= start[:, None]) & (kc[None, :] < start[:, None] + 16)
    key, query = p[None, :], p[:, None]
    far, none = np.float32(-1e30), np.zeros((P, P), np.float32)
    before = np.where(key >= query, 0, far)
    after = np.where(key <= query, 0, far)
    c = {
        "ident": np.eye(P), "flip": np.eye(P)[::-1], "upper": query < key,
        "m01": ok, "madd": np.where(ok, 0, far),
        "swa": np.concatenate([before, none, after, none, before, none, none], 1),
        "less": np.broadcast_to((np.arange(NE)[None, :] < np.arange(NE)[:, None]).reshape(1, -1), (P, NE * NE)),
        "w4": np.broadcast_to(np.arange(4, 0, -1), (P, 4)),
        "ebase": np.broadcast_to(np.arange(NE) * P, (P, NE)),
        "ovshift": np.broadcast_to(NE * P - CAP - np.arange(NE) * P, (P, NE)),
        "chunk_at": np.broadcast_to(CAP + np.arange(4) * P, (P, 4)),
        "chunk": np.broadcast_to(np.arange(NOVF), (P, NOVF)),
    }
    pos = np.arange(DEC)
    for dim in (32, 64):
        half = dim // 4
        freq = (10000.0 ** (-np.arange(half, dtype=np.float32) / half)).astype(np.float32)
        cs, sn = [], []
        for x in (pos // GRID_W, pos % GRID_W):
            ang = x.astype(np.float32)[:, None] * freq[None, :]
            cs += [np.cos(ang), np.cos(ang)]
            sn += [-np.sin(ang), np.sin(ang)]
        for n, parts in (("cos", cs), ("sin", sn)):
            full = np.concatenate(parts, 1).reshape(4, P, dim)
            c[n + str(dim)] = full.transpose(1, 0, 2).reshape(P, 4 * dim)
    return np.concatenate([np.asarray(c[n], np.float32).reshape(P, w) for n, w in CONSTS], 1)


def kernel(**inputs):
    import concourse.bacc as bacc
    from concourse.bass_utils import run_bass_kernel_spmd

    x = {k: np.ascontiguousarray(v) for k, v in inputs.items()}
    w = x["w_in"]
    swa_q = w[:, :, 416:672].reshape(DEPTH, D, 4, 64)[:, :, [0, 2, 1, 3]].reshape(DEPTH, D, 256)
    w_in = np.concatenate([w[:, :, 0:416], swa_q, w[:, :, 672:800], w[:, :, 928:1440], w[:, :, 800:928],
                           w[:, :, 1440:1696]], 2)
    w_ukv = x["w_ukv"].reshape(DEPTH, 128, MLA_H, 2, 64).transpose(0, 1, 3, 2, 4).reshape(DEPTH, 128, 1024)
    rpb = np.pad(x["na_rpb"], ((0, 0), (0, 0), (0, 0), (0, RPB_ROW - 31))).reshape(DEPTH * 4, 15 * RPB_ROW)
    flat = {
        "consts": constants(),
        "x0": np.concatenate([x["x_sample"][0], x["x_prompt"][0]], 0),
        "c": x["c"], "c_ctx": x["c_ctx"], "w_mod": x["w_mod"], "b_mod": x["b_mod"],
        "norm1": x["norm1"], "norm2": x["norm2"], "norm_final": x["norm_final"],
        "w_in": w_in, "g_qa": x["g_qa"], "w_uq": x["w_uq"], "g_kva": x["g_kva"], "w_ukv": w_ukv,
        "swa_sink": x["swa_sink"], "rpb": np.pad(rpb, ((0, 0), (P, 64))),
        "w_out": x["w_out"], "w_r": np.concatenate([x["w_router_grp"], x["w_router_exp"]], 2),
        "w_gate": x["w_gate"], "w_up": x["w_up"], "w_down": x["w_down"],
        "cache_mla_ckv": x["cache_mla_ckv"][0], "cache_mla_kpe": x["cache_mla_kpe"][0],
        "cache_swa_k": x["cache_swa_k"].reshape(DEPTH, P, 128), "cache_na_k": x["cache_na_k"].reshape(DEPTH, P, 256),
        "cache_v": np.concatenate([x["cache_swa_v"].reshape(DEPTH, P, 128), x["cache_na_v"].reshape(DEPTH, P, 256)], 2),
    }
    nc = bacc.Bacc("TRN2", target_bir_lowering=False, num_devices=1)
    arrays, t_in, t_out = {}, {}, {}
    for n, a in flat.items():
        arrays["in_" + n] = a = np.ascontiguousarray(a)
        t_in[n] = nc.dram_tensor("in_" + n, a.shape, mybir.dt.from_np(a.dtype), kind="ExternalInput").ap()
    outs = {"y_prompt": (SEQ, D), "y_sample": (DEC, D), "ckv": (DEPTH, SEQ, 128), "kpe": (DEPTH, SEQ, 32),
            "ks": (DEPTH, SEQ, 128), "vs": (DEPTH, SEQ, 128), "kn": (DEPTH, SEQ, 256), "vn": (DEPTH, SEQ, 256)}
    for n, shape in outs.items():
        t_out[n] = nc.dram_tensor("out_" + n, shape, F32, kind="ExternalOutput").ap()
    program(nc, t_in, t_out)
    r = run_bass_kernel_spmd(nc, [arrays], core_ids=[0]).results[0]
    shapes = {"y_prompt": (1, SEQ, D), "y_sample": (1, DEC, D), "ckv": (1, DEPTH, SEQ, 128), "kpe": (1, DEPTH, SEQ, 32),
              "ks": (1, DEPTH, SEQ, 2, 64), "vs": (1, DEPTH, SEQ, 2, 64), "kn": (1, DEPTH, SEQ, 4, 64),
              "vn": (1, DEPTH, SEQ, 4, 64)}
    return tuple(np.asarray(r["out_" + n]).reshape(shape) for n, shape in shapes.items())
```
